# Optimizing a Trainium2 kernel written in Bass

```python
import math
import jax, jax.numpy as jnp
from jax import lax
import numpy as np

D_MODEL = 2048
BATCH = 1
SEQ = 256
DEPTH = 1

CHUNK = 64
Q_BLOCK = 128
FOX_HEADS = 8
FOX_HEAD_DIM = 128
FOX_WIDTH = FOX_HEADS * FOX_HEAD_DIM
HG_HEADS = 8
HG_KEY_DIM = 128
HG_VAL_DIM = 128
HG_KW = HG_HEADS * HG_KEY_DIM
HG_VW = HG_HEADS * HG_VAL_DIM
PEER_HEADS = 8
PEER_NKEYS = 128
PEER_EXPERTS = PEER_NKEYS * PEER_NKEYS
PEER_DKEY = 256
PEER_HALF = PEER_DKEY // 2
PEER_TOPK = 16
PEER_TOK_BLOCK = 128
EPS = 1e-6
SPLIT_SIZES = (FOX_WIDTH, FOX_WIDTH, FOX_WIDTH, FOX_HEADS,
               HG_KW, HG_KW, HG_VW, HG_VW,
               D_MODEL, D_MODEL)
N_IN = sum(SPLIT_SIZES)

kernel_name = "fox_hgrn2_peer_gated_hybrid"

def rms_norm(x, g):
    xf = x.astype(jnp.float32)
    y = xf * lax.rsqrt(jnp.mean(xf * xf, axis=-1, keepdims=True) + EPS)
    return (y * g.astype(jnp.float32)).astype(x.dtype)

def split_cols(z):
    idx = np.cumsum(np.array(SPLIT_SIZES))[:-1].tolist()
    return jnp.split(z, idx, axis=-1)

def forgetting_attention(q, k, v, log_f):
    B, S, H, Dh = q.shape
    c = jnp.cumsum(log_f, axis=1)
    cT = c.transpose(0, 2, 1)
    nb = S // Q_BLOCK
    qb = q.reshape(B, nb, Q_BLOCK, H, Dh).transpose(1, 0, 2, 3, 4)
    cb = cT.reshape(B, H, nb, Q_BLOCK).transpose(2, 0, 1, 3)
    kpos = jnp.arange(S)
    scale = Dh ** -0.5

    def block(args):
        i, qi, ci = args
        s = jnp.einsum('bqhd,bkhd->bhqk', qi, k,
                       preferred_element_type=jnp.float32) * scale
        bias = ci[..., :, None] - cT[..., None, :]
        qpos = i * Q_BLOCK + jnp.arange(Q_BLOCK)
        mask = kpos[None, :] <= qpos[:, None]
        logits = jnp.where(mask, s + bias, -jnp.inf)
        p = jax.nn.softmax(logits, axis=-1)
        return jnp.einsum('bhqk,bkhd->bqhd', p.astype(v.dtype), v)

    out = lax.map(block, (jnp.arange(nb), qb, cb))
    return out.transpose(1, 0, 2, 3, 4).reshape(B, S, H, Dh)

def hgrn2_recurrence(q, k, v, log_f):
    B, S, H, K = q.shape
    V = v.shape[-1]
    nc = S // CHUNK

    def to_chunks(a):
        return a.reshape(B, nc, CHUNK, H, a.shape[-1]).transpose(1, 0, 3, 2, 4)

    qc, kc, vc, gc = to_chunks(q), to_chunks(k), to_chunks(v), to_chunks(log_f)
    causal = jnp.tril(jnp.ones((CHUNK, CHUNK), dtype=bool))

    def step(state, inp):
        qt, kt, vt, gt = inp
        b = jnp.cumsum(gt, axis=2)
        diff = b[:, :, :, None, :] - b[:, :, None, :, :]
        decay = jnp.exp(jnp.where(causal[None, None, :, :, None], diff, -jnp.inf))
        attn = jnp.einsum('bhtk,bhsk,bhtsk->bhts', qt, kt, decay)
        o = (jnp.einsum('bhts,bhsv->bhtv', attn, vt)
             + jnp.einsum('bhtk,bhkv->bhtv', qt * jnp.exp(b), state))
        b_last = b[:, :, -1:, :]
        new_state = (jnp.exp(b_last[:, :, 0, :])[..., None] * state
                     + jnp.einsum('bhsk,bhsv->bhkv', kt * jnp.exp(b_last - b), vt))
        return new_state, o

    s0 = jnp.zeros((B, H, K, V), jnp.float32)
    _, o = lax.scan(step, s0, (qc, kc, vc, gc))
    return o.transpose(1, 0, 3, 2, 4).reshape(B, S, H, V)

def peer_layer(x, wq, keys, U, Vt):
    B, S, D = x.shape
    T = B * S
    xt = x.reshape(T, D)
    q = (xt @ wq).reshape(T, PEER_HEADS, 2, PEER_HALF)
    scores = jnp.einsum('thcd,hcnd->thcn', q, keys,
                        preferred_element_type=jnp.float32)
    s_top, i_top = lax.top_k(scores, PEER_TOPK)
    cand = s_top[:, :, 0, :, None] + s_top[:, :, 1, None, :]
    cand_idx = i_top[:, :, 0, :, None] * PEER_NKEYS + i_top[:, :, 1, None, :]
    best, pos = lax.top_k(cand.reshape(T, PEER_HEADS, PEER_TOPK * PEER_TOPK), PEER_TOPK)
    idx = jnp.take_along_axis(
        cand_idx.reshape(T, PEER_HEADS, PEER_TOPK * PEER_TOPK), pos, axis=-1)
    gate = jax.nn.softmax(best, axis=-1).astype(x.dtype)

    nb = T // PEER_TOK_BLOCK

    def blk(args):
        xb, ib, gb = args
        u = U[ib]
        hid = jax.nn.gelu(jnp.einsum('td,thkd->thk', xb, u))
        v = Vt[ib]
        return jnp.einsum('thk,thkd->td', gb * hid, v)

    out = lax.map(blk, (xt.reshape(nb, PEER_TOK_BLOCK, D),
                        idx.reshape(nb, PEER_TOK_BLOCK, PEER_HEADS, PEER_TOPK),
                        gate.reshape(nb, PEER_TOK_BLOCK, PEER_HEADS, PEER_TOPK)))
    return out.reshape(B, S, D)

def setup_inputs(seed: int = 0) -> dict:
    key = jax.random.key(seed)
    ks = jax.random.split(key, 16)
    f32 = jnp.float32
    nrm = lambda k, shape, s: (jax.random.normal(k, shape, f32) * s)
    return {
        "x": nrm(ks[0], (BATCH, SEQ, D_MODEL), 1.0),
        "norm1_g": 1.0 + nrm(ks[1], (DEPTH, D_MODEL), 0.02),
        "w_in": nrm(ks[2], (DEPTH, D_MODEL, N_IN), D_MODEL ** -0.5),
        "fox_f_bias": 2.0 + nrm(ks[3], (DEPTH, FOX_HEADS), 0.1),
        "hg_lb_logits": nrm(ks[4], (DEPTH + 1, HG_KW), 0.1),
        "hg_norm_g": 1.0 + nrm(ks[5], (DEPTH, HG_VW), 0.02),
        "w_a_up": nrm(ks[6], (DEPTH, FOX_WIDTH, D_MODEL), FOX_WIDTH ** -0.5),
        "w_b_up": nrm(ks[7], (DEPTH, HG_VW, D_MODEL), HG_VW ** -0.5),
        "w_o": nrm(ks[8], (DEPTH, D_MODEL, D_MODEL), D_MODEL ** -0.5),
        "norm2_g": 1.0 + nrm(ks[9], (DEPTH, D_MODEL), 0.02),
        "peer_wq": nrm(ks[10], (DEPTH, D_MODEL, PEER_HEADS * PEER_DKEY), D_MODEL ** -0.5),
        "peer_keys": nrm(ks[11], (DEPTH, PEER_HEADS, 2, PEER_NKEYS, PEER_HALF), PEER_HALF ** -0.5),
        "peer_u": nrm(ks[12], (DEPTH, PEER_EXPERTS, D_MODEL), D_MODEL ** -0.5),
        "peer_v": nrm(ks[13], (DEPTH, PEER_EXPERTS, D_MODEL), (PEER_HEADS * PEER_TOPK) ** -0.5),
        "norm_f_g": 1.0 + nrm(ks[14], (D_MODEL,), 0.02),
    }

def reference(x, norm1_g, w_in, fox_f_bias, hg_lb_logits, hg_norm_g, w_a_up, w_b_up,
              w_o, norm2_g, peer_wq, peer_keys, peer_u, peer_v, norm_f_g):
    B, S, D = x.shape
    lb_all = jnp.cumsum(jax.nn.softmax(hg_lb_logits.astype(jnp.float32), axis=0), axis=0)
    for l in range(DEPTH):
        h = rms_norm(x, norm1_g[l])
        z = h @ w_in[l]
        fq, fk, fv, ff, hq, hf, hi, hgate, ga, gb = split_cols(z)

        log_fa = jax.nn.log_sigmoid(ff.astype(jnp.float32) + fox_f_bias[l].astype(jnp.float32))
        shp = (B, S, FOX_HEADS, FOX_HEAD_DIM)
        ya = forgetting_attention(fq.reshape(shp), fk.reshape(shp), fv.reshape(shp), log_fa)
        ya = ya.reshape(B, S, FOX_WIDTH) @ w_a_up[l]

        lb = lb_all[l]
        f_gate = lb + (1.0 - lb) * jax.nn.sigmoid(hf.astype(jnp.float32))
        log_fb = jnp.log(f_gate).reshape(B, S, HG_HEADS, HG_KEY_DIM)
        k_in = (1.0 - f_gate).reshape(B, S, HG_HEADS, HG_KEY_DIM)
        q_in = jax.nn.silu(hq.astype(jnp.float32)).reshape(B, S, HG_HEADS, HG_KEY_DIM)
        v_in = hi.astype(jnp.float32).reshape(B, S, HG_HEADS, HG_VAL_DIM)
        ob = hgrn2_recurrence(q_in, k_in, v_in, log_fb)
        ob = ob * lax.rsqrt(jnp.mean(ob * ob, axis=-1, keepdims=True) + EPS)
        ob = ob.reshape(B, S, HG_VW) * hg_norm_g[l].astype(jnp.float32)
        ob = (ob * jax.nn.silu(hgate.astype(jnp.float32))).astype(x.dtype)
        yb = ob @ w_b_up[l]

        merged = jax.nn.sigmoid(ga) * ya + jax.nn.sigmoid(gb) * yb
        x = x + merged @ w_o[l]

        h2 = rms_norm(x, norm2_g[l])
        x = x + peer_layer(h2, peer_wq[l], peer_keys[l], peer_u[l], peer_v[l])
    return rms_norm(x, norm_f_g)


_drawn_inputs = setup_inputs


def setup_inputs(seed=0):
    import zlib

    import numpy as np

    out = dict(_drawn_inputs(seed))
    spreads = {}
    factors = {'norm1_g': 4.518,
     'fox_f_bias': 3.882,
     'hg_lb_logits': 8.0,
     'hg_norm_g': 21.357,
     'norm2_g': 64.0,
     'norm_f_g': 7.763}
    for name, (base, spread) in spreads.items():
        noise = np.random.default_rng([zlib.crc32(name.encode()), seed]).standard_normal(out[name].shape)
        drawn = base * np.exp(spread * noise) if base else spread * noise
        out[name] = __import__('jax').numpy.asarray(drawn.astype(out[name].dtype))
    for name, factor in factors.items():
        out[name] = (out[name] * factor).astype(out[name].dtype)
    return out
```

```python
import numpy as np
import concourse.bass as bass
from concourse import mybir
from contextlib import ExitStack

P = 128
S = 256
NT = S // P
D = 2048
KD = D // P
H = 8
HW = H * P
GW = 512
FB = GW // P
CH = 64
EPS = 1e-6
TOPK = 16
NSEL = H * TOPK
SCALE = float(P) ** -0.5
COL_FQ, COL_FV, COL_FF = 0, 2 * HW, 3 * HW
COL_HQ = COL_FF + H
COL_HI = COL_HQ + 2 * HW
COL_GA = COL_HI + 2 * HW
COL_GB = COL_GA + D
G_HQF, G_HIG, G_FQK, G_FV, G_GA, G_AUP, G_GB, G_WO, G_WQ, G_END = 0, 4, 8, 12, 14, 18, 22, 30, 34, 38
LEVELS = 8
MASKED = LEVELS - 1
SLOTS = 8
NEG = -1.0e30
TANH_A, TANH_B = 0.7978845608028654, 0.044715


def scratch_uses():
    uses = [("vectors", 0)] + [(f"h{n}", n % 2) for n in range(4)]
    for lv in range(MASKED):
        uses += [(f"level{lv}a", 0), (f"level{lv}b", 1)]
    uses += [("across", 0), ("forget", 1), ("diagonala", 0), ("diagonalb", 1), ("cumulative", 0),
             ("o1", 1), ("o0", 0), ("ob1", 1), ("ob0", 0)]
    for pair in range(4):
        uses += [(f"qk{pair}", 0), (f"pT{pair}", 1), (f"pv{pair}", 1)]
    uses += [(f"keys{n}", n) for n in range(2)]
    uses += [(f"h2{n}", n % 2) for n in range(4)]
    uses += [(f"score{n}", n % 2) for n in range(4)]
    return uses


USES = scratch_uses()


def half_of(name):
    return dict(USES)[name]


def use_number(name):
    half, count = half_of(name), 0
    for other, h in USES:
        count += h == half
        if other == name:
            return count


class Chain:

    def __init__(self, engine, sem):
        self.engine, self.sem, self.n, self.turn = engine, sem, 0, 0

    def link(self, instruction):
        self.n += 1
        instruction.then_inc(self.sem, 1)
        self.engine.wait_ge(self.sem, self.n + self.turn)

    def enter(self, i, links):
        self.turn, self.start, self.links = i * links, self.n, links

    def leave(self, turns):
        assert self.n - self.start == self.links, (self.n - self.start, self.links)
        self.n, self.turn = self.start + self.links * turns, 0


def build(nc, x, norm1_g, w_in, fox_f_bias, hg_lb_logits, hg_norm_g, w_a_up, w_b_up, w_o, norm2_g,
          peer_wq, peer_keys, peer_u, peer_v, norm_f_g, out):
    fp32, u32 = mybir.dt.float32, mybir.dt.uint32
    ALU, ACT, AX = mybir.AluOpType, mybir.ActivationFunctionType, mybir.AxisListType
    ds = bass.ds

    x_d = x.rearrange("b (t p) d -> p (b t) d", p=P)
    out_d = out.rearrange("b (t p) d -> p (b t) d", p=P)
    w_in_d = w_in.rearrange("l (k p) n -> p (l k) n", p=P)
    w_a_d = w_a_up.rearrange("l (k p) n -> p (l k) n", p=P)
    w_b_d = w_b_up.rearrange("l (k p) n -> p (l k) n", p=P)
    w_o_d = w_o.rearrange("l (k p) n -> p (l k) n", p=P)
    wq_d = peer_wq.rearrange("l (k p) n -> p (l k) n", p=P)
    keys_d = peer_keys.rearrange("l h c n d -> n (l h c) d")
    u_rows = peer_u.rearrange("l e d -> (l e) d")
    v_rows = peer_v.rearrange("l e d -> (l e) d")

    ctx = ExitStack()
    with ctx:
        def sb(name, shape, dt=fp32):
            return ctx.enter_context(nc.sbuf_tensor(name, shape, dt))

        def sem(name):
            return ctx.enter_context(nc.semaphore(name))

        X = sb("X", [P, NT, D])
        hT = sb("hT", [P, KD, S])
        W = sb("W", [P, 2, KD * GW])
        Z1 = sb("Z1", [P, 16 * S])
        N1 = sb("N1", [P, NT, D])
        Z2 = sb("Z2", [P, 16 * S])
        V1 = sb("V1", [P, NT * HW])
        T1 = sb("T1", [P, 16 * S])
        T2 = sb("T2", [P, 16 * S])
        A2 = sb("A2", [P, 3 * HW])
        masks = sb("masks", [P, LEVELS, P])
        ident = sb("ident", [P, P])
        fox_mask = sb("fox_mask", [P, S])
        vec = sb("vec", [32, P])
        vecT = sb("vecT", [P, 32])
        wff = sb("wff", [P, KD, H])
        ff_bias = sb("ff_bias", [H, 1])
        ff = sb("ff", [H, 4, S])
        c_tok = sb("c_tok", [P, NT, H])
        lb = sb("lb", [P, 4, H])
        stat = sb("stat", [P, 6, 16])
        fstat = sb("fstat", [P, 3, 16])
        iota16 = sb("iota16", [P, TOPK])

        peer_room = hT[:, :, :].rearrange("p k s -> p (k s)")
        room = [0]

        def carve(*shape):
            n = int(np.prod(shape))
            lo, room[0] = room[0], room[0] + n
            assert room[0] <= KD * S
            a = peer_room[:, lo:lo + n]
            return a if len(shape) == 1 else a.rearrange("p (a b) -> p a b", b=shape[1])

        topv, topf, topi = carve(16, TOPK), carve(16, TOPK), carve(16, TOPK).bitcast(u32)
        best, expert = carve(NT, NSEL), carve(NT, NSEL).bitcast(u32)
        bpos, bposf, rest = carve(3, NSEL).bitcast(u32), carve(4, NSEL), carve(2 * P)
        gate, hid = carve(2, NSEL), carve(3, NSEL)
        stage = sb("stage", [P, 2, SLOTS], u32)
        gsum = sb("gsum", [P, 2, H])

        q_hg, k_hg = Z1[:, 0:8 * S], Z1[:, 8 * S:16 * S]
        o_hg = Z1[:, 0:8 * S].rearrange("p (t f) -> p t f", t=NT)
        obT = Z1[:, 8 * S:16 * S].rearrange("p (h s) -> p h s", h=H)
        scores = Z1[:, :].rearrange("p (t u n) -> p t u n", t=NT, n=P)
        hg_v, hg_gate = N1[:, :, 0:HW], N1[:, :, HW:D]
        fqT = Z2[:, 0:8 * S].rearrange("p (h s) -> p h s", h=H)
        fkT = Z2[:, 8 * S:16 * S].rearrange("p (h s) -> p h s", h=H)
        pqT = Z2[:, :].rearrange("p (u s) -> p u s", s=S)
        fv = V1[:, :].rearrange("p (t f) -> p t f", t=NT)
        keysT = V1[:, :].rearrange("p (u n) -> p u n", n=P)
        b_chunk, b_tile = T1[:, 0:8 * S], T1[:, 8 * S:16 * S]
        merged = T1[:, :].rearrange("p (k s) -> p k s", s=S)
        level = [T2[:, 0:8 * S], T2[:, 8 * S:16 * S]]
        hg_gain = T2[:, 0:HW]
        prob = T2[:, 2 * HW:2 * HW + 2 * 384].rearrange("p (a s) -> p a s", a=2)
        probT = T2[:, 3 * HW:3 * HW + 2 * 384].rearrange("p (a s) -> p a s", a=2)
        gain2, gain_f = T1[:, 0:D], T1[:, D:2 * D]
        cand, hot = T2[:, 0:D], T2[:, D:2 * D]
        attn = A2[:, 0:2 * HW].rearrange("p (u s) -> p u s", s=P)
        attn_across = A2[:, 2 * HW:3 * HW].rearrange("p (h s) -> p h s", s=P)
        yaT = A2[:, 0:2 * HW].rearrange("p (h s) -> p h s", h=H)
        keys_sb = A2[:, 0:2 * HW].rearrange("p (u d) -> p u d", d=P)
        slots = W[:, :, :].rearrange("p a n -> p (a n)").rearrange("p (j d) -> p j d", j=SLOTS)
        diag = masks

        acc = ctx.enter_context(nc.psum_tensor("acc", [P, 2, 2 * GW], fp32))
        scr = ctx.enter_context(nc.psum_tensor("scr", [P, 2, 2 * GW], fp32))

        x_in, vec_in, small_in = sem("x_in"), sem("vec_in"), sem("small_in")
        w_landed = [sem("w_landed0"), sem("w_landed1")]
        group_done = sem("group_done")
        acc_free = [sem("acc_free0"), sem("acc_free1")]
        scr_ready = [sem("scr_ready0"), sem("scr_ready1")]
        scr_free = [sem("scr_free0"), sem("scr_free1")]
        consts_ready, pool_step = sem("consts_ready"), sem("pool_step")
        dve_step, act_step = sem("dve_step"), sem("act_step")
        mean_ready, root_ready = sem("mean_ready"), sem("root_ready")
        normed, h_ready = sem("normed"), sem("h_ready")
        lb_diff, lb_exp = sem("lb_diff"), sem("lb_exp")
        hqf_ready, hqf_act = sem("hqf_ready"), sem("hqf_act")
        f_ready, logf_ready = sem("f_ready"), sem("logf_ready")
        hgate_in, hgate_ready = sem("hgate_in"), sem("hgate_ready")
        kq_ready = sem("kq_ready")
        diff_ready, decay_ready, level_ready = sem("diff_ready"), sem("decay_ready"), sem("level_ready")
        attn_ready = sem("attn_ready")
        ff_in, ff_exp, c_ready = sem("ff_in"), sem("ff_exp"), sem("c_ready")
        gain_free, hg_gain_in = sem("gain_free"), sem("hg_gain_in")
        ob_ready, obT_ready = sem("ob_ready"), sem("obT_ready")
        fox_ready = sem("fox_ready")
        logit_ready, exp_ready, p_ready = sem("logit_ready"), sem("exp_ready"), sem("p_ready")
        pT_ready, ya_ready = sem("pT_ready"), sem("ya_ready")
        ga_in, ga_ready = sem("ga_in"), sem("ga_ready")
        gb_ready, gb_used = sem("gb_ready"), sem("gb_used")
        merged_ready = sem("merged_ready")
        keys_in, gains_in = sem("keys_in"), sem("gains_in")
        keysT_ready, q_ready = sem("keysT_ready"), sem("q_ready")
        shifted, gate_exp = sem("shifted"), sem("gate_exp")
        expert_ready = sem("expert_ready")
        granted, granted_w = sem("granted"), sem("granted_w")
        row_landed = [sem(f"row_landed{j}") for j in range(SLOTS)]
        row_used = [sem(f"row_used{j}") for j in range(SLOTS)]
        tanh_in, tanh_ready, weight_ready = sem("tanh_in"), sem("tanh_ready"), sem("weight_ready")
        diag_ready = [sem(f"diag_ready{j}") for j in range(SLOTS)]
        y_done = sem("y_done")
        y_ready, out_done = sem("y_ready"), sem("out_done")

        block = ctx.enter_context(nc.Block())

        @block.sync
        def _(sp):
            sp.dma_start(X[:, :, :], x_d).then_inc(x_in, 16)
            sp.dma_start(vec[0:16, :], norm1_g.rearrange("l (k p) -> (l k) p", p=P)).then_inc(vec_in, 16)
            sp.dma_start(vec[16:32, :], hg_lb_logits.rearrange("l (h p) -> (l h) p", p=P)).then_inc(vec_in, 16)

            def load(slot, pair, src, cols, turn=0, first=False):
                if not first:
                    sp.wait_ge(group_done, 2 * pair + slot - 1 + 2 * turn)
                    sp.sem_inc(granted_w, 1)
                kb = src.shape[1]
                sp.dma_start(W[:, slot, 0:kb * GW].rearrange("p (k n) -> p k n", n=GW),
                             src[:, :, cols]).then_inc(w_landed[slot], 16)

            def load_loop(g0, groups, src, col0):
                with sp.Fori(0, groups // 2) as i:
                    for slot in range(2):
                        load(slot, g0 // 2, src, ds(col0 + (2 * i + slot) * GW, GW), turn=i)

            for slot in range(2):
                load(slot, 0, w_in_d, slice(COL_HQ + slot * GW, COL_HQ + (slot + 1) * GW), first=True)
            sp.dma_start(wff[:, :, :], w_in_d[:, :, COL_FF:COL_FF + H]).then_inc(small_in, 16)
            sp.dma_start(ff_bias[:, :], fox_f_bias.rearrange("l h -> h l")).then_inc(small_in, 16)
            load_loop(G_HQF + 2, 2, w_in_d, COL_HQ + 2 * GW)
            load_loop(G_HIG, 4, w_in_d, COL_HI)
            load_loop(G_FQK, 4, w_in_d, COL_FQ)
            load_loop(G_FV, 2, w_in_d, COL_FV)
            load_loop(G_GA, 4, w_in_d, COL_GA)
            load_loop(G_AUP, 4, w_a_d, 0)
            with sp.Fori(0, 4) as i:
                load(0, G_GB // 2, w_in_d, ds(COL_GB + i * GW, GW), turn=i)
                load(1, G_GB // 2, w_b_d, ds(i * GW, GW), turn=i)
            load_loop(G_WO, 4, w_o_d, 0)
            load_loop(G_WQ, 4, wq_d, 0)
            for t in range(NT):
                sp.wait_ge(y_ready, t + 1)
                sp.dma_start(out_d[:, t, :], X[:, t, :]).then_inc(out_done, 16)
            sp.wait_ge(out_done, 16 * NT)

        @block.gpsimd
        def _(pool):
            g = nc.gpsimd
            steps = Chain(pool, pool_step)
            g.memset(ident[:, :], 0.0)
            g.memset(masks[:, :, :], 0.0)
            steps.link(g.memset(fox_mask[:, :], 0.0))
            g.affine_select(out=ident[:, :], in_=ident[:, :], compare_op=ALU.not_equal, fill=1.0, base=0,
                            pattern=[[-1, P]], channel_multiplier=1)
            steps.link(g.affine_select(out=fox_mask[:, P:S], in_=fox_mask[:, P:S], compare_op=ALU.is_ge,
                                       fill=NEG, base=0, pattern=[[-1, P]], channel_multiplier=1))
            steps.link(g.iota(iota16[:, :], [[1, TOPK]], base=0, channel_multiplier=0,
                              allow_small_or_imprecise_dtypes=True))
            halves = []
            for lv in range(MASKED):
                half = 1 << lv
                halves.append(masks[:, lv, :].rearrange("p (n u h) -> p n u h", u=2, h=half)[:, :, 1, :])
                last = g.memset(halves[lv], 1.0)
            steps.link(last)
            for lv in range(MASKED):
                half, n = 1 << lv, P >> (lv + 1)
                last = g.affine_select(out=halves[lv], in_=halves[lv], compare_op=ALU.is_ge, fill=0.0, base=0,
                                       pattern=[[-2 * half, n], [0, half]], channel_multiplier=1)
            steps.link(last)
            for lv in range(MASKED):
                half, n = 1 << lv, P >> (lv + 1)
                g.affine_select(out=halves[lv], in_=halves[lv], compare_op=ALU.is_ge, fill=0.0, base=half - 1,
                                pattern=[[2 * half, n], [0, half]], channel_multiplier=-1)
            g.affine_select(out=masks[:, MASKED, :], in_=masks[:, MASKED, :], compare_op=ALU.not_equal, fill=1.0,
                            base=0, pattern=[[-1, P]], channel_multiplier=1).then_inc(consts_ready, 1)
            pool.wait_ge(gain_free, 1)
            pool.dma_start(hg_gain, hg_norm_g.partition_broadcast(P).rearrange("q l f -> q (l f)")).then_inc(hg_gain_in, 16)
            pool.wait_ge(group_done, G_AUP + 4)
            pool.dma_start(keys_sb, keys_d).then_inc(keys_in, 16)
            pool.wait_ge(group_done, G_WO + 4)
            pool.dma_start(gain2, norm2_g.partition_broadcast(P).rearrange("q l f -> q (l f)")).then_inc(gains_in, 16)
            pool.dma_start(gain_f, norm_f_g.rearrange("(l f) -> l f", l=1).partition_broadcast(P)
                           .rearrange("q l f -> q (l f)")).then_inc(gains_in, 16)
            pool.wait_ge(group_done, G_END)
            rounds = NSEL // SLOTS
            for t in range(NT):
                pool.wait_ge(expert_ready, t + 1)
                for table in range(2):
                    first_round = (2 * t + table) * rounds
                    rows = (u_rows, v_rows)[table]
                    with pool.Fori(0, rounds // 2) as i:
                        steps.enter(i, 2)
                        for side in range(2):
                            steps.link(g.tensor_copy(stage[:, side, :],
                                                     expert[:, t, ds((2 * i + side) * SLOTS, SLOTS)]))
                            for j in range(SLOTS):
                                pool.wait_ge(row_used[j], 1 + first_round + 2 * i + side)
                                pool.sem_inc(granted, 1)
                                pool.indirect_dma_start(slots[:, j, :], None, rows,
                                                        bass.IndirectOffsetOnAxis(ap=stage[:, side, j:j + 1], axis=0)
                                                        ).then_inc(row_landed[j], 16)
                        steps.leave(rounds // 2)

        @block.scalar
        def _(act):
            a = nc.scalar
            act.wait_ge(mean_ready, 1)
            a.activation(stat[:, 2, 0:NT], stat[:, 1, 0:NT], ACT.Sqrt).then_inc(root_ready, 1)
            act.wait_ge(lb_diff, 1)
            a.activation(lb[:, 0:2, :], lb[:, 2:4, :], ACT.Exp).then_inc(lb_exp, 1)
            act.wait_ge(hqf_ready, 1)
            a.activation(k_hg, k_hg, ACT.Sigmoid).then_inc(hqf_act, 1)
            a.activation(q_hg, q_hg, ACT.Silu).then_inc(hqf_act, 1)
            act.wait_ge(f_ready, 1)
            a.activation(b_tile, level[0], ACT.Ln).then_inc(logf_ready, 1)
            act.wait_ge(hgate_in, 1)
            a.activation(hg_gate, hg_gate, ACT.Silu).then_inc(hgate_ready, 1)
            for lv in range(LEVELS):
                act.wait_ge(diff_ready, lv + 1)
                a.activation(level[lv % 2], level[lv % 2], ACT.Exp).then_inc(decay_ready, 1)
            act.wait_ge(ff_in, 1)
            a.activation(ff[:, 1, :], ff[:, 0, :], ACT.Abs).then_inc(act_step, 1)
            act.wait_ge(act_step, 1)
            a.activation(ff[:, 2, :], ff[:, 1, :], ACT.Exp, scale=-1.0).then_inc(act_step, 1)
            act.wait_ge(act_step, 2)
            a.activation(ff[:, 1, :], ff[:, 2, :], ACT.Ln, bias=1.0).then_inc(ff_exp, 1)
            act.wait_ge(mean_ready, 2)
            a.activation(stat[:, 2, :], stat[:, 1, :], ACT.Sqrt).then_inc(root_ready, 1)
            for h in range(H):
                for t in range(NT):
                    n, lo = 2 * h + t, (0, P)[t]
                    act.wait_ge(logit_ready, n + 1)
                    p = prob[:, h % 2, lo:lo + (t + 1) * P]
                    a.activation(p, p, ACT.Exp, bias=fstat[:, 0, n:n + 1],
                                 accum_out=fstat[:, 1, n:n + 1]).then_inc(exp_ready, 1)
            act.wait_ge(ga_in, 1)
            a.activation(T1[:, :], T1[:, :], ACT.Sigmoid).then_inc(ga_ready, 1)
            with act.Fori(0, 4) as i:
                act.wait_ge(group_done, G_GB + 2 * i + 1)
                act.wait_ge(gb_used, 1 + i)
                act.sem_inc(act_step, 1)
                a.activation(T2[:, 0:2 * GW], acc[:, 0, :], ACT.Sigmoid).then_inc(gb_ready, 1)
                act.wait_ge(gb_ready, i + 1)
                act.sem_inc(acc_free[0], 1)
            act.wait_ge(mean_ready, 3)
            a.activation(stat[:, 2, 0:NT], stat[:, 1, 0:NT], ACT.Sqrt).then_inc(root_ready, 1)
            for t in range(NT):
                act.wait_ge(shifted, t + 1)
                a.activation(gate[:, 0, :], gate[:, 0, :], ACT.Exp).then_inc(gate_exp, 1)
                act.wait_ge(tanh_in, t + 1)
                a.activation(hid[:, 1, :], hid[:, 1, :], ACT.Tanh).then_inc(tanh_ready, 1)
                act.wait_ge(weight_ready, t + 1)
                rounds = NSEL // SLOTS
                with act.Fori(0, rounds) as i:
                    for j in range(SLOTS):
                        act.wait_ge(row_used[j], 1 + (2 * t + 1) * rounds + i)
                        act.sem_inc(act_step, 1)
                        a.activation(diag[:, j, :], ident[:, :], ACT.Copy,
                                     scale=gate[:, 1, ds(i * SLOTS + j, 1)]).then_inc(diag_ready[j], 1)
            act.wait_ge(mean_ready, 4)
            a.activation(stat[:, 2, 0:NT], stat[:, 1, 0:NT], ACT.Sqrt).then_inc(root_ready, 1)

        @block.vector
        def _(dve):
            v = nc.vector
            steps = Chain(dve, dve_step)
            link = steps.link
            for free in (*acc_free, *row_used, gb_used):
                dve.sem_inc(free, 1)

            def evacuated(ins, slot):
                ins.then_inc(acc_free[slot], 1)

            def scratch(name):
                dve.wait_ge(scr_ready[half_of(name)], use_number(name))
                return half_of(name)

            def inverse_root(n, width, count):
                m, root, r, s = (stat[:, k, 0:n] for k in (1, 2, 3, 4))
                v.tensor_scalar(m, stat[:, 0, 0:n], 1.0 / width, EPS, ALU.mult, ALU.add).then_inc(mean_ready, 1)
                dve.wait_ge(root_ready, count)
                link(v.reciprocal(r, root))
                link(v.tensor_tensor(s, r, r, ALU.mult))
                link(v.tensor_tensor(s, s, m, ALU.mult))
                link(v.tensor_scalar(s, s, -0.5, 1.5, ALU.mult, ALU.add))
                link(v.tensor_tensor(r, r, s, ALU.mult))

            dve.wait_ge(x_in, 16)
            for t in range(NT):
                link(v.scalar_tensor_tensor(out=N1[:, t, :], in0=X[:, t, :], scalar=1.0, in1=X[:, t, :],
                                            op0=ALU.mult, op1=ALU.mult, accum_out=stat[:, 0, t:t + 1]))
            inverse_root(NT, D, 1)
            for t in range(NT):
                v.tensor_scalar(N1[:, t, :], X[:, t, :], stat[:, 3, t:t + 1], None, ALU.mult).then_inc(normed, 1)
            half = scratch("vectors")
            link(v.tensor_copy(vecT[:, :], scr[:, half, 0:32]))
            dve.sem_inc(scr_free[half], 1)
            for n in range(4):
                half = scratch(f"h{n}")
                for k in range(4):
                    last = v.tensor_scalar(hT[:, 4 * n + k, :], scr[:, half, k * S:(k + 1) * S],
                                           vecT[:, 4 * n + k:4 * n + k + 1], None, ALU.mult)
                last.then_inc(scr_free[half], 1)
            dve.wait_ge(scr_free[half], use_number("h3"))
            dve.sem_inc(h_ready, 1)

            l0, l1 = vecT[:, 16:24], vecT[:, 24:32]
            link(v.tensor_tensor(lb[:, 0, :], l0, l1, ALU.max))
            v.tensor_tensor(lb[:, 2, :], l0, lb[:, 0, :], ALU.subtract)
            v.tensor_tensor(lb[:, 3, :], l1, lb[:, 0, :], ALU.subtract).then_inc(lb_diff, 1)
            dve.wait_ge(lb_exp, 1)
            link(v.tensor_tensor(lb[:, 2, :], lb[:, 0, :], lb[:, 1, :], ALU.add))
            link(v.reciprocal(lb[:, 2, :], lb[:, 2, :]))
            link(v.tensor_tensor(lb[:, 0, :], lb[:, 0, :], lb[:, 2, :], ALU.mult))
            link(v.tensor_scalar(lb[:, 1, :], lb[:, 0, :], -1.0, 1.0, ALU.mult, ALU.add))

            def copy_groups(g0, groups, dst):
                with dve.Fori(0, groups // 2) as i:
                    for slot in range(2):
                        dve.wait_ge(group_done, g0 + slot + 1 + 2 * i)
                        src = acc[:, slot, :]
                        to = dst(2 * i + slot)
                        if len(to.shape) == 3:
                            src = src.rearrange("p (t n) -> p t n", t=NT)
                        evacuated(v.tensor_copy(to, src), slot)

            copy_groups(G_HQF, 4, lambda n: Z1[:, ds(n * 2 * GW, 2 * GW)])
            dve.wait_ge(acc_free[1], 1 + 2)
            dve.wait_ge(acc_free[0], 1 + 2)
            dve.sem_inc(hqf_ready, 1)

            reset = level[1]
            link(v.memset(reset, 1.0))
            link(v.memset(reset.rearrange("p (c s) -> p c s", s=CH)[:, :, 0:1], 0.0))
            dve.wait_ge(hqf_act, 1)
            f = level[0]
            for h in range(H):
                last = v.tensor_scalar(f[:, h * S:(h + 1) * S], k_hg[:, h * S:(h + 1) * S], lb[:, 1, h:h + 1],
                                       lb[:, 0, h:h + 1], ALU.mult, ALU.add)
            last.then_inc(f_ready, 1)
            dve.wait_ge(f_ready, 1)
            dve.wait_ge(hqf_act, 2)
            v.tensor_scalar(k_hg, f, -1.0, 1.0, ALU.mult, ALU.add).then_inc(kq_ready, 1)
            dve.wait_ge(logf_ready, 1)
            dve.wait_ge(kq_ready, 1)
            link(v.tensor_tensor_scan(b_chunk, reset, b_tile, 0.0, ALU.mult, ALU.add))
            bc = b_chunk.rearrange("p (u c s) -> p u c s", c=2, s=CH)
            bt = b_tile.rearrange("p (u c s) -> p u c s", c=2, s=CH)
            v.tensor_copy(bt[:, :, 0, :], bc[:, :, 0, :])
            link(v.tensor_tensor(bt[:, :, 1, :], bc[:, :, 1, :], bc[:, :, 0, CH - 1:CH].to_broadcast([P, 2 * H, CH]),
                                 ALU.add))
            copy_groups(G_HIG, 4, lambda n: N1[:, :, ds(n * GW, GW)])
            dve.wait_ge(acc_free[1], 1 + 4)
            dve.wait_ge(acc_free[0], 1 + 4)
            dve.sem_inc(hgate_in, 1)
            link(v.memset(A2[:, :], 0.0))

            def prepare(lv):
                if lv >= 2:
                    dve.wait_ge(scr_ready[1], use_number(f"level{lv - 2}b"))
                size = 2 << lv
                blocks = 8 * S // size

                def halves(a):
                    v4 = a.rearrange("p (n u h) -> p n u h", u=2, h=size // 2)
                    return v4[:, :, 0, :], v4[:, :, 1, :]

                e_lo, e_up = halves(level[lv % 2])
                b = b_tile if lv == LEVELS - 1 else b_chunk
                b_lo, b_up = halves(b)
                ref = b_lo[:, :, size // 2 - 1:size // 2].to_broadcast([P, blocks, size // 2])
                v.tensor_tensor(e_lo, ref, b_lo, ALU.subtract)
                if lv < LEVELS - 2:
                    last = v.tensor_tensor(e_up, b_up, ref, ALU.subtract)
                else:
                    last = v.tensor_copy(e_up, b_up)
                last.then_inc(diff_ready, 1)
                dve.wait_ge(decay_ready, lv + 1)
                k_lo, _ = halves(k_hg)
                _, q_up = halves(q_hg)
                v.tensor_tensor(e_lo, e_lo, k_lo, ALU.mult)
                v.tensor_tensor(e_up, e_up, q_up, ALU.mult).then_inc(level_ready, 1)

            def place(name, lv, side):
                half = scratch(name)
                to = attn[:, side * H:(side + 1) * H, :]
                mask = masks[:, lv:lv + 1, :].to_broadcast([P, H, P]).bitcast(u32)
                v.copy_predicated(to, mask, scr[:, half, :].rearrange("p (u s) -> p u s", s=P)
                                  ).then_inc(scr_free[half], 1)

            def copy_group(g, to):
                dve.wait_ge(group_done, g + 1)
                src = acc[:, g % 2, :]
                if len(to.shape) == 3:
                    src = src.rearrange("p (t n) -> p t n", t=NT)
                evacuated(v.tensor_copy(to, src), g % 2)

            dve.wait_ge(consts_ready, 1)
            prepare(0)
            prepare(1)
            for n in range(4):
                copy_group(G_FQK + n, Z2[:, n * 2 * GW:(n + 1) * 2 * GW])
                for lv in (2 * n, 2 * n + 1):
                    if lv == LEVELS - 1:
                        half = scratch("across")
                        v.tensor_copy(attn_across, scr[:, half, :].rearrange("p (h s) -> p h s", s=P)
                                      ).then_inc(scr_free[half], 1)
                    else:
                        if lv:
                            dve.wait_ge(scr_free[1], use_number(f"level{lv - 1}b"))
                        place(f"level{lv}a", lv, 0)
                        place(f"level{lv}b", lv, 1)
                    if lv + 2 < LEVELS:
                        prepare(lv + 2)
            dve.wait_ge(scr_free[1], use_number(f"level{MASKED - 1}b"))
            dve.wait_ge(scr_free[0], use_number("across"))
            dve.sem_inc(gain_free, 1)
            link(v.tensor_scalar(Z2[:, 0:8 * S], Z2[:, 0:8 * S], SCALE, None, ALU.mult))
            half = scratch("forget")
            dve.wait_ge(small_in, 32)
            v.tensor_scalar(ff[:, 0, :], scr[0:H, half, 0:S], ff_bias[:, 0:1], None, ALU.add).then_inc(ff_in, 1)
            dve.wait_ge(ff_in, 1)
            dve.sem_inc(scr_free[half], 1)
            place("diagonala", MASKED, 0)
            place("diagonalb", MASKED, 1)
            dve.wait_ge(scr_free[0], use_number("diagonala"))
            dve.wait_ge(scr_free[1], use_number("diagonalb"))
            dve.sem_inc(attn_ready, 1)
            dve.wait_ge(ff_exp, 1)
            link(v.scalar_tensor_tensor(out=ff[:, 2, :], in0=ff[:, 0, :], scalar=0.0, in1=ff[:, 1, :],
                                        op0=ALU.min, op1=ALU.subtract))
            link(v.memset(ff[:, 0, :], 1.0))
            link(v.tensor_tensor_scan(ff[:, 1, :], ff[:, 0, :], ff[:, 2, :], 0.0, ALU.mult, ALU.add))
            v.tensor_scalar(ff[:, 3, :], ff[:, 1, :], -1.0, None, ALU.mult).then_inc(c_ready, 1)
            half = scratch("cumulative")
            v.tensor_copy(c_tok[:, :, :], scr[:, half, 0:NT * H].rearrange("p (t h) -> p t h", t=NT)
                          ).then_inc(scr_free[half], 1)
            for n in range(2):
                copy_group(G_FV + n, fv[:, :, n * GW:(n + 1) * GW])
            dve.wait_ge(acc_free[0], 1 + G_GA // 2)
            dve.wait_ge(acc_free[1], 1 + G_GA // 2)
            dve.sem_inc(fox_ready, 1)
            for t in (1, 0):
                half = scratch(f"o{t}")
                v.tensor_copy(o_hg[:, t, :], scr[:, half, :]).then_inc(scr_free[half], 1)
            dve.wait_ge(scr_free[0], use_number("o0"))
            dve.wait_ge(scr_free[1], use_number("o1"))
            o_flat = Z1[:, 0:8 * S]
            sq = T2[:, HW:3 * HW]
            link(v.tensor_tensor(sq, o_flat, o_flat, ALU.mult))
            link(v.tensor_reduce(stat[:, 0, :], sq.rearrange("p (u n) -> p u n", n=P), AX.X, ALU.add))
            inverse_root(16, P, 2)
            o_heads = o_flat.rearrange("p (u n) -> p u n", n=P)
            link(v.tensor_tensor(o_heads, o_heads, stat[:, 3, :].unsqueeze(2).to_broadcast([P, 16, P]), ALU.mult))
            dve.wait_ge(hg_gain_in, 16)
            link(v.tensor_tensor(o_hg, o_hg, hg_gain.unsqueeze(1).to_broadcast([P, NT, HW]), ALU.mult))
            dve.wait_ge(hgate_ready, 1)
            v.tensor_tensor(o_hg, o_hg, hg_gate, ALU.mult).then_inc(ob_ready, 1)
            for t in (1, 0):
                half = scratch(f"ob{t}")
                v.tensor_copy(obT[:, :, t * P:(t + 1) * P], scr[:, half, :].rearrange("p (h s) -> p h s", h=H)
                              ).then_inc(scr_free[half], 1)
            dve.wait_ge(scr_free[0], use_number("ob0"))
            dve.wait_ge(scr_free[1], use_number("ob1"))
            dve.sem_inc(obT_ready, 1)

            def softmax(pair):
                half = scratch(f"qk{pair}")
                if pair:
                    dve.wait_ge(scr_ready[1], use_number(f"pT{pair - 1}"))
                for a in range(2):
                    h = 2 * pair + a
                    src = scr[:, half, a * GW:a * GW + 384]
                    for t in range(NT):
                        n, lo, width = 2 * h + t, (0, P)[t], (t + 1) * P
                        link(v.scalar_tensor_tensor(out=prob[:, a, lo:lo + width], in0=src[:, lo:lo + width],
                                                    scalar=c_tok[:, t, h:h + 1], in1=fox_mask[:, S - width:S],
                                                    op0=ALU.add, op1=ALU.add))
                        v.tensor_reduce(fstat[:, 0, n:n + 1], prob[:, a, lo:lo + width], AX.X, ALU.max,
                                        negate=True).then_inc(logit_ready, 1)
                dve.sem_inc(scr_free[half], 1)
                for a in range(2):
                    h = 2 * pair + a
                    dve.wait_ge(exp_ready, 2 * h + 2)
                    link(v.reciprocal(fstat[:, 2, 2 * h:2 * h + 2], fstat[:, 1, 2 * h:2 * h + 2]))
                    for t in range(NT):
                        n, lo, width = 2 * h + t, (0, P)[t], (t + 1) * P
                        last = v.tensor_scalar(prob[:, a, lo:lo + width], prob[:, a, lo:lo + width],
                                               fstat[:, 2, n:n + 1], None, ALU.mult)
                    last.then_inc(p_ready, 1)

            def copy_pT(pair):
                half = scratch(f"pT{pair}")
                v.tensor_copy(probT, scr[:, half, :].rearrange("p (a s) -> p a s", a=2)[:, :, 0:384]
                              ).then_inc(pT_ready, 1)
                dve.wait_ge(pT_ready, pair + 1)
                dve.sem_inc(scr_free[half], 1)

            def copy_ya(pair):
                half = scratch(f"pv{pair}")
                v.tensor_copy(yaT[:, 2 * pair:2 * pair + 2, :],
                              scr[:, half, :].rearrange("p (a s) -> p a s", a=2)[:, :, 0:S]
                              ).then_inc(scr_free[half], 1)

            dve.wait_ge(scr_free[0], use_number("cumulative"))
            for n in range(4):
                softmax(n)
                copy_group(G_GA + n, T1[:, n * 2 * GW:(n + 1) * 2 * GW])
                copy_pT(n)
                copy_ya(n)
            dve.wait_ge(scr_free[1], use_number("pv3"))
            dve.sem_inc(ya_ready, 1)
            dve.wait_ge(acc_free[0], 1 + G_AUP // 2)
            dve.wait_ge(acc_free[1], 1 + G_AUP // 2)
            dve.sem_inc(ga_in, 1)

            dve.wait_ge(ga_ready, 1)
            with dve.Fori(0, 2) as i:
                for slot in range(2):
                    dve.wait_ge(group_done, G_AUP + slot + 1 + 2 * i)
                    part = T1[:, ds((2 * i + slot) * 2 * GW, 2 * GW)]
                    evacuated(v.tensor_tensor(part, part, acc[:, slot, :], ALU.mult), slot)
            gated = T2[:, 2 * GW:4 * GW]
            with dve.Fori(0, 4) as i:
                steps.enter(i, 1)
                dve.wait_ge(group_done, G_GB + 2 * i + 2)
                dve.wait_ge(gb_ready, i + 1)
                dve.wait_ge(gb_used, 1 + i)
                evac = v.tensor_tensor(gated, T2[:, 0:2 * GW], acc[:, 1, :], ALU.mult)
                link(evac)
                dve.sem_inc(acc_free[1], 1)
                part = T1[:, ds(i * 2 * GW, 2 * GW)]
                v.tensor_tensor(part, part, gated, ALU.add).then_inc(gb_used, 1)
                steps.leave(4)
            dve.wait_ge(gb_used, 1 + 4)
            dve.sem_inc(merged_ready, 1)
            for n in range(2):
                half = scratch(f"keys{n}")
                v.tensor_copy(V1[:, n * HW:(n + 1) * HW], scr[:, half, :]).then_inc(scr_free[half], 1)
            with dve.Fori(0, 2) as i:
                for slot in range(2):
                    dve.wait_ge(group_done, G_WO + slot + 1 + 2 * i)
                    part = X[:, :, ds((2 * i + slot) * GW, GW)]
                    evacuated(v.tensor_tensor(part, part, acc[:, slot, :].rearrange("p (t n) -> p t n", t=NT),
                                              ALU.add), slot)
            dve.wait_ge(acc_free[0], 1 + G_WQ // 2)
            dve.wait_ge(acc_free[1], 1 + G_WQ // 2)
            for t in range(NT):
                link(v.scalar_tensor_tensor(out=N1[:, t, :], in0=X[:, t, :], scalar=1.0, in1=X[:, t, :],
                                            op0=ALU.mult, op1=ALU.mult, accum_out=stat[:, 0, t:t + 1]))
            inverse_root(NT, D, 3)
            dve.wait_ge(gains_in, 32)
            for t in range(NT):
                v.scalar_tensor_tensor(out=N1[:, t, :], in0=X[:, t, :], scalar=stat[:, 3, t:t + 1], in1=gain2,
                                       op0=ALU.mult, op1=ALU.mult).then_inc(normed, 1)
            for n in range(4):
                half = scratch(f"h2{n}")
                last = v.tensor_copy(hT[:, 4 * n:4 * n + 4, :], scr[:, half, :].rearrange("p (k s) -> p k s", s=S))
                last.then_inc(scr_free[half], 1)
            dve.wait_ge(scr_free[0], use_number("h22"))
            dve.wait_ge(scr_free[1], use_number("h23"))
            dve.sem_inc(h_ready, 1)
            copy_groups(G_WQ, 4, lambda n: Z2[:, ds(n * 2 * GW, 2 * GW)])
            dve.wait_ge(acc_free[0], 1 + G_END // 2)
            dve.wait_ge(acc_free[1], 1 + G_END // 2)
            dve.sem_inc(q_ready, 1)
            for n in range(4):
                half = scratch(f"score{n}")
                v.tensor_copy(Z1[:, n * HW:(n + 1) * HW], scr[:, half, :]).then_inc(scr_free[half], 1)

            def top16(values, src, indices):
                w = src.shape[1]
                link(v.max(values[:, 0:8], src))
                v.max_index(indices[:, 0:8], values[:, 0:8], src)
                link(v.match_replace(rest[:, 0:w], values[:, 0:8], src, -3.0e38))
                link(v.max(values[:, 8:16], rest[:, 0:w]))
                link(v.max_index(indices[:, 8:16], values[:, 8:16], rest[:, 0:w]))

            def select(t):
                for u in range(16):
                    top16(topv[:, u, :], scores[:, t, u, :], topi[:, u, :])
                link(v.tensor_copy(topf[:, :, :], topi[:, :, :]))
                tv = topv[:, :, :].rearrange("p (h c) k -> p h c k", c=2)
                tf = topf[:, :, :].rearrange("p (h c) k -> p h c k", c=2)
                pairs = cand.rearrange("p (h i j) -> p h i j", i=TOPK, j=TOPK)
                link(v.tensor_tensor(pairs, tv[:, :, 0, :].unsqueeze(3).to_broadcast([P, H, TOPK, TOPK]),
                                     tv[:, :, 1, :].unsqueeze(2).to_broadcast([P, H, TOPK, TOPK]), ALU.add))
                for h in range(H):
                    top16(best[:, t, h * TOPK:(h + 1) * TOPK], cand[:, h * S:(h + 1) * S],
                          bpos[:, 0, h * TOPK:(h + 1) * TOPK])
                v.tensor_scalar(bpos[:, 1, :], bpos[:, 0, :], 4, None, ALU.logical_shift_right)
                link(v.tensor_scalar(bpos[:, 2, :], bpos[:, 0, :], TOPK - 1, None, ALU.bitwise_and))
                link(v.tensor_copy(bposf[:, 0:2, :], bpos[:, 1:3, :]))
                hots = hot.rearrange("p (m i) -> p m i", i=TOPK)
                hot4 = hot.rearrange("p (h m i) -> p h m i", m=TOPK, i=TOPK)
                for c in range(2):
                    link(v.tensor_tensor(hots, bposf[:, c, :].unsqueeze(2).to_broadcast([P, NSEL, TOPK]),
                                         iota16[:, :].unsqueeze(1).to_broadcast([P, NSEL, TOPK]), ALU.is_equal))
                    link(v.tensor_tensor(hot4, hot4, tf[:, :, c, :].unsqueeze(2).to_broadcast([P, H, TOPK, TOPK]),
                                         ALU.mult))
                    link(v.tensor_reduce(bposf[:, 2 + c, :], hots, AX.X, ALU.add))
                link(v.scalar_tensor_tensor(out=bposf[:, 2, :], in0=bposf[:, 2, :], scalar=float(P),
                                            in1=bposf[:, 3, :], op0=ALU.mult, op1=ALU.add))
                v.tensor_copy(expert[:, t, :], bposf[:, 2, :]).then_inc(expert_ready, 1)

            def dots(t):
                rounds = NSEL // SLOTS
                with dve.Fori(0, rounds) as i:
                    for j in range(SLOTS):
                        dve.wait_ge(row_landed[j], (2 * t * rounds + 1 + i) * 16)
                        v.scalar_tensor_tensor(out=slots[:, j, :], in0=slots[:, j, :], scalar=1.0, in1=N1[:, t, :],
                                               op0=ALU.mult, op1=ALU.mult,
                                               accum_out=hid[:, 0, ds(i * SLOTS + j, 1)]).then_inc(row_used[j], 1)
                for j in range(SLOTS):
                    dve.wait_ge(row_used[j], 1 + (2 * t + 1) * rounds)

            def weights(t):
                if t:
                    dve.wait_ge(y_done, t)
                g3 = gate[:, 0, :].rearrange("p (h k) -> p h k", h=H)
                b3 = best[:, t, :].rearrange("p (h k) -> p h k", h=H)
                v.tensor_tensor(g3, b3, b3[:, :, 0:1].to_broadcast([P, H, TOPK]), ALU.subtract).then_inc(shifted, 1)
                dve.wait_ge(gate_exp, t + 1)
                link(v.tensor_reduce(gsum[:, 0, :], g3, AX.X, ALU.add))
                link(v.reciprocal(gsum[:, 1, :], gsum[:, 0, :]))
                link(v.tensor_tensor(g3, g3, gsum[:, 1, :].unsqueeze(2).to_broadcast([P, H, TOPK]), ALU.mult))
                z, w = hid[:, 0, :], hid[:, 1, :]
                link(v.tensor_tensor(w, z, z, ALU.mult))
                link(v.tensor_scalar(w, w, TANH_A * TANH_B, TANH_A, ALU.mult, ALU.add))
                v.tensor_tensor(w, w, z, ALU.mult).then_inc(tanh_in, 1)
                dve.wait_ge(tanh_ready, t + 1)
                link(v.scalar_tensor_tensor(out=hid[:, 2, :], in0=w, scalar=1.0, in1=z, op0=ALU.add, op1=ALU.mult))
                v.scalar_tensor_tensor(out=gate[:, 1, :], in0=hid[:, 2, :], scalar=0.5, in1=gate[:, 0, :],
                                       op0=ALU.mult, op1=ALU.mult).then_inc(weight_ready, 1)

            dve.wait_ge(scr_free[0], use_number("score2"))
            dve.wait_ge(scr_free[1], use_number("score3"))
            select(0)
            dots(0)
            weights(0)
            select(1)
            dots(1)
            weights(1)
            y = [acc[:, :, :].rearrange("p a n -> p (a n)"), scr[:, :, :].rearrange("p a n -> p (a n)")]
            for t in range(NT):
                dve.wait_ge(y_done, t + 1)
                link(v.tensor_copy(X[:, t, :], y[t]))
                link(v.scalar_tensor_tensor(out=N1[:, t, :], in0=X[:, t, :], scalar=1.0, in1=X[:, t, :],
                                            op0=ALU.mult, op1=ALU.mult, accum_out=stat[:, 0, t:t + 1]))
            inverse_root(NT, D, 4)
            for t in range(NT):
                v.scalar_tensor_tensor(out=X[:, t, :], in0=X[:, t, :], scalar=stat[:, 3, t:t + 1], in1=gain_f,
                                       op0=ALU.mult, op1=ALU.mult).then_inc(y_ready, 1)

        @block.tensor
        def _(pe):
            t_ = nc.tensor

            def enter(name):
                if use_number(name) > 1:
                    pe.wait_ge(scr_free[half_of(name)], use_number(name) - 1)
                return half_of(name)

            def done(name, last):
                last.then_inc(scr_ready[half_of(name)], 1)

            def arrived(g0, slot, i):
                pe.wait_ge(w_landed[slot], (g0 // 2 + 1 + i) * 16)
                pe.wait_ge(acc_free[slot], 1 + g0 // 2 + i)

            def transposed(slot, kb, src):
                w = W[:, slot, 0:kb * GW].rearrange("p (k n) -> p k n", n=GW)
                for f in range(FB):
                    for k in range(kb):
                        last = t_.matmul(acc[:, slot, f * S:(f + 1) * S], w[:, k, f * P:(f + 1) * P], src[:, k, :],
                                         start=(k == 0), stop=(k == kb - 1))
                last.then_inc(group_done, 1)

            def natural(slot, src):
                w = W[:, slot, :].rearrange("p (k n) -> p k n", n=GW)
                for t in range(NT):
                    for k in range(KD):
                        last = t_.matmul(acc[:, slot, t * GW:(t + 1) * GW], src[:, k, t * P:(t + 1) * P], w[:, k, :],
                                         start=(k == 0), stop=(k == KD - 1))
                last.then_inc(group_done, 1)

            def transposed_loop(g0, groups, kb, src):
                with pe.Fori(0, groups // 2) as i:
                    for slot in range(2):
                        arrived(g0, slot, i)
                        transposed(slot, kb, src)

            def natural_loop(g0, groups, src):
                with pe.Fori(0, groups // 2) as i:
                    for slot in range(2):
                        arrived(g0, slot, i)
                        natural(slot, src)

            def transpose_norm(prefix):
                for n in range(4):
                    half = enter(f"{prefix}{n}")
                    for k in range(4):
                        for t in range(NT):
                            lo = k * S + t * P
                            last = t_.transpose(scr[:, half, lo:lo + P],
                                                N1[:, t, (4 * n + k) * P:(4 * n + k + 1) * P], ident[:, :])
                    done(f"{prefix}{n}", last)

            pe.wait_ge(consts_ready, 1)
            pe.wait_ge(vec_in, 32)
            half = enter("vectors")
            done("vectors", t_.transpose(scr[:, half, 0:32], vec[:, :], ident[0:32, 0:32]))
            pe.wait_ge(normed, 2)
            transpose_norm("h")
            pe.wait_ge(h_ready, 1)
            transposed_loop(G_HQF, 4, KD, hT)
            natural_loop(G_HIG, 4, hT)

            def level_products(name, a, b, side, pieces):
                half = enter(name)
                for u in range(H):
                    lo_a, lo_b = pieces(side * H + u)
                    last = t_.matmul(scr[:, half, u * P:(u + 1) * P], a[:, lo_a:lo_a + P], b[:, lo_b:lo_b + P],
                                     start=True, stop=True)
                done(name, last)

            def own(u):
                return u * P, u * P

            for n in range(4):
                arrived(G_FQK + n - n % 2, n % 2, 0)
                transposed(n % 2, KD, hT)
                for lv in (2 * n, 2 * n + 1):
                    pe.wait_ge(level_ready, lv + 1)
                    e = level[lv % 2]
                    if lv < MASKED:
                        level_products(f"level{lv}a", e, e, 0, own)
                        level_products(f"level{lv}b", e, e, 1, own)
                    else:
                        level_products("across", e, e, 0, lambda u: (u * S, u * S + P))
            pe.wait_ge(small_in, 32)
            half = enter("forget")
            for k in range(KD):
                last = t_.matmul(scr[0:H, half, 0:S], wff[:, k, :], hT[:, k, :], start=(k == 0), stop=(k == KD - 1))
            done("forget", last)
            level_products("diagonala", k_hg, q_hg, 0, own)
            level_products("diagonalb", k_hg, q_hg, 1, own)
            for n in range(2):
                arrived(G_FV, n, 0)
                natural(n, hT)
                if n == 0:
                    pe.wait_ge(c_ready, 1)
                    half = enter("cumulative")
                    for t in range(NT):
                        last = t_.transpose(scr[:, half, t * H:(t + 1) * H], ff[:, 1, t * P:(t + 1) * P],
                                            ident[0:H, 0:H])
                    done("cumulative", last)
            pe.wait_ge(attn_ready, 1)
            for t in (1, 0):
                half = enter(f"o{t}")
                for h in range(H):
                    to, cols = scr[:, half, h * P:(h + 1) * P], slice(h * P, (h + 1) * P)
                    if t:
                        t_.matmul(to, attn_across[:, h, :], hg_v[:, 0, cols], start=True, stop=False)
                    last = t_.matmul(to, attn[:, 2 * h + t, :], hg_v[:, t, cols], start=(t == 0), stop=True)
                done(f"o{t}", last)

            def logits(pair):
                half = enter(f"qk{pair}")
                for a in range(2):
                    h = 2 * pair + a
                    for t in range(NT):
                        lo, width = a * GW + (0, P)[t], (t + 1) * P
                        to = scr[:, half, lo:lo + width]
                        t_.matmul(to, fqT[:, h, t * P:(t + 1) * P], fkT[:, h, 0:width], start=True, stop=False)
                        last = t_.matmul(to, ident[0:H, h:h + 1].to_broadcast([H, P]), ff[:, 3, 0:width],
                                         start=False, stop=True)
                done(f"qk{pair}", last)

            def transpose_p(pair):
                half = enter(f"pT{pair}")
                for a in range(2):
                    pe.wait_ge(p_ready, 2 * pair + a + 1)
                    for n in range(3):
                        last = t_.transpose(scr[:, half, a * GW + n * P:a * GW + (n + 1) * P],
                                            prob[:, a, n * P:(n + 1) * P], ident[:, :])
                done(f"pT{pair}", last)

            def weighted_v(pair):
                half = enter(f"pv{pair}")
                pe.wait_ge(pT_ready, pair + 1)
                for a in range(2):
                    h = 2 * pair + a
                    cols = slice(h * P, (h + 1) * P)
                    t_.matmul(scr[:, half, a * GW:a * GW + S], fv[:, 0, cols], probT[:, a, 0:S],
                              start=True, stop=False)
                    last = t_.matmul(scr[:, half, a * GW + P:a * GW + S], fv[:, 1, cols], probT[:, a, S:384],
                                     start=False, stop=True)
                done(f"pv{pair}", last)

            pe.wait_ge(ob_ready, 1)
            for t in (1, 0):
                half = enter(f"ob{t}")
                for h in range(H):
                    last = t_.transpose(scr[:, half, h * P:(h + 1) * P], o_hg[:, t, h * P:(h + 1) * P], ident[:, :])
                done(f"ob{t}", last)
            pe.wait_ge(fox_ready, 1)
            for n in range(4):
                logits(n)
                arrived(G_GA + n - n % 2, n % 2, 0)
                transposed(n % 2, KD, hT)
                transpose_p(n)
                weighted_v(n)
            pe.wait_ge(ya_ready, 1)
            transposed_loop(G_AUP, 4, H, yaT)
            pe.wait_ge(obT_ready, 1)
            with pe.Fori(0, 4) as i:
                arrived(G_GB, 0, i)
                transposed(0, KD, hT)
                arrived(G_GB, 1, i)
                transposed(1, H, obT)
            pe.wait_ge(keys_in, 16)
            for n in range(2):
                half = enter(f"keys{n}")
                for u in range(8):
                    last = t_.transpose(scr[:, half, u * P:(u + 1) * P], keys_sb[:, 8 * n + u, :], ident[:, :])
                done(f"keys{n}", last)
            pe.wait_ge(merged_ready, 1)
            natural_loop(G_WO, 4, merged)
            pe.wait_ge(normed, 4)
            transpose_norm("h2")
            pe.wait_ge(h_ready, 2)
            transposed_loop(G_WQ, 4, KD, hT)
            pe.wait_ge(q_ready, 1)
            for n in range(4):
                half = enter(f"score{n}")
                t = n // 2
                for u in range(8):
                    b = 8 * (n % 2) + u
                    last = t_.matmul(scr[:, half, u * P:(u + 1) * P], pqT[:, b, t * P:(t + 1) * P], keysT[:, b, :],
                                     start=True, stop=True)
                done(f"score{n}", last)
            pe.wait_ge(scr_free[0], use_number("score2"))
            pe.wait_ge(scr_free[1], use_number("score3"))
            rounds = NSEL // SLOTS
            banks = [[(acc, scr)[t][:, b // 2, (b % 2) * GW:(b % 2 + 1) * GW] for b in range(4)] for t in range(NT)]
            for t in range(NT):
                for b in range(4):
                    t_.matmul(banks[t][b], ident[:, :], X[:, t, b * GW:(b + 1) * GW], start=True, stop=False)

                def add_rows(i, last_round):
                    for j in range(SLOTS):
                        pe.wait_ge(row_landed[j], ((2 * t + 1) * rounds + 1 + i) * 16)
                        pe.wait_ge(diag_ready[j], t * rounds + 1 + i)
                        for b in range(4):
                            last = t_.matmul(banks[t][b], diag[:, j, :], slots[:, j, b * GW:(b + 1) * GW],
                                             start=False, stop=last_round and j == SLOTS - 1)
                        last.then_inc(row_used[j], 1)

                with pe.Fori(0, rounds - 1) as i:
                    add_rows(i, False)
                add_rows(rounds - 1, True)
                for j in range(SLOTS):
                    pe.wait_ge(row_used[j], 1 + (2 * t + 2) * rounds)
                pe.sem_inc(y_done, 1)


_INS = ["x", "norm1_g", "w_in", "fox_f_bias", "hg_lb_logits", "hg_norm_g", "w_a_up", "w_b_up", "w_o", "norm2_g",
        "peer_wq", "peer_keys", "peer_u", "peer_v", "norm_f_g"]


def kernel(**inputs):
    import numpy as np
    import concourse.bacc as bacc
    from concourse.bass_utils import run_bass_kernel_spmd as run

    nc = bacc.Bacc("TRN2", target_bir_lowering=False, num_devices=1)
    arrays, args = {}, []
    for name in _INS:
        a = np.ascontiguousarray(inputs[name])
        arrays[f"in_{name}"] = a
        args.append(nc.dram_tensor(f"in_{name}", a.shape, mybir.dt.from_np(a.dtype), kind="ExternalInput").ap())
    args.append(nc.dram_tensor("out_0", (1, S, D), mybir.dt.float32, kind="ExternalOutput").ap())
    build(nc, *args)
    return run(nc, [arrays], core_ids=[0]).results[0]["out_0"]
```

```python
import numpy as np
import concourse.bass as bass
from concourse import mybir
from contextlib import ExitStack

P = 128
S = 256
NT = S // P
D = 2048
KD = D // P
H = 8
HW = H * P
GW = 512
FB = GW // P
CH = 64
EPS = 1e-6
TOPK = 16
NSEL = H * TOPK
SCALE = float(P) ** -0.5
COL_FQ, COL_FV, COL_FF = 0, 2 * HW, 3 * HW
COL_HQ = COL_FF + H
COL_HI = COL_HQ + 2 * HW
COL_GA = COL_HI + 2 * HW
COL_GB = COL_GA + D
G_HQF, G_HIG, G_FQK, G_FV, G_GA, G_AUP, G_GB, G_WO, G_WQ, G_END = 0, 4, 8, 12, 14, 18, 22, 30, 34, 38
UK = 4


def units_of(g):
    narrow = G_AUP <= g < G_GB or (G_GB <= g < G_WO and (g - G_GB) % 2)
    return (HW if narrow else D) // P // UK


UNIT0 = [sum(units_of(i) for i in range(g)) for g in range(G_END + 1)]
LEVELS = 8
MASKED = LEVELS - 1
SLOTS = 8
V_SLOTS = (3, 7)
T_SLOTS = tuple(j for j in range(SLOTS) if j not in V_SLOTS)
NEG = -1.0e30
TANH_A, TANH_B = 0.7978845608028654, 0.044715


def scratch_uses():
    uses = [("vectors", 0)] + [(f"h{n}", n % 2) for n in range(4)]
    for lv in range(MASKED):
        uses += [(f"level{lv}a", 0), (f"level{lv}b", 1)]
    uses += [("across", 0), ("forget", 1), ("forgetT", 0), ("diagonala", 0), ("diagonalb", 1),
             ("cumulative", 0), ("o1", 1), ("qk0", 0), ("o0", 1)]
    for pair in range(4):
        uses += [(f"pT{pair}", 1)] + [(f"qk{pair + 1}", 0)] * (pair < 3) + [(f"pv{pair}", 1)]
    uses += [("ob1", 0), ("ob0", 1)]
    uses += [(f"keys{n}", n) for n in range(2)]
    uses += [(f"h2{n}", n % 2) for n in range(4)]
    uses += [(f"score{n}", n % 2) for n in range(4)]
    return uses


USES = scratch_uses()


def half_of(name):
    return dict(USES)[name]


def use_number(name):
    half, count = half_of(name), 0
    for other, h in USES:
        count += h == half
        if other == name:
            return count


def halves(a, size):
    blocks = a.rearrange("p (n u h) -> p n u h", u=2, h=size // 2)
    return blocks[:, :, 0, :], blocks[:, :, 1, :]


class Chain:

    def __init__(self, engine, sem):
        self.engine, self.sem, self.n, self.turn = engine, sem, 0, 0

    def link(self, instruction):
        self.n += 1
        instruction.then_inc(self.sem, 1)
        self.engine.wait_ge(self.sem, self.n + self.turn)

    def enter(self, i, links):
        self.turn, self.start, self.links = i * links, self.n, links

    def leave(self, turns):
        assert self.n - self.start == self.links, (self.n - self.start, self.links)
        self.n, self.turn = self.start + self.links * turns, 0


def build(nc, x, norm1_g, w_in, fox_f_bias, hg_lb_logits, hg_norm_g, w_a_up, w_b_up, w_o, norm2_g,
          peer_wq, peer_keys, peer_u, peer_v, norm_f_g, out):
    fp32, u32, f32r = mybir.dt.float32, mybir.dt.uint32, mybir.dt.float32r
    ALU, ACT, AX = mybir.AluOpType, mybir.ActivationFunctionType, mybir.AxisListType
    ds = bass.ds

    x_d = x.rearrange("b (t p) d -> p (b t) d", p=P)
    out_d = out.rearrange("b (t p) d -> p (b t) d", p=P)
    w_in_d = w_in.rearrange("l (k p) n -> p (l k) n", p=P)
    w_a_d = w_a_up.rearrange("l (k p) n -> p (l k) n", p=P)
    w_b_d = w_b_up.rearrange("l (k p) n -> p (l k) n", p=P)
    w_o_d = w_o.rearrange("l (k p) n -> p (l k) n", p=P)
    wq_d = peer_wq.rearrange("l (k p) n -> p (l k) n", p=P)
    keys_d = peer_keys.rearrange("l h c n d -> n (l h c) d")
    u_rows = peer_u.rearrange("l e d -> (l e) d")
    v_rows = peer_v.rearrange("l e d -> (l e) d")

    ctx = ExitStack()
    with ctx:
        def sb(name, shape, dt=fp32):
            return ctx.enter_context(nc.sbuf_tensor(name, shape, dt))

        def sem(name):
            return ctx.enter_context(nc.semaphore(name))

        ident = sb("ident", [P, P])
        fox_mask = sb("fox_mask", [P, S])
        vec = sb("vec", [16, P])
        vecT = sb("vecT", [P, 16])
        wff = sb("wff", [P, KD, H])
        wff_hi, wff_lo = sb("wff_hi", [P, KD, H], f32r), sb("wff_lo", [P, KD, H], f32r)
        ff_bias = sb("ff_bias", [H, 1])
        ff_tok = sb("ff_tok", [P, NT, H])
        c_tok = sb("c_tok", [P, NT, H])
        lb = sb("lb", [P, 4, H])
        stat = sb("stat", [P, 6, 16])
        fstat = sb("fstat", [P, 3, 16])
        iota16 = sb("iota16", [P, TOPK])
        stage = sb("stage", [P, 2, SLOTS], u32)
        gsum = sb("gsum", [P, 2, H])

        KB = 256
        arena_at = (nc.sbuf_base + 31) // 32 * 32
        sb("arena", [P, 202 * KB])

        def at(name, kib, shape, dt=fp32):
            return nc.alloc_sbuf_tensor_at(name, [P, *shape], dt, offset=arena_at + kib * 1024)

        X = at("X", 0, [NT, D])
        hT_hi = at("hT_hi", 16, [KD, S], f32r)
        hT_lo = at("hT_lo", 32, [KD, S], f32r)
        raw = at("raw", 48, [2, UK, GW])
        w_hi = at("w_hi", 64, [2, UK, GW], f32r)
        w_lo = at("w_lo", 80, [2, UK, GW], f32r)
        slots = at("slots", 32, [SLOTS, D])
        Z1 = at("Z1", 96, [16 * S])
        N1 = at("N1", 112, [NT, D])
        ob_hi = at("ob_hi", 112, [H, S], f32r)
        ob_lo = at("ob_lo", 120, [H, S], f32r)
        Z2 = at("Z2", 128, [16 * S])
        ya_hi = at("ya_hi", 128, [H, S], f32r)
        ya_lo = at("ya_lo", 136, [H, S], f32r)
        V1 = at("V1", 144, [NT * HW])
        T1 = at("T1", 152, [16 * S])
        T2 = at("T2", 168, [16 * S])
        A2 = at("A2", 184, [3 * HW])
        masks = at("masks", 196, [LEVELS, P])
        diag = at("diag", 196, [SLOTS, P])
        ff_room = at("ff_room", 200, [2 * KB])

        room = [0]

        def carve(name, *shape, dt=fp32):
            lo, room[0] = room[0], room[0] + int(np.prod(shape)) * 4
            assert room[0] <= 16 * 1024
            return nc.alloc_sbuf_tensor_at(name, [P, *shape], dt, offset=arena_at + 16 * 1024 + lo)

        gate, hid = carve("gate", 2, NSEL), carve("hid", 3, NSEL)
        spot = [0]

        def spare(name, *shape, dt=fp32):
            lo, spot[0] = spot[0], spot[0] + int(np.prod(shape)) * 4
            assert spot[0] <= 12 * 1024
            return nc.alloc_sbuf_tensor_at(name, [P, *shape], dt, offset=arena_at + 184 * 1024 + lo)

        topv, topf, topi = spare("topv", 16, TOPK), spare("topf", 16, TOPK), spare("topi", 16, TOPK, dt=u32)
        best, expert = spare("best", NT, NSEL), spare("expert", NT, NSEL, dt=u32)
        bpos, bposf, rest = spare("bpos", 3, NSEL, dt=u32), spare("bposf", 4, NSEL), spare("rest", 2 * P)

        q_hg, k_hg = Z1[:, 0:8 * S], Z1[:, 8 * S:16 * S]
        o_hg = Z1[:, 0:8 * S].rearrange("p (t f) -> p t f", t=NT)
        scores = Z1[:, :].rearrange("p (t u n) -> p t u n", t=NT, n=P)
        hg_v, hg_gate = N1[:, :, 0:HW], N1[:, :, HW:D]
        fqT = Z2[:, 0:8 * S].rearrange("p (h s) -> p h s", h=H)
        fkT = Z2[:, 8 * S:16 * S].rearrange("p (h s) -> p h s", h=H)
        pqT = Z2[:, :].rearrange("p (u s) -> p u s", s=S)
        fv = V1[:, :].rearrange("p (t f) -> p t f", t=NT)
        keysT = V1[:, :].rearrange("p (u n) -> p u n", n=P)
        b_chunk, b_tile = T1[:, 0:8 * S], T1[:, 8 * S:16 * S]
        merged = T1[:, :].rearrange("p (k s) -> p k s", s=S)
        gain1 = T1[:, 0:D]
        level = [T2[:, 0:8 * S], T2[:, 8 * S:16 * S]]
        hg_gain = T2[:, 0:HW]
        prob = T2[:, 2 * HW:2 * HW + 2 * 384].rearrange("p (a s) -> p a s", a=2)
        probT = T2[:, 3 * HW:3 * HW + 2 * 384].rearrange("p (a s) -> p a s", a=2)
        gain2, gain_f = T1[:, 0:D], T1[:, D:2 * D]
        cand, hot, y_dve = T2[:, 0:2 * S], T2[:, 2 * S:4 * S], T2[:, D:2 * D]
        attn = A2[:, 0:2 * HW].rearrange("p (u s) -> p u s", s=P)
        attn_across = A2[:, 2 * HW:3 * HW].rearrange("p (h s) -> p h s", s=P)
        yaT = A2[:, 0:2 * HW].rearrange("p (h s) -> p h s", h=H)
        keys_sb = A2[:, 0:2 * HW].rearrange("p (u d) -> p u d", d=P)
        ff = T2[0:H, 0:4 * S].rearrange("p (n s) -> p n s", s=S)
        neg_c = ff_room[0:H, 0:S]

        acc = ctx.enter_context(nc.psum_tensor("acc", [P, 2, 2 * GW], fp32))
        scr = ctx.enter_context(nc.psum_tensor("scr", [P, 2, 2 * GW], fp32))

        x_in, gain1_in, vec_in, small_in = sem("x_in"), sem("gain1_in"), sem("vec_in"), sem("small_in")
        raw_landed = [sem("raw_landed0"), sem("raw_landed1")]
        hi_ready, lo_ready = sem("hi_ready"), sem("lo_ready")
        unit_done, group_done = sem("unit_done"), sem("group_done")
        acc_free = [sem("acc_free0"), sem("acc_free1")]
        scr_ready = [sem("scr_ready0"), sem("scr_ready1")]
        scr_free = [sem("scr_free0"), sem("scr_free1")]
        consts_ready, pool_step, dve_step = sem("consts_ready"), sem("pool_step"), sem("dve_step")
        mean_ready, root_ready, normed = sem("mean_ready"), sem("root_ready"), sem("normed")
        h_hi_ready, h_ready = sem("h_hi_ready"), sem("h_ready")
        lb_diff, lb_exp = sem("lb_diff"), sem("lb_exp")
        hqf_ready, k_sig, q_silu = sem("hqf_ready"), sem("k_sig"), sem("q_silu")
        f_ready, logf_ready, k_ready = sem("f_ready"), sem("logf_ready"), sem("k_ready")
        b_ready, reset_ready = sem("b_ready"), sem("reset_ready")
        hgate_in, hgate_ready = sem("hgate_in"), sem("hgate_ready")
        diff_ready, decay_ready, level_ready = sem("diff_ready"), sem("decay_ready"), sem("level_ready")
        wff_hi_ready, wff_ready = sem("wff_hi_ready"), sem("wff_ready")
        ff_tok_ready, ff_in, ff_abs, ff_exp = sem("ff_tok_ready"), sem("ff_in"), sem("ff_abs"), sem("ff_exp")
        ff_log, c_ready, attn_ready, q_scaled = sem("ff_log"), sem("c_ready"), sem("attn_ready"), sem("q_scaled")
        fv_ready, gain_free, hg_gain_in = sem("fv_ready"), sem("gain_free"), sem("hg_gain_in")
        o_ready, ob_ready, ob_hi_ready, ob_split = sem("o_ready"), sem("ob_ready"), sem("ob_hi_ready"), sem("ob_split")
        logit_ready, exp_ready, p_ready = sem("logit_ready"), sem("exp_ready"), sem("p_ready")
        pT_ready, ya_in, ya_hi_ready, ya_split = sem("pT_ready"), sem("ya_in"), sem("ya_hi_ready"), sem("ya_split")
        ga_ready, gb_ready, gb_used = sem("ga_ready"), sem("gb_ready"), sem("gb_used")
        merged_ready, merged_hi, merged_split = sem("merged_ready"), sem("merged_hi"), sem("merged_split")
        keys_in, gains_in, keys_copied, q_copied = sem("keys_in"), sem("gains_in"), sem("keys_copied"), sem("q_copied")
        shifted, gate_exp, expert_ready = sem("shifted"), sem("gate_exp"), sem("expert_ready")
        granted, granted_w = sem("granted"), sem("granted_w")
        row_landed = [sem(f"row_landed{j}") for j in range(SLOTS)]
        row_used = [sem(f"row_used{j}") for j in range(SLOTS)]
        tanh_in, tanh_ready, weight_ready = sem("tanh_in"), sem("tanh_ready"), sem("weight_ready")
        diag_ready = [sem(f"diag_ready{j}") for j in range(SLOTS)]
        diag_step, y_done = sem("diag_step"), sem("y_done")
        y_summed, y_squared, y_ready, out_done = sem("y_summed"), sem("y_squared"), sem("y_ready"), sem("out_done")

        block = ctx.enter_context(nc.Block())

        @block.sync
        def _(sp):
            for t in range(NT):
                sp.dma_start(X[:, t, :], x_d[:, t, :]).then_inc(x_in, 16)
            sp.dma_start(gain1, norm1_g.partition_broadcast(P).rearrange("q l f -> q (l f)")).then_inc(gain1_in, 16)
            sp.dma_start(vec[:, :], hg_lb_logits.rearrange("l (h p) -> (l h) p", p=P)).then_inc(vec_in, 16)

            def load(src, cols, m, u, wait=True):
                if wait:
                    sp.wait_ge(lo_ready, u - 1)
                    sp.sem_inc(granted_w, 1)
                sp.dma_start(raw[:, m % 2, :, :], src[:, m * UK:(m + 1) * UK, cols]).then_inc(raw_landed[m % 2], 16)

            def load_loop(g0, groups, src, col0):
                n = units_of(g0)
                with sp.Fori(0, groups) as i:
                    for m in range(n):
                        load(src, ds(col0 + i * GW, GW), m, UNIT0[g0] + m + i * n)

            for m in range(4):
                load(w_in_d, slice(COL_HQ, COL_HQ + GW), m, m, wait=m >= 2)
            sp.dma_start(wff[:, :, :], w_in_d[:, :, COL_FF:COL_FF + H]).then_inc(small_in, 16)
            sp.dma_start(ff_bias[:, :], fox_f_bias.rearrange("l h -> h l")).then_inc(small_in, 16)
            load_loop(G_HQF + 1, 3, w_in_d, COL_HQ + GW)
            load_loop(G_HIG, 4, w_in_d, COL_HI)
            load_loop(G_FQK, 4, w_in_d, COL_FQ)
            load_loop(G_FV, 2, w_in_d, COL_FV)
            load_loop(G_GA, 4, w_in_d, COL_GA)
            load_loop(G_AUP, 4, w_a_d, 0)
            with sp.Fori(0, 4) as i:
                for m in range(units_of(G_GB)):
                    load(w_in_d, ds(COL_GB + i * GW, GW), m, UNIT0[G_GB] + m + 6 * i)
                for m in range(units_of(G_GB + 1)):
                    load(w_b_d, ds(i * GW, GW), m, UNIT0[G_GB + 1] + m + 6 * i)
            load_loop(G_WO, 4, w_o_d, 0)
            load_loop(G_WQ, 4, wq_d, 0)
            for n in range(2 * NT):
                t, cols = n // 2, slice(n % 2 * D // 2, (n % 2 + 1) * D // 2)
                sp.wait_ge(y_ready, n + 1)
                sp.dma_start(out_d[:, t, cols], X[:, t, cols]).then_inc(out_done, 16)
            sp.wait_ge(out_done, 16 * 2 * NT)

        @block.gpsimd
        def _(pool):
            g = nc.gpsimd
            steps = Chain(pool, pool_step)
            g.memset(ident[:, :], 0.0)
            g.memset(masks[:, :, :], 0.0)
            steps.link(g.memset(fox_mask[:, :], 0.0))
            g.affine_select(out=ident[:, :], in_=ident[:, :], compare_op=ALU.not_equal, fill=1.0, base=0,
                            pattern=[[-1, P]], channel_multiplier=1).then_inc(consts_ready, 1)
            steps.link(g.affine_select(out=fox_mask[:, P:S], in_=fox_mask[:, P:S], compare_op=ALU.is_ge,
                                       fill=NEG, base=0, pattern=[[-1, P]], channel_multiplier=1))
            steps.link(g.iota(iota16[:, :], [[1, TOPK]], base=0, channel_multiplier=0,
                              allow_small_or_imprecise_dtypes=True))
            uppers = []
            for lv in range(MASKED):
                half = 1 << lv
                uppers.append(masks[:, lv, :].rearrange("p (n u h) -> p n u h", u=2, h=half)[:, :, 1, :])
                last = g.memset(uppers[lv], 1.0)
            steps.link(last)
            for lv in range(MASKED):
                half, n = 1 << lv, P >> (lv + 1)
                last = g.affine_select(out=uppers[lv], in_=uppers[lv], compare_op=ALU.is_ge, fill=0.0, base=0,
                                       pattern=[[-2 * half, n], [0, half]], channel_multiplier=1)
            steps.link(last)
            for lv in range(MASKED):
                half, n = 1 << lv, P >> (lv + 1)
                g.affine_select(out=uppers[lv], in_=uppers[lv], compare_op=ALU.is_ge, fill=0.0, base=half - 1,
                                pattern=[[2 * half, n], [0, half]], channel_multiplier=-1)
            g.affine_select(out=masks[:, MASKED, :], in_=masks[:, MASKED, :], compare_op=ALU.not_equal, fill=1.0,
                            base=0, pattern=[[-1, P]], channel_multiplier=1).then_inc(consts_ready, 1)
            pool.wait_ge(b_ready, 1)
            for lv in range(LEVELS):
                if lv >= 2:
                    pool.wait_ge(scr_ready[1], use_number(f"level{lv - 2}b"))
                size = 2 << lv
                e_lo, e_up = halves(level[lv % 2], size)
                b_lo, b_up = halves(b_tile if lv == LEVELS - 1 else b_chunk, size)
                ref = b_lo[:, :, size // 2 - 1:size // 2].to_broadcast([P, 8 * S // size, size // 2])
                g.tensor_tensor(e_lo, ref, b_lo, ALU.subtract)
                if lv < LEVELS - 2:
                    last = g.tensor_tensor(e_up, b_up, ref, ALU.subtract)
                else:
                    last = g.tensor_copy(e_up, b_up)
                last.then_inc(diff_ready, 1)
            pool.wait_ge(gain_free, 1)
            pool.dma_start(hg_gain, hg_norm_g.partition_broadcast(P).rearrange("q l f -> q (l f)")
                           ).then_inc(hg_gain_in, 16)
            pool.wait_ge(ya_split, 2)
            pool.dma_start(keys_sb, keys_d).then_inc(keys_in, 16)
            pool.wait_ge(merged_split, 4)
            pool.dma_start(gain2, norm2_g.partition_broadcast(P).rearrange("q l f -> q (l f)")).then_inc(gains_in, 16)
            pool.dma_start(gain_f, norm_f_g.rearrange("(l f) -> l f", l=1).partition_broadcast(P)
                           .rearrange("q l f -> q (l f)")).then_inc(gains_in, 16)
            pool.wait_ge(group_done, G_END)
            rounds = NSEL // SLOTS
            for t in range(NT):
                for table in range(2):
                    for pair in range(4):
                        if table == 0:
                            pool.wait_ge(expert_ready, 4 * t + pair + 1)
                        first_round = (2 * t + table) * rounds + pair * rounds // 4
                        rows = (u_rows, v_rows)[table]
                        with pool.Fori(0, rounds // 8) as i:
                            steps.enter(i, 2)
                            for side in range(2):
                                steps.link(g.tensor_copy(stage[:, side, :], expert[:, t, ds(
                                    pair * NSEL // 4 + (2 * i + side) * SLOTS, SLOTS)]))
                                for j in range(SLOTS):
                                    pool.wait_ge(row_used[j], 1 + first_round + 2 * i + side)
                                    pool.sem_inc(granted, 1)
                                    pool.indirect_dma_start(
                                        slots[:, j, :], None, rows,
                                        bass.IndirectOffsetOnAxis(ap=stage[:, side, j:j + 1], axis=0)
                                    ).then_inc(row_landed[j], 16)
                            steps.leave(rounds // 8)

        @block.scalar
        def _(act):
            a = nc.scalar

            def hi(g, m, i=0, per=0):
                u = UNIT0[g] + m
                act.wait_ge(raw_landed[m % 2], (u // 2 + 1) * 16 + i * per * 8)
                if u >= 2 or per:
                    act.wait_ge(unit_done, u - 1 + i * per)
                a.activation(w_hi[:, m % 2, :, :], raw[:, m % 2, :, :], ACT.Copy).then_inc(hi_ready, 1)

            def group(g):
                for m in range(units_of(g)):
                    hi(g, m)

            act.wait_ge(mean_ready, 1)
            a.activation(stat[:, 2, 0:NT], stat[:, 1, 0:NT], ACT.Sqrt).then_inc(root_ready, 1)
            act.wait_ge(lb_diff, 1)
            a.activation(lb[:, 0:2, :], lb[:, 2:4, :], ACT.Exp).then_inc(lb_exp, 1)
            hi(0, 0)
            hi(0, 1)

            def split_hi(name, to, ready):
                half = half_of(name)
                act.wait_ge(scr_ready[half], use_number(name))
                a.activation(to, scr[:, half, :].rearrange("p (k s) -> p k s", k=to.shape[1]),
                             ACT.Copy).then_inc(ready, 1)

            for n in range(4):
                split_hi(f"h{n}", hT_hi[:, 4 * n:4 * n + 4, :], h_hi_ready)
            act.wait_ge(small_in, 32)
            a.activation(wff_hi[:, :, :], wff[:, :, :], ACT.Copy).then_inc(wff_hi_ready, 1)
            hi(0, 2)
            hi(0, 3)
            for g in range(1, G_HIG):
                group(g)
            hi(G_HIG, 0)
            hi(G_HIG, 1)
            act.wait_ge(hqf_ready, 1)
            a.activation(k_hg, k_hg, ACT.Sigmoid).then_inc(k_sig, 1)
            hi(G_HIG, 2)
            a.activation(q_hg, q_hg, ACT.Silu).then_inc(q_silu, 1)
            hi(G_HIG, 3)
            hi(G_HIG + 1, 0)
            hi(G_HIG + 1, 1)
            act.wait_ge(f_ready, 1)
            a.activation(b_tile, level[0], ACT.Ln).then_inc(logf_ready, 1)
            hi(G_HIG + 1, 2)
            hi(G_HIG + 1, 3)
            group(G_HIG + 2)
            group(G_HIG + 3)

            def decay(lv):
                act.wait_ge(diff_ready, lv + 1)
                a.activation(level[lv % 2], level[lv % 2], ACT.Exp).then_inc(decay_ready, 1)

            decay(0)
            for n in range(4):
                g = G_FQK + n
                hi(g, 0)
                hi(g, 1)
                if n == 0:
                    act.wait_ge(hgate_in, 1)
                    a.activation(hg_gate, hg_gate, ACT.Silu).then_inc(hgate_ready, 1)
                decay(2 * n + 1)
                hi(g, 2)
                hi(g, 3)
                if n < 3:
                    decay(2 * n + 2)
            hi(G_FV, 0)
            hi(G_FV, 1)
            hi(G_FV, 2)
            act.wait_ge(ff_in, 1)
            a.activation(ff[:, 1, :], ff[:, 0, :], ACT.Abs).then_inc(ff_abs, 1)
            act.wait_ge(ff_abs, 1)
            a.activation(ff[:, 2, :], ff[:, 1, :], ACT.Exp, scale=-1.0).then_inc(ff_exp, 1)
            act.wait_ge(ff_exp, 1)
            a.activation(ff[:, 1, :], ff[:, 2, :], ACT.Ln, bias=1.0).then_inc(ff_log, 1)
            hi(G_FV, 3)
            group(G_FV + 1)

            def exps(pair):
                for n in range(4 * pair, 4 * pair + 4):
                    h, t = n // NT, n % NT
                    lo = (0, P)[t]
                    act.wait_ge(logit_ready, n + 1)
                    p = prob[:, h % 2, lo:lo + (t + 1) * P]
                    a.activation(p, p, ACT.Exp, bias=fstat[:, 0, n:n + 1],
                                 accum_out=fstat[:, 1, n:n + 1]).then_inc(exp_ready, 1)

            def gate_a(n):
                act.wait_ge(group_done, G_GA + n + 1)
                a.activation(T1[:, n * 2 * GW:(n + 1) * 2 * GW], acc[:, n % 2, :], ACT.Sigmoid).then_inc(ga_ready, 1)
                act.wait_ge(ga_ready, n + 1)
                act.sem_inc(acc_free[n % 2], 1)

            for n in range(4):
                hi(G_GA + n, 0)
                exps(n)
                hi(G_GA + n, 1)
                if n:
                    gate_a(n - 1)
                hi(G_GA + n, 2)
                hi(G_GA + n, 3)
            hi(G_AUP, 0)
            hi(G_AUP, 1)
            for n in range(2):
                act.wait_ge(ya_in, n + 1)
                a.activation(ya_hi[:, 4 * n:4 * n + 4, :], yaT[:, 4 * n:4 * n + 4, :], ACT.Copy).then_inc(ya_hi_ready, 1)
            gate_a(3)
            for n in range(1, 4):
                group(G_AUP + n)
                if n == 2:
                    act.wait_ge(mean_ready, 2)
                    a.activation(stat[:, 2, :], stat[:, 1, :], ACT.Sqrt).then_inc(root_ready, 1)
            hi(G_GB, 0)
            hi(G_GB, 1)
            for n, t in enumerate((1, 0)):
                split_hi(f"ob{t}", ob_hi[:, :, t * P:(t + 1) * P], ob_hi_ready)
            hi(G_GB, 2)
            hi(G_GB, 3)
            for n in range(4):
                if n:
                    group(G_GB + 2 * n)
                group(G_GB + 2 * n + 1)
                act.wait_ge(group_done, G_GB + 2 * n + 1)
                act.wait_ge(gb_used, 1 + n)
                a.activation(T2[:, 0:2 * GW], acc[:, 0, :], ACT.Sigmoid).then_inc(gb_ready, 1)
                act.wait_ge(gb_ready, n + 1)
                act.sem_inc(acc_free[0], 1)
            hi(G_WO, 0)
            hi(G_WO, 1)
            for n in range(4):
                act.wait_ge(merged_ready, 1)
                a.activation(hT_hi[:, 4 * n:4 * n + 4, :], merged[:, 4 * n:4 * n + 4, :], ACT.Copy
                             ).then_inc(merged_hi, 1)
            hi(G_WO, 2)
            hi(G_WO, 3)
            with act.Fori(0, 3) as i:
                for m in range(4):
                    hi(G_WO + 1, m, i, 4)
            hi(G_WQ, 0)
            hi(G_WQ, 1)
            act.wait_ge(mean_ready, 3)
            a.activation(stat[:, 2, 0:NT], stat[:, 1, 0:NT], ACT.Sqrt).then_inc(root_ready, 1)
            for n in range(4):
                split_hi(f"h2{n}", hT_hi[:, 4 * n:4 * n + 4, :], h_hi_ready)
            hi(G_WQ, 2)
            hi(G_WQ, 3)
            with act.Fori(0, 3) as i:
                for m in range(4):
                    hi(G_WQ + 1, m, i, 4)
            for t in range(NT):
                if t:
                    act.wait_ge(mean_ready, 3 + t)
                    a.activation(stat[:, 2, 0:1], stat[:, 1, 0:1], ACT.Sqrt).then_inc(root_ready, 1)
                act.wait_ge(shifted, t + 1)
                a.activation(gate[:, 0, :], gate[:, 0, :], ACT.Exp).then_inc(gate_exp, 1)
                act.wait_ge(tanh_in, t + 1)
                a.activation(hid[:, 1, :], hid[:, 1, :], ACT.Tanh).then_inc(tanh_ready, 1)
                act.wait_ge(weight_ready, t + 1)
                rounds = NSEL // SLOTS
                with act.Fori(0, rounds) as i:
                    for j in T_SLOTS:
                        act.wait_ge(row_used[j], 1 + (2 * t + 1) * rounds + i)
                        act.sem_inc(diag_step, 1)
                        a.activation(diag[:, j, :], ident[:, :], ACT.Copy,
                                     scale=gate[:, 1, ds(i * SLOTS + j, 1)]).then_inc(diag_ready[j], 1)
            act.wait_ge(y_summed, 1)
            a.activation(N1[:, 0, 0:D // 2], X[:, NT - 1, 0:D // 2], ACT.Square,
                         accum_out=stat[:, 5, 0:1]).then_inc(y_squared, 1)
            act.wait_ge(mean_ready, 5)
            a.activation(stat[:, 2, 0:1], stat[:, 1, 0:1], ACT.Sqrt).then_inc(root_ready, 1)

        @block.vector
        def _(dve):
            v = nc.vector
            steps = Chain(dve, dve_step)
            link = steps.link
            for free in (*acc_free, *row_used, gb_used):
                dve.sem_inc(free, 1)

            def lo(g, m):
                dve.wait_ge(hi_ready, UNIT0[g] + m + 1)
                v.tensor_tensor(w_lo[:, m % 2, :, :], raw[:, m % 2, :, :], w_hi[:, m % 2, :, :].bitcast(fp32),
                                ALU.subtract).then_inc(lo_ready, 1)

            def scratch(name):
                dve.wait_ge(scr_ready[half_of(name)], use_number(name))
                return half_of(name)

            def inverse_root(n, width, count):
                m, root, r, s = (stat[:, k, 0:n] for k in (1, 2, 3, 4))
                v.tensor_scalar(m, stat[:, 0, 0:n], 1.0 / width, EPS, ALU.mult, ALU.add).then_inc(mean_ready, 1)
                dve.wait_ge(root_ready, count)
                link(v.reciprocal(r, root))
                link(v.tensor_tensor(s, r, r, ALU.mult))
                link(v.tensor_tensor(s, s, m, ALU.mult))
                link(v.tensor_scalar(s, s, -0.5, 1.5, ALU.mult, ALU.add))
                link(v.tensor_tensor(r, r, s, ALU.mult))

            def norm(gain, count):
                for t in range(NT):
                    link(v.scalar_tensor_tensor(out=N1[:, t, :], in0=X[:, t, :], scalar=1.0, in1=X[:, t, :],
                                                op0=ALU.mult, op1=ALU.mult, accum_out=stat[:, 0, t:t + 1]))
                inverse_root(NT, D, count)
                dve.wait_ge(*((gain1_in, 16) if count == 1 else (gains_in, 32)))
                for t in range(NT):
                    v.scalar_tensor_tensor(out=N1[:, t, :], in0=X[:, t, :], scalar=stat[:, 3, t:t + 1], in1=gain,
                                           op0=ALU.mult, op1=ALU.mult).then_inc(normed, 1)

            def split_h(prefix, before):
                for n in range(4):
                    half = scratch(f"{prefix}{n}")
                    dve.wait_ge(h_hi_ready, before + n + 1)
                    k = slice(4 * n, 4 * n + 4)
                    v.tensor_tensor(hT_lo[:, k, :], scr[:, half, :].rearrange("p (k s) -> p k s", k=4),
                                    hT_hi[:, k, :].bitcast(fp32), ALU.subtract).then_inc(h_ready, 1)
                    dve.wait_ge(h_ready, before + n + 1)
                    dve.sem_inc(scr_free[half], 1)

            dve.wait_ge(x_in, 32)
            norm(gain1, 1)
            half = scratch("vectors")
            link(v.tensor_copy(vecT[:, :], scr[:, half, 0:16]))
            dve.sem_inc(scr_free[half], 1)
            l0, l1 = vecT[:, 0:8], vecT[:, 8:16]
            link(v.tensor_tensor(lb[:, 0, :], l0, l1, ALU.max))
            v.tensor_tensor(lb[:, 2, :], l0, lb[:, 0, :], ALU.subtract)
            v.tensor_tensor(lb[:, 3, :], l1, lb[:, 0, :], ALU.subtract).then_inc(lb_diff, 1)
            dve.wait_ge(lb_exp, 1)
            link(v.tensor_tensor(lb[:, 2, :], lb[:, 0, :], lb[:, 1, :], ALU.add))
            link(v.reciprocal(lb[:, 2, :], lb[:, 2, :]))
            link(v.tensor_tensor(lb[:, 0, :], lb[:, 0, :], lb[:, 2, :], ALU.mult))
            link(v.tensor_scalar(lb[:, 1, :], lb[:, 0, :], -1.0, 1.0, ALU.mult, ALU.add))
            lo(0, 0)
            lo(0, 1)
            split_h("h", 0)

            def copy_group(g, to):
                dve.wait_ge(group_done, g + 1)
                src = acc[:, g % 2, :]
                if len(to.shape) == 3:
                    src = src.rearrange("p (t n) -> p t n", t=NT)
                v.tensor_copy(to, src).then_inc(acc_free[g % 2], 1)

            def copied(g):
                dve.wait_ge(acc_free[g % 2], g // 2 + 2)
                dve.wait_ge(acc_free[1 - g % 2], (g + 1) // 2 + 1)

            def hqf(n):
                copy_group(G_HQF + n, Z1[:, n * 2 * GW:(n + 1) * 2 * GW])

            def hig(n):
                copy_group(G_HIG + n, N1[:, :, n * GW:(n + 1) * GW])

            def fqk(n):
                copy_group(G_FQK + n, Z2[:, n * 2 * GW:(n + 1) * 2 * GW])

            lo(0, 2)
            lo(0, 3)
            dve.wait_ge(wff_hi_ready, 1)
            v.tensor_tensor(wff_lo[:, :, :], wff[:, :, :], wff_hi[:, :, :].bitcast(fp32),
                            ALU.subtract).then_inc(wff_ready, 1)
            for n in range(1, 4):
                for m in range(4):
                    lo(G_HQF + n, m)
                    if m == 1:
                        hqf(n - 1)

            g = G_HIG
            reset = level[1]
            lo(g, 0)
            lo(g, 1)
            hqf(3)
            copied(G_HQF + 3)
            dve.sem_inc(hqf_ready, 1)
            link(v.memset(reset, 1.0))
            v.memset(reset.rearrange("p (c s) -> p c s", s=CH)[:, :, 0:1], 0.0).then_inc(reset_ready, 1)
            lo(g, 2)
            lo(g, 3)
            dve.wait_ge(k_sig, 1)
            f = level[0]
            for h in range(H):
                last = v.tensor_scalar(f[:, h * S:(h + 1) * S], k_hg[:, h * S:(h + 1) * S], lb[:, 1, h:h + 1],
                                       lb[:, 0, h:h + 1], ALU.mult, ALU.add)
            last.then_inc(f_ready, 1)
            lo(g + 1, 0)
            lo(g + 1, 1)
            hig(0)
            dve.wait_ge(f_ready, 1)
            v.tensor_scalar(k_hg, f, -1.0, 1.0, ALU.mult, ALU.add).then_inc(k_ready, 1)
            lo(g + 1, 2)
            dve.wait_ge(logf_ready, 1)
            dve.wait_ge(reset_ready, 1)
            link(v.tensor_tensor_scan(b_chunk, reset, b_tile, 0.0, ALU.mult, ALU.add))
            lo(g + 1, 3)
            bc = b_chunk.rearrange("p (u c s) -> p u c s", c=2, s=CH)
            bt = b_tile.rearrange("p (u c s) -> p u c s", c=2, s=CH)
            v.tensor_copy(bt[:, :, 0, :], bc[:, :, 0, :])
            v.tensor_tensor(bt[:, :, 1, :], bc[:, :, 1, :], bc[:, :, 0, CH - 1:CH].to_broadcast([P, 2 * H, CH]),
                            ALU.add).then_inc(b_ready, 1)
            lo(g + 2, 0)
            lo(g + 2, 1)
            hig(1)
            link(v.memset(A2[:, :], 0.0))
            lo(g + 2, 2)
            lo(g + 2, 3)
            dve.wait_ge(k_ready, 1)
            dve.wait_ge(q_silu, 1)

            def times(lv):
                dve.wait_ge(decay_ready, lv + 1)
                size = 2 << lv
                (e_lo, e_up), (k_lo, _), (_, q_up) = (halves(b, size) for b in (level[lv % 2], k_hg, q_hg))
                v.tensor_tensor(e_lo, e_lo, k_lo, ALU.mult)
                v.tensor_tensor(e_up, e_up, q_up, ALU.mult).then_inc(level_ready, 1)

            def place(lv):
                if lv == LEVELS - 1:
                    half = scratch("across")
                    v.tensor_copy(attn_across, scr[:, half, :].rearrange("p (h s) -> p h s", s=P)
                                  ).then_inc(scr_free[half], 1)
                    return
                k, stem = (MASKED, "diagonal") if lv == LEVELS else (lv, f"level{lv}")
                if lv:
                    dve.wait_ge(scr_free[1], use_number(f"level{min(lv, MASKED) - 1}b"))
                for side in range(2):
                    half = scratch(f"{stem}{'ab'[side]}")
                    to = attn[:, side * H:(side + 1) * H, :]
                    mask = masks[:, k:k + 1, :].to_broadcast([P, H, P]).bitcast(u32)
                    v.copy_predicated(to, mask, scr[:, half, :].rearrange("p (u s) -> p u s", s=P)
                                      ).then_inc(scr_free[half], 1)

            lo(g + 3, 0)
            lo(g + 3, 1)
            hig(2)
            lo(g + 3, 2)
            lo(g + 3, 3)
            dve.wait_ge(consts_ready, 2)
            for n in range(4):
                g = G_FQK + n
                lo(g, 0)
                if n:
                    place(2 * n - 1)
                lo(g, 1)
                if n == 0:
                    hig(3)
                    copied(G_HIG + 3)
                    dve.sem_inc(hgate_in, 1)
                else:
                    fqk(n - 1)
                times(2 * n)
                lo(g, 2)
                lo(g, 3)
                place(2 * n)
                times(2 * n + 1)

            lo(G_FV, 0)
            place(LEVELS - 1)
            lo(G_FV, 1)
            half = scratch("forget")
            v.tensor_copy(ff_tok[:, :, :], scr[:, half, 0:NT * H].rearrange("p (t h) -> p t h", t=NT)
                          ).then_inc(ff_tok_ready, 1)
            dve.wait_ge(ff_tok_ready, 1)
            dve.sem_inc(scr_free[half], 1)
            fqk(3)
            copied(G_FQK + 3)
            v.tensor_scalar(Z2[:, 0:8 * S], Z2[:, 0:8 * S], SCALE, None, ALU.mult).then_inc(q_scaled, 1)
            half = scratch("forgetT")
            v.tensor_scalar(ff[:, 0, :], scr[0:H, half, 0:S], ff_bias[:, 0:1], None, ALU.add).then_inc(ff_in, 1)
            dve.wait_ge(ff_in, 1)
            dve.sem_inc(scr_free[half], 1)
            lo(G_FV, 2)
            lo(G_FV, 3)
            dve.wait_ge(ff_log, 1)
            link(v.scalar_tensor_tensor(out=ff[:, 2, :], in0=ff[:, 0, :], scalar=0.0, in1=ff[:, 1, :],
                                        op0=ALU.min, op1=ALU.subtract))
            link(v.memset(ff[:, 0, :], 1.0))
            link(v.tensor_tensor_scan(ff[:, 1, :], ff[:, 0, :], ff[:, 2, :], 0.0, ALU.mult, ALU.add))
            v.tensor_scalar(neg_c, ff[:, 1, :], -1.0, None, ALU.mult).then_inc(c_ready, 1)
            lo(G_FV + 1, 0)
            place(LEVELS)
            dve.wait_ge(scr_free[0], use_number("diagonala"))
            dve.wait_ge(scr_free[1], use_number("diagonalb"))
            dve.sem_inc(attn_ready, 1)
            lo(G_FV + 1, 1)
            copy_group(G_FV, fv[:, :, 0:GW])
            half = scratch("cumulative")
            v.tensor_copy(c_tok[:, :, :], scr[:, half, 0:NT * H].rearrange("p (t h) -> p t h", t=NT)
                          ).then_inc(scr_free[half], 1)
            dve.wait_ge(scr_free[half], use_number("cumulative"))
            dve.sem_inc(gain_free, 1)
            lo(G_FV + 1, 2)

            def copy_o(t):
                half = scratch(f"o{t}")
                v.tensor_copy(o_hg[:, t, :], scr[:, half, :]).then_inc(o_ready, 1)
                dve.wait_ge(o_ready, 2 - t)
                dve.sem_inc(scr_free[half], 1)

            copy_o(1)
            lo(G_FV + 1, 3)

            def shift(pair):
                half = scratch(f"qk{pair}")
                if pair:
                    dve.wait_ge(scr_ready[1], use_number(f"pT{pair - 1}"))
                for b in range(2):
                    h = 2 * pair + b
                    src = scr[:, half, b * GW:b * GW + 384]
                    for t in range(NT):
                        n, at0, width = 2 * h + t, (0, P)[t], (t + 1) * P
                        link(v.scalar_tensor_tensor(out=prob[:, b, at0:at0 + width], in0=src[:, at0:at0 + width],
                                                    scalar=c_tok[:, t, h:h + 1], in1=fox_mask[:, S - width:S],
                                                    op0=ALU.add, op1=ALU.add))
                        v.tensor_reduce(fstat[:, 0, n:n + 1], prob[:, b, at0:at0 + width], AX.X, ALU.max,
                                        negate=True).then_inc(logit_ready, 1)
                dve.sem_inc(scr_free[half], 1)

            def normalize(pair):
                for b in range(2):
                    h = 2 * pair + b
                    dve.wait_ge(exp_ready, 2 * h + 2)
                    link(v.reciprocal(fstat[:, 2, 2 * h:2 * h + 2], fstat[:, 1, 2 * h:2 * h + 2]))
                    for t in range(NT):
                        n, at0, width = 2 * h + t, (0, P)[t], (t + 1) * P
                        last = v.tensor_scalar(prob[:, b, at0:at0 + width], prob[:, b, at0:at0 + width],
                                               fstat[:, 2, n:n + 1], None, ALU.mult)
                    last.then_inc(p_ready, 1)

            def copy_pT(pair):
                half = scratch(f"pT{pair}")
                v.tensor_copy(probT, scr[:, half, :].rearrange("p (b s) -> p b s", b=2)[:, :, 0:384]
                              ).then_inc(pT_ready, 1)
                dve.wait_ge(pT_ready, pair + 1)
                dve.sem_inc(scr_free[half], 1)

            def copy_ya(pair):
                half = scratch(f"pv{pair}")
                v.tensor_copy(yaT[:, 2 * pair:2 * pair + 2, :],
                              scr[:, half, :].rearrange("p (b s) -> p b s", b=2)[:, :, 0:S]
                              ).then_inc(scr_free[half], 1)
                if pair % 2:
                    dve.wait_ge(scr_free[half], use_number(f"pv{pair}"))
                    dve.sem_inc(ya_in, 1)

            for n in range(4):
                g = G_GA + n
                lo(g, 0)
                if n == 0:
                    copy_group(G_FV + 1, fv[:, :, GW:2 * GW])
                    copied(G_FV + 1)
                    dve.sem_inc(fv_ready, 1)
                shift(n)
                if n == 0:
                    copy_o(0)
                else:
                    copy_pT(n - 1)
                lo(g, 1)
                normalize(n)
                lo(g, 2)
                lo(g, 3)
                if n:
                    copy_ya(n - 1)
            lo(G_AUP, 0)
            lo(G_AUP, 1)
            copy_pT(3)
            copy_ya(3)
            for n in range(2):
                dve.wait_ge(ya_hi_ready, n + 1)
                k = slice(4 * n, 4 * n + 4)
                v.tensor_tensor(ya_lo[:, k, :], yaT[:, k, :], ya_hi[:, k, :].bitcast(fp32),
                                ALU.subtract).then_inc(ya_split, 1)

            def times_ya(n):
                dve.wait_ge(group_done, G_AUP + n + 1)
                dve.wait_ge(ga_ready, n + 1)
                part = T1[:, n * 2 * GW:(n + 1) * 2 * GW]
                v.tensor_tensor(part, part, acc[:, n % 2, :], ALU.mult).then_inc(acc_free[n % 2], 1)

            o_flat, sq = Z1[:, 0:8 * S], T2[:, HW:3 * HW]
            o_heads = o_flat.rearrange("p (u n) -> p u n", n=P)
            lo(G_AUP + 1, 0)
            link(v.tensor_tensor(sq, o_flat, o_flat, ALU.mult))
            lo(G_AUP + 1, 1)
            times_ya(0)
            link(v.tensor_reduce(stat[:, 0, :], sq.rearrange("p (u n) -> p u n", n=P), AX.X, ALU.add))
            lo(G_AUP + 2, 0)
            lo(G_AUP + 2, 1)
            times_ya(1)
            inverse_root(16, P, 2)
            lo(G_AUP + 3, 0)
            link(v.tensor_tensor(o_heads, o_heads, stat[:, 3, :].unsqueeze(2).to_broadcast([P, 16, P]), ALU.mult))
            lo(G_AUP + 3, 1)
            times_ya(2)
            dve.wait_ge(hg_gain_in, 16)
            link(v.tensor_tensor(o_hg, o_hg, hg_gain.unsqueeze(1).to_broadcast([P, NT, HW]), ALU.mult))
            lo(G_GB, 0)
            dve.wait_ge(hgate_ready, 1)
            v.tensor_tensor(o_hg, o_hg, hg_gate, ALU.mult).then_inc(ob_ready, 1)
            lo(G_GB, 1)
            times_ya(3)
            for n, t in enumerate((1, 0)):
                half = scratch(f"ob{t}")
                dve.wait_ge(ob_hi_ready, n + 1)
                cols = slice(t * P, (t + 1) * P)
                v.tensor_tensor(ob_lo[:, :, cols], scr[:, half, :].rearrange("p (h s) -> p h s", h=H),
                                ob_hi[:, :, cols].bitcast(fp32), ALU.subtract).then_inc(ob_split, 1)
                dve.wait_ge(ob_split, n + 1)
                dve.sem_inc(scr_free[half], 1)
            lo(G_GB, 2)
            lo(G_GB, 3)
            gated = T2[:, 2 * GW:4 * GW]

            def add_yb(n):
                dve.wait_ge(group_done, G_GB + 2 * n + 2)
                dve.wait_ge(gb_ready, n + 1)
                if n:
                    dve.wait_ge(gb_used, 1 + n)
                part = T1[:, n * 2 * GW:(n + 1) * 2 * GW]
                link(v.tensor_tensor(gated, T2[:, 0:2 * GW], acc[:, 1, :], ALU.mult))
                dve.sem_inc(acc_free[1], 1)
                v.tensor_tensor(part, part, gated, ALU.add).then_inc(gb_used, 1)

            for n in range(4):
                if n:
                    for m in range(4):
                        lo(G_GB + 2 * n, m)
                        if m == 1:
                            add_yb(n - 1)
                            if n < 3:
                                half = scratch(f"keys{n - 1}")
                                v.tensor_copy(V1[:, (n - 1) * HW:n * HW], scr[:, half, :]
                                              ).then_inc(scr_free[half], 1)
                lo(G_GB + 2 * n + 1, 0)
                lo(G_GB + 2 * n + 1, 1)
            lo(G_WO, 0)
            lo(G_WO, 1)
            add_yb(3)
            dve.wait_ge(gb_used, 5)
            dve.sem_inc(merged_ready, 1)
            for n in range(4):
                dve.wait_ge(merged_hi, n + 1)
                k = slice(4 * n, 4 * n + 4)
                v.tensor_tensor(hT_lo[:, k, :], merged[:, k, :], hT_hi[:, k, :].bitcast(fp32),
                                ALU.subtract).then_inc(merged_split, 1)
            lo(G_WO, 2)
            lo(G_WO, 3)

            def add_residual(n):
                dve.wait_ge(group_done, G_WO + n + 1)
                part = X[:, :, n * GW:(n + 1) * GW]
                v.tensor_tensor(part, part, acc[:, n % 2, :].rearrange("p (t n) -> p t n", t=NT), ALU.add
                                ).then_inc(acc_free[n % 2], 1)

            for n in range(1, 4):
                for m in range(4):
                    lo(G_WO + n, m)
                    if m == 1:
                        add_residual(n - 1)
            lo(G_WQ, 0)
            lo(G_WQ, 1)
            add_residual(3)
            copied(G_WO + 3)
            norm(gain2, 3)
            split_h("h2", 4)
            lo(G_WQ, 2)
            lo(G_WQ, 3)

            def top16(values, src, indices):
                w = src.shape[1]
                link(v.max(values[:, 0:8], src))
                v.max_index(indices[:, 0:8], values[:, 0:8], src)
                link(v.match_replace(rest[:, 0:w], values[:, 0:8], src, -3.0e38))
                link(v.max(values[:, 8:16], rest[:, 0:w]))
                link(v.max_index(indices[:, 8:16], values[:, 8:16], rest[:, 0:w]))

            def top_keys(t, u):
                top16(topv[:, u, :], scores[:, t, u, :], topi[:, u, :])

            def top_pairs(t, pair):
                us, hs = slice(4 * pair, 4 * pair + 4), slice(2 * pair, 2 * pair + 2)
                link(v.tensor_copy(topf[:, us, :], topi[:, us, :]))
                tv = topv[:, us, :].rearrange("p (h c) k -> p h c k", c=2)
                tf = topf[:, us, :].rearrange("p (h c) k -> p h c k", c=2)
                cands = cand.rearrange("p (h i j) -> p h i j", i=TOPK, j=TOPK)
                link(v.tensor_tensor(cands, tv[:, :, 0, :].unsqueeze(3).to_broadcast([P, 2, TOPK, TOPK]),
                                     tv[:, :, 1, :].unsqueeze(2).to_broadcast([P, 2, TOPK, TOPK]), ALU.add))
                ks = slice(2 * pair * TOPK, 2 * (pair + 1) * TOPK)
                for h in range(2):
                    kh = slice((2 * pair + h) * TOPK, (2 * pair + h + 1) * TOPK)
                    top16(best[:, t, kh], cand[:, h * S:(h + 1) * S], bpos[:, 0, kh])
                v.tensor_scalar(bpos[:, 1, ks], bpos[:, 0, ks], 4, None, ALU.logical_shift_right)
                link(v.tensor_scalar(bpos[:, 2, ks], bpos[:, 0, ks], TOPK - 1, None, ALU.bitwise_and))
                link(v.tensor_copy(bposf[:, 0:2, ks], bpos[:, 1:3, ks]))
                hots = hot.rearrange("p (m i) -> p m i", i=TOPK)
                hot4 = hot.rearrange("p (h m i) -> p h m i", m=TOPK, i=TOPK)
                for c in range(2):
                    link(v.tensor_tensor(hots, bposf[:, c, ks].unsqueeze(2).to_broadcast([P, 2 * TOPK, TOPK]),
                                         iota16[:, :].unsqueeze(1).to_broadcast([P, 2 * TOPK, TOPK]), ALU.is_equal))
                    link(v.tensor_tensor(hot4, hot4, tf[:, :, c, :].unsqueeze(2).to_broadcast([P, 2, TOPK, TOPK]),
                                         ALU.mult))
                    link(v.tensor_reduce(bposf[:, 2 + c, ks], hots, AX.X, ALU.add))
                link(v.scalar_tensor_tensor(out=bposf[:, 2, ks], in0=bposf[:, 2, ks], scalar=float(P),
                                            in1=bposf[:, 3, ks], op0=ALU.mult, op1=ALU.add))
                v.tensor_copy(expert[:, t, ks], bposf[:, 2, ks]).then_inc(expert_ready, 1)

            def copy_q(n):
                copy_group(G_WQ + n, Z2[:, n * 2 * GW:(n + 1) * 2 * GW])
                copied(G_WQ + n)
                dve.sem_inc(q_copied, 1)

            def copy_scores(n):
                half = scratch(f"score{n}")
                link(v.tensor_copy(scores[:, :, 4 * n:4 * n + 4, :].rearrange("p t u n -> p t (u n)"),
                                   scr[:, half, :].rearrange("p (t n) -> p t n", t=NT)))
                dve.sem_inc(scr_free[half], 1)

            for n in range(1, 4):
                lo(G_WQ + n, 0)
                lo(G_WQ + n, 1)
                copy_q(n - 1)
                if n > 1:
                    top_pairs(0, n - 2)
                lo(G_WQ + n, 2)
                copy_scores(n - 1)
                top_keys(0, 4 * (n - 1))
                top_keys(0, 4 * (n - 1) + 1)
                lo(G_WQ + n, 3)
                top_keys(0, 4 * (n - 1) + 2)
                top_keys(0, 4 * (n - 1) + 3)
            top_pairs(0, 2)
            copy_q(3)
            copy_scores(3)
            for u in range(12, 16):
                top_keys(0, u)
            top_pairs(0, 3)

            rounds = NSEL // SLOTS

            def dots(t):
                with dve.Fori(0, rounds) as i:
                    for j in range(SLOTS):
                        dve.wait_ge(row_landed[j], (2 * t * rounds + 1 + i) * 16)
                        v.scalar_tensor_tensor(out=slots[:, j, :], in0=slots[:, j, :], scalar=1.0, in1=N1[:, t, :],
                                               op0=ALU.mult, op1=ALU.mult,
                                               accum_out=hid[:, 0, ds(i * SLOTS + j, 1)]).then_inc(row_used[j], 1)
                for j in range(SLOTS):
                    dve.wait_ge(row_used[j], 1 + (2 * t + 1) * rounds)

            def weights(t):
                g3 = gate[:, 0, :].rearrange("p (h k) -> p h k", h=H)
                b3 = best[:, t, :].rearrange("p (h k) -> p h k", h=H)
                v.tensor_tensor(g3, b3, b3[:, :, 0:1].to_broadcast([P, H, TOPK]), ALU.subtract).then_inc(shifted, 1)
                dve.wait_ge(gate_exp, t + 1)
                link(v.tensor_reduce(gsum[:, 0, :], g3, AX.X, ALU.add))
                link(v.reciprocal(gsum[:, 1, :], gsum[:, 0, :]))
                link(v.tensor_tensor(g3, g3, gsum[:, 1, :].unsqueeze(2).to_broadcast([P, H, TOPK]), ALU.mult))
                z, w = hid[:, 0, :], hid[:, 1, :]
                link(v.tensor_tensor(w, z, z, ALU.mult))
                link(v.tensor_scalar(w, w, TANH_A * TANH_B, TANH_A, ALU.mult, ALU.add))
                v.tensor_tensor(w, w, z, ALU.mult).then_inc(tanh_in, 1)
                dve.wait_ge(tanh_ready, t + 1)
                link(v.scalar_tensor_tensor(out=hid[:, 2, :], in0=w, scalar=1.0, in1=z, op0=ALU.add, op1=ALU.mult))
                v.scalar_tensor_tensor(out=gate[:, 1, :], in0=hid[:, 2, :], scalar=0.5, in1=gate[:, 0, :],
                                       op0=ALU.mult, op1=ALU.mult).then_inc(weight_ready, 1)
                dve.wait_ge(weight_ready, t + 1)

            def add_rows(t, i, j):
                dve.wait_ge(row_landed[j], ((2 * t + 1) * rounds + 1 + i) * 16)
                link(v.scalar_tensor_tensor(out=y_dve, in0=slots[:, j, :], scalar=gate[:, 1, ds(i * SLOTS + j, 1)],
                                            in1=y_dve, op0=ALU.mult, op1=ALU.add))
                dve.sem_inc(row_used[j], 1)

            y = [acc[:, :, :].rearrange("p a n -> p (a n)"), scr[:, :, :].rearrange("p a n -> p (a n)")]
            squares = N1[:, 0, :]

            def finish_tile(t):
                dve.wait_ge(y_done, t + 1)
                if t < NT - 1:
                    link(v.tensor_tensor(X[:, t, :], y[t], y_dve, ALU.add))
                    link(v.scalar_tensor_tensor(out=squares, in0=X[:, t, :], scalar=1.0, in1=X[:, t, :],
                                                op0=ALU.mult, op1=ALU.mult, accum_out=stat[:, 0, 0:1]))
                else:
                    a_, b_ = slice(0, D // 2), slice(D // 2, D)
                    v.tensor_tensor(X[:, t, a_], y[t][:, a_], y_dve[:, a_], ALU.add).then_inc(y_summed, 1)
                    link(v.tensor_tensor(X[:, t, b_], y[t][:, b_], y_dve[:, b_], ALU.add))
                    link(v.scalar_tensor_tensor(out=squares[:, b_], in0=X[:, t, b_], scalar=1.0, in1=X[:, t, b_],
                                                op0=ALU.mult, op1=ALU.mult, accum_out=stat[:, 0, 0:1]))
                    dve.wait_ge(y_squared, 1)
                    dve.wait_ge(y_summed, 1)
                    link(v.tensor_tensor(stat[:, 0, 0:1], stat[:, 0, 0:1], stat[:, 5, 0:1], ALU.add))
                inverse_root(1, D, 4 + t)
                for part in range(2):
                    cols = slice(part * D // 2, (part + 1) * D // 2)
                    v.scalar_tensor_tensor(out=X[:, t, cols], in0=X[:, t, cols], scalar=stat[:, 3, 0:1],
                                           in1=gain_f[:, cols], op0=ALU.mult, op1=ALU.mult).then_inc(y_ready, 1)

            dots(0)
            weights(0)
            link(v.memset(y_dve, 0.0))
            for i in range(rounds):
                for k, j in enumerate(V_SLOTS):
                    add_rows(0, i, j)
                    u = 2 * i + k
                    if u < 16:
                        top_keys(1, u)
                    elif u < 24 and k == 0:
                        top_pairs(1, (u - 16) // 2)
            finish_tile(0)
            link(v.memset(y_dve, 0.0))
            dots(1)
            weights(1)
            with dve.Fori(0, rounds) as i:
                steps.enter(i, len(V_SLOTS))
                for j in V_SLOTS:
                    add_rows(1, i, j)
                steps.leave(rounds)
            finish_tile(1)

        @block.tensor
        def _(pe):
            t_ = nc.tensor

            def enter(name):
                if use_number(name) > 1:
                    pe.wait_ge(scr_free[half_of(name)], use_number(name) - 1)
                return half_of(name)

            def done(name, last):
                last.then_inc(scr_ready[half_of(name)], 1)

            def transposed_unit(g, m, src, i=0, per=0):
                pe.wait_ge(lo_ready, UNIT0[g] + m + 1 + i * per)
                if m == 0:
                    pe.wait_ge(acc_free[g % 2], 1 + g // 2 + i)
                hi_, lo_ = src
                end = m == units_of(g) - 1
                for k in range(UK):
                    kk = m * UK + k
                    for f in range(FB):
                        to, cols = acc[:, g % 2, f * S:(f + 1) * S], slice(f * P, (f + 1) * P)
                        wh, wl = w_hi[:, m % 2, k, cols], w_lo[:, m % 2, k, cols]
                        last_k = end and k == UK - 1
                        t_.matmul(to, wh, hi_[:, kk, :], start=kk == 0 and f % 2 == 0, stop=False,
                                  skip_group_check=True)
                        t_.matmul(to, wh, lo_[:, kk, :], start=False, stop=False, skip_group_check=True)
                        last = t_.matmul(to, wl, hi_[:, kk, :], start=False, stop=last_k, skip_group_check=True)
                last.then_inc(unit_done, 1)

            def natural_unit(g, m, src, i=0, per=0):
                pe.wait_ge(lo_ready, UNIT0[g] + m + 1 + i * per)
                if m == 0:
                    pe.wait_ge(acc_free[g % 2], 1 + g // 2 + i)
                hi_, lo_ = src
                end = m == units_of(g) - 1
                for k in range(UK):
                    kk = m * UK + k
                    for t in range(NT):
                        to, cols = acc[:, g % 2, t * GW:(t + 1) * GW], slice(t * P, (t + 1) * P)
                        t_.matmul(to, hi_[:, kk, cols], w_hi[:, m % 2, k, :], start=kk == 0, stop=False)
                        t_.matmul(to, hi_[:, kk, cols], w_lo[:, m % 2, k, :], start=False, stop=False)
                        last = t_.matmul(to, lo_[:, kk, cols], w_hi[:, m % 2, k, :], start=False,
                                         stop=end and k == UK - 1)
                last.then_inc(unit_done, 1)

            def finish(g, i=0, per=0):
                pe.wait_ge(unit_done, UNIT0[g + 1] + i * per)
                pe.sem_inc(group_done, 1)

            def loop_two(g0, unit, src):
                n = units_of(g0)
                with pe.Fori(0, 2) as i:
                    for g in (g0, g0 + 1):
                        for m in range(n):
                            unit(g, m, src, i, 2 * n)
                        finish(g, i, 2 * n)

            def transpose_norm(prefix):
                for n in range(4):
                    half = enter(f"{prefix}{n}")
                    for k in range(4):
                        for t in range(NT):
                            at0 = k * S + t * P
                            last = t_.transpose(scr[:, half, at0:at0 + P],
                                                N1[:, t, (4 * n + k) * P:(4 * n + k + 1) * P], ident[:, :])
                    done(f"{prefix}{n}", last)

            hT = (hT_hi, hT_lo)
            pe.wait_ge(consts_ready, 1)
            pe.wait_ge(vec_in, 16)
            half = enter("vectors")
            done("vectors", t_.transpose(scr[:, half, 0:16], vec[:, :], ident[0:16, 0:16]))
            pe.wait_ge(normed, 2)
            transpose_norm("h")
            pe.wait_ge(h_ready, 4)
            loop_two(G_HQF, transposed_unit, hT)
            loop_two(G_HIG, natural_unit, hT)

            def level_products(name, a, b, side, pieces):
                half = enter(name)
                for u in range(H):
                    at_a, at_b = pieces(side * H + u)
                    last = t_.matmul(scr[:, half, u * P:(u + 1) * P], a[:, at_a:at_a + P], b[:, at_b:at_b + P],
                                     start=True, stop=True)
                done(name, last)

            def own(u):
                return u * P, u * P

            for n in range(4):
                g = G_FQK + n
                for m in range(4):
                    transposed_unit(g, m, hT)
                    if m == 3:
                        finish(g)
                    if m % 2:
                        lv = 2 * n + m // 2
                        pe.wait_ge(level_ready, lv + 1)
                        e = level[lv % 2]
                        if lv < MASKED:
                            level_products(f"level{lv}a", e, e, 0, own)
                            level_products(f"level{lv}b", e, e, 1, own)
                        else:
                            level_products("across", e, e, 0, lambda u: (u * S, u * S + P))
            pe.wait_ge(wff_ready, 1)
            half = enter("forget")
            for t in range(NT):
                cols = slice(t * P, (t + 1) * P)
                to = scr[:, half, t * H:(t + 1) * H]
                for k in range(KD):
                    t_.matmul(to, hT_hi[:, k, cols], wff_hi[:, k, :], start=k == 0, stop=False)
                    t_.matmul(to, hT_hi[:, k, cols], wff_lo[:, k, :], start=False, stop=False)
                    last = t_.matmul(to, hT_lo[:, k, cols], wff_hi[:, k, :], start=False, stop=k == KD - 1)
            done("forget", last)
            natural_unit(G_FV, 0, hT)
            natural_unit(G_FV, 1, hT)
            half = enter("forgetT")
            pe.wait_ge(ff_tok_ready, 1)
            for t in range(NT):
                last = t_.transpose(scr[0:H, half, t * P:(t + 1) * P], ff_tok[:, t, :], ident[:, :])
            done("forgetT", last)
            natural_unit(G_FV, 2, hT)
            natural_unit(G_FV, 3, hT)
            finish(G_FV)
            level_products("diagonala", k_hg, q_hg, 0, own)
            level_products("diagonalb", k_hg, q_hg, 1, own)
            natural_unit(G_FV + 1, 0, hT)
            natural_unit(G_FV + 1, 1, hT)
            pe.wait_ge(c_ready, 1)
            half = enter("cumulative")
            for t in range(NT):
                last = t_.transpose(scr[:, half, t * H:(t + 1) * H], ff[:, 1, t * P:(t + 1) * P], ident[0:H, 0:H])
            done("cumulative", last)

            def hg_output(t):
                half = enter(f"o{t}")
                for h in range(H):
                    to, cols = scr[:, half, h * P:(h + 1) * P], slice(h * P, (h + 1) * P)
                    if t:
                        t_.matmul(to, attn_across[:, h, :], hg_v[:, 0, cols], start=True, stop=False)
                    last = t_.matmul(to, attn[:, 2 * h + t, :], hg_v[:, t, cols], start=(t == 0), stop=True)
                done(f"o{t}", last)

            pe.wait_ge(attn_ready, 1)
            hg_output(1)
            natural_unit(G_FV + 1, 2, hT)
            natural_unit(G_FV + 1, 3, hT)
            finish(G_FV + 1)

            def logits(pair):
                half = enter(f"qk{pair}")
                for b in range(2):
                    h = 2 * pair + b
                    for t in range(NT):
                        at0, width = b * GW + (0, P)[t], (t + 1) * P
                        to = scr[:, half, at0:at0 + width]
                        t_.matmul(to, fqT[:, h, t * P:(t + 1) * P], fkT[:, h, 0:width], start=True, stop=False)
                        last = t_.matmul(to, ident[0:H, h:h + 1].to_broadcast([H, P]), neg_c[:, 0:width],
                                         start=False, stop=True)
                done(f"qk{pair}", last)

            def transpose_p(pair):
                half = enter(f"pT{pair}")
                for b in range(2):
                    pe.wait_ge(p_ready, 2 * pair + b + 1)
                    for n in range(3):
                        last = t_.transpose(scr[:, half, b * GW + n * P:b * GW + (n + 1) * P],
                                            prob[:, b, n * P:(n + 1) * P], ident[:, :])
                done(f"pT{pair}", last)

            def weighted_v(pair):
                half = enter(f"pv{pair}")
                pe.wait_ge(pT_ready, pair + 1)
                for b in range(2):
                    h = 2 * pair + b
                    cols = slice(h * P, (h + 1) * P)
                    t_.matmul(scr[:, half, b * GW:b * GW + S], fv[:, 0, cols], probT[:, b, 0:S],
                              start=True, stop=False)
                    last = t_.matmul(scr[:, half, b * GW + P:b * GW + S], fv[:, 1, cols], probT[:, b, S:384],
                                     start=False, stop=True)
                done(f"pv{pair}", last)

            pe.wait_ge(q_scaled, 1)
            logits(0)
            hg_output(0)
            for n in range(4):
                g = G_GA + n
                transposed_unit(g, 0, hT)
                transposed_unit(g, 1, hT)
                if n:
                    if n == 1:
                        pe.wait_ge(fv_ready, 1)
                    weighted_v(n - 1)
                transposed_unit(g, 2, hT)
                transposed_unit(g, 3, hT)
                finish(g)
                transpose_p(n)
                if n < 3:
                    logits(n + 1)
            weighted_v(3)
            pe.wait_ge(ya_split, 2)
            loop_two(G_AUP, transposed_unit, (ya_hi, ya_lo))
            for n in range(4):
                g = G_GB + 2 * n
                for m in range(4):
                    transposed_unit(g, m, hT)
                    if n == 0 and m == 0:
                        pe.wait_ge(ob_ready, 1)
                        for t in (1, 0):
                            half = enter(f"ob{t}")
                            for h in range(H):
                                last = t_.transpose(scr[:, half, h * P:(h + 1) * P], o_hg[:, t, h * P:(h + 1) * P],
                                                    ident[:, :])
                            done(f"ob{t}", last)
                finish(g)
                if n == 0:
                    pe.wait_ge(ob_split, 2)
                transposed_unit(g + 1, 0, (ob_hi, ob_lo))
                transposed_unit(g + 1, 1, (ob_hi, ob_lo))
                finish(g + 1)
                if n < 2:
                    pe.wait_ge(keys_in, 16)
                    half = enter(f"keys{n}")
                    for u in range(8):
                        last = t_.transpose(scr[:, half, u * P:(u + 1) * P], keys_sb[:, 8 * n + u, :], ident[:, :])
                    done(f"keys{n}", last)
            for m in range(4):
                pe.wait_ge(merged_split, m + 1)
                natural_unit(G_WO, m, hT)
            finish(G_WO)
            for g in range(G_WO + 1, G_WQ):
                for m in range(4):
                    natural_unit(g, m, hT)
                finish(g)
            pe.wait_ge(normed, 4)
            transpose_norm("h2")

            def score(n):
                half = enter(f"score{n}")
                pe.wait_ge(q_copied, n + 1)
                for t in range(NT):
                    for u in range(4):
                        b = 4 * n + u
                        last = t_.matmul(scr[:, half, (4 * t + u) * P:(4 * t + u + 1) * P],
                                         pqT[:, b, t * P:(t + 1) * P], keysT[:, b, :], start=True, stop=True)
                done(f"score{n}", last)

            for n in range(4):
                g = G_WQ + n
                for m in range(4):
                    if n == 0:
                        pe.wait_ge(h_ready, 4 + m + 1)
                    transposed_unit(g, m, hT)
                    if n and m == 1:
                        score(n - 1)
                finish(g)
            score(3)
            pe.wait_ge(acc_free[0], 1 + G_END // 2)
            pe.wait_ge(acc_free[1], 1 + G_END // 2)
            pe.wait_ge(scr_free[0], use_number("score2"))
            pe.wait_ge(scr_free[1], use_number("score3"))
            rounds = NSEL // SLOTS
            banks = [[(acc, scr)[t][:, b // 2, (b % 2) * GW:(b % 2 + 1) * GW] for b in range(4)] for t in range(NT)]
            for t in range(NT):
                for b in range(4):
                    t_.matmul(banks[t][b], ident[:, :], X[:, t, b * GW:(b + 1) * GW], start=True, stop=False)

                def add_rows(i, last_round):
                    for j in T_SLOTS:
                        pe.wait_ge(row_landed[j], ((2 * t + 1) * rounds + 1 + i) * 16)
                        pe.wait_ge(diag_ready[j], t * rounds + 1 + i)
                        for b in range(4):
                            last = t_.matmul(banks[t][b], diag[:, j, :], slots[:, j, b * GW:(b + 1) * GW],
                                             start=False, stop=last_round and j == T_SLOTS[-1])
                        last.then_inc(row_used[j], 1)

                with pe.Fori(0, rounds - 1) as i:
                    add_rows(i, False)
                add_rows(rounds - 1, True)
                for j in T_SLOTS:
                    pe.wait_ge(row_used[j], 1 + (2 * t + 2) * rounds)
                pe.sem_inc(y_done, 1)


_INS = ["x", "norm1_g", "w_in", "fox_f_bias", "hg_lb_logits", "hg_norm_g", "w_a_up", "w_b_up", "w_o", "norm2_g",
        "peer_wq", "peer_keys", "peer_u", "peer_v", "norm_f_g"]


def kernel(**inputs):
    import numpy as np
    import concourse.bacc as bacc
    from concourse.bass_utils import run_bass_kernel_spmd as run

    nc = bacc.Bacc("TRN2", target_bir_lowering=False, num_devices=1)
    arrays, args = {}, []
    for name in _INS:
        a = np.ascontiguousarray(inputs[name])
        arrays[f"in_{name}"] = a
        args.append(nc.dram_tensor(f"in_{name}", a.shape, mybir.dt.from_np(a.dtype), kind="ExternalInput").ap())
    args.append(nc.dram_tensor("out_0", (1, S, D), mybir.dt.float32, kind="ExternalOutput").ap())
    build(nc, *args)
    return run(nc, [arrays], core_ids=[0]).results[0]["out_0"]
```

```python
import numpy as np
import concourse.bass as bass
from concourse import mybir
from contextlib import ExitStack

P = 128
S = 256
NT = S // P
D = 2048
KD = D // P
H = 8
HW = H * P
GW = 512
FB = GW // P
CH = 64
EPS = 1e-6
TOPK = 16
NSEL = H * TOPK
SCALE = float(P) ** -0.5
COL_FQ, COL_FV, COL_FF = 0, 2 * HW, 3 * HW
COL_HQ = COL_FF + H
COL_HI = COL_HQ + 2 * HW
COL_GA = COL_HI + 2 * HW
COL_GB = COL_GA + D
G_HQF, G_HIG, G_FQK, G_FV, G_GA, G_AUP, G_GB, G_WO, G_WQ, G_END = 0, 4, 8, 12, 14, 18, 22, 30, 34, 38
UK = 4


def units_of(g):
    narrow = G_AUP <= g < G_GB or (G_GB <= g < G_WO and (g - G_GB) % 2)
    return (HW if narrow else D) // P // UK


UNIT0 = [sum(units_of(i) for i in range(g)) for g in range(G_END + 1)]
LEVELS = 8
MASKED = LEVELS - 1
SLOTS = 8
ROUNDS = H * TOPK // SLOTS
SC = 4
CW = GW
DW = D - CW
VW = DW // 2
CRING = 4
VRING = 4
PIECES = 4
NEG = -1.0e30
TANH_A, TANH_B = 0.7978845608028654, 0.044715


def scratch_uses():
    uses = [("vectors", 0)] + [(f"h{n}", n % 2) for n in range(4)]
    for lv in range(MASKED):
        uses += [(f"level{lv}a", 0), (f"level{lv}b", 1)]
    uses += [("across", 0), ("forget", 1), ("diagonala", 0), ("diagonalb", 1),
             ("cumulative", 0), ("o1", 1), ("qk0", 0), ("o0", 1)]
    for pair in range(4):
        uses += [(f"pT{pair}", 1)] + [(f"qk{pair + 1}", 0)] * (pair < 3) + [(f"pv{pair}", 1)]
    uses += [("ob1", 0), ("ob0", 1)]
    uses += [(f"keys{n}", n) for n in range(2)]
    uses += [(f"h2{n}", n % 2) for n in range(4)]
    uses += [(f"score{n}", n % 2) for n in range(4)]
    return uses


USES = scratch_uses()


def half_of(name):
    return dict(USES)[name]


def use_number(name):
    half, count = half_of(name), 0
    for other, h in USES:
        count += h == half
        if other == name:
            return count


def halves(a, size):
    blocks = a.rearrange("p (n u h) -> p n u h", u=2, h=size // 2)
    return blocks[:, :, 0, :], blocks[:, :, 1, :]


class Chain:

    def __init__(self, engine, sem):
        self.engine, self.sem, self.n, self.turn = engine, sem, 0, 0

    def link(self, instruction):
        self.n += 1
        instruction.then_inc(self.sem, 1)
        self.engine.wait_ge(self.sem, self.n + self.turn)

    def enter(self, i, links):
        self.turn, self.start, self.links = i * links, self.n, links

    def leave(self, turns):
        assert self.n - self.start == self.links, (self.n - self.start, self.links)
        self.n, self.turn = self.start + self.links * turns, 0


def build(nc, x, norm1_g, w_in, fox_f_bias, hg_lb_logits, hg_norm_g, w_a_up, w_b_up, w_o, norm2_g,
          peer_wq, peer_keys, peer_u, peer_v, norm_f_g, out):
    fp32, u32, f32r = mybir.dt.float32, mybir.dt.uint32, mybir.dt.float32r
    ALU, ACT, AX = mybir.AluOpType, mybir.ActivationFunctionType, mybir.AxisListType
    ds = bass.ds

    x_d = x.rearrange("b (t p) d -> p (b t) d", p=P)
    out_d = out.rearrange("b (t p) d -> p (b t) d", p=P)
    w_in_d = w_in.rearrange("l (k p) n -> p (l k) n", p=P)
    w_a_d = w_a_up.rearrange("l (k p) n -> p (l k) n", p=P)
    w_b_d = w_b_up.rearrange("l (k p) n -> p (l k) n", p=P)
    w_o_d = w_o.rearrange("l (k p) n -> p (l k) n", p=P)
    wq_d = peer_wq.rearrange("l (k p) n -> p (l k) n", p=P)
    keys_d = peer_keys.rearrange("l h c n d -> n (l h c) d")
    u_rows = peer_u.rearrange("l e d -> (l e) d")
    v_starts = peer_v.rearrange("l e (c d) -> (l e c) d", d=CW)
    v_d = peer_v.rearrange("l (a b) d -> b (l a) d", b=P)

    ctx = ExitStack()
    with ctx:
        def sb(name, shape, dt=fp32):
            return ctx.enter_context(nc.sbuf_tensor(name, shape, dt))

        def sem(name):
            return ctx.enter_context(nc.semaphore(name))

        ident = sb("ident", [P, P])
        fox_mask = sb("fox_mask", [P, S])
        vec = sb("vec", [16, P])
        vecT = sb("vecT", [P, 16])
        wff = sb("wff", [P, KD, H])
        wff_hi, wff_lo = sb("wff_hi", [P, KD, H], f32r), sb("wff_lo", [P, KD, H], f32r)
        ff_bias = sb("ff_bias", [H, 1])
        c_tok = sb("c_tok", [P, NT, H])
        lb = sb("lb", [P, 4, H])
        stat = sb("stat", [P, 6, 16])
        fstat = sb("fstat", [P, 3, 16])
        iota16 = sb("iota16", [P, TOPK])
        stage = sb("stage", [P, 2, SLOTS], u32)
        gsum = sb("gsum", [P, 2, H])
        ij_stage, start_stage = sb("ij_stage", [P, 2, SC]), sb("start_stage", [P, CRING], u32)

        KB = 256
        arena_at = (nc.sbuf_base + 31) // 32 * 32
        sb("arena", [P, 202 * KB])

        def at(name, kib, shape, dt=fp32):
            return nc.alloc_sbuf_tensor_at(name, [P, *shape], dt, offset=arena_at + kib * 1024)

        X = at("X", 0, [NT, D])
        hT_hi = at("hT_hi", 16, [KD, S], f32r)
        hT_lo = at("hT_lo", 32, [KD, S], f32r)
        raw = at("raw", 48, [2, UK, GW])
        w_hi = at("w_hi", 64, [2, UK, GW], f32r)
        w_lo = at("w_lo", 80, [2, UK, GW], f32r)
        slots = at("slots", 32, [SLOTS, D])
        scores = at("scores", 16, [NT, 16, P])
        Z1 = at("Z1", 96, [16 * S])
        h2T_hi = at("h2T_hi", 96, [KD, S], f32r)
        N1 = at("N1", 112, [NT, D])
        ob_hi = at("ob_hi", 112, [H, S], f32r)
        ob_lo = at("ob_lo", 120, [H, S], f32r)
        Z2 = at("Z2", 128, [16 * S])
        h2T_lo = at("h2T_lo", 128, [KD, S], f32r)
        ya_hi = at("ya_hi", 128, [H, S], f32r)
        ya_lo = at("ya_lo", 136, [H, S], f32r)
        V1 = at("V1", 144, [NT * HW])
        T1 = at("T1", 152, [16 * S])
        T2 = at("T2", 168, [16 * S])
        A2 = at("A2", 184, [3 * HW])
        masks = at("masks", 196, [LEVELS, P])
        weight_of1 = at("weight_of1", 32, [P, P])
        weight_of = [[at(f"weight_of0_{q}", kib, [P // PIECES, P]) for q, kib in enumerate((16, 128, 144, 168))],
                     [weight_of1[:, q * P // PIECES:(q + 1) * P // PIECES, :] for q in range(PIECES)]]
        v_raw = [at("v_raw0", 112, [2, VW]), at("v_raw1", 118, [2, VW])]
        v_hi, v_lo = at("v_hi", 184, [4, VW], f32r), at("v_lo", 160, [2, VW], f32r)
        gain_f = at("gain_f", 16, [D])
        starts = [at("starts0", 124, [2, CW]), at("starts1", 196, [2, CW])]
        ff_room = at("ff_room", 200, [2 * KB])

        room = [0]

        def carve(name, *shape, dt=fp32):
            lo, room[0] = room[0], room[0] + int(np.prod(shape)) * 4
            assert room[0] <= 16 * 1024
            return nc.alloc_sbuf_tensor_at(name, [P, *shape], dt, offset=arena_at + 96 * 1024 + lo)

        gate, weight, hid = carve("gate", NSEL), carve("weight", NT, NSEL), carve("hid", 3, NSEL)
        ijT, gateT = carve("ijT", NT, 2, P), carve("gateT", NT, P)
        hot_a, hot_b = carve("hot_a", 2, SC, P), carve("hot_b", 2, SC, P)
        hot_a1 = at("hot_a1", 160, [4, SC, P])
        room[0] -= 2 * 2 * SC * P * 4
        e_hi, e_lo = carve("e_hi", 2, NT, P, dt=f32r), carve("e_lo", 2, NT, P, dt=f32r)
        spot = [0]

        def spare(name, *shape, dt=fp32):
            lo, spot[0] = spot[0], spot[0] + int(np.prod(shape)) * 4
            assert spot[0] <= 12 * 1024
            return nc.alloc_sbuf_tensor_at(name, [P, *shape], dt, offset=arena_at + 184 * 1024 + lo)

        topv, topf, topi = spare("topv", 16, TOPK), spare("topf", 16, TOPK), spare("topi", 16, TOPK, dt=u32)
        best = spare("best", NT, NSEL)
        expert = at("expert", 200, [NT, NSEL], u32)
        bpos, bposf, rest = spare("bpos", 3, NSEL, dt=u32), spare("bposf", 3, NSEL), spare("rest", 2 * P)
        ij = spare("ij", NT, 2, NSEL)

        q_hg, k_hg = Z1[:, 0:8 * S], Z1[:, 8 * S:16 * S]
        o_hg = Z1[:, 0:8 * S].rearrange("p (t f) -> p t f", t=NT)
        hg_v, hg_gate = N1[:, :, 0:HW], N1[:, :, HW:D]
        fqT = Z2[:, 0:8 * S].rearrange("p (h s) -> p h s", h=H)
        fkT = Z2[:, 8 * S:16 * S].rearrange("p (h s) -> p h s", h=H)
        pqT = T2[:, D:2 * D].rearrange("p (a u s) -> p a u s", a=2, s=S)
        fv = V1[:, :].rearrange("p (t f) -> p t f", t=NT)
        keysT = V1[:, :].rearrange("p (u n) -> p u n", n=P)
        b_chunk, b_tile = T1[:, 0:8 * S], T1[:, 8 * S:16 * S]
        merged = T1[:, :].rearrange("p (k s) -> p k s", s=S)
        gain1 = T1[:, 0:D]
        level = [T2[:, 0:8 * S], T2[:, 8 * S:16 * S]]
        hg_gain = T2[:, 0:HW]
        prob = T2[:, 2 * HW:2 * HW + 2 * 384].rearrange("p (a s) -> p a s", a=2)
        probT = T2[:, 3 * HW:3 * HW + 2 * 384].rearrange("p (a s) -> p a s", a=2)
        squares = T2[:, 0:4 * GW].rearrange("p (a n) -> p a n", n=GW)
        gain2 = T1[:, 0:D]
        cand, hot = T2[:, 0:2 * S], T2[:, 2 * S:4 * S]
        attn = A2[:, 0:2 * HW].rearrange("p (u s) -> p u s", s=P)
        attn_across = A2[:, 2 * HW:3 * HW].rearrange("p (h s) -> p h s", s=P)
        yaT = A2[:, 0:2 * HW].rearrange("p (h s) -> p h s", h=H)
        keys_sb = A2[:, 0:2 * HW].rearrange("p (u d) -> p u d", d=P)
        ff = T2[0:H, 0:4 * S].rearrange("p (n s) -> p n s", s=S)
        neg_c = ff_room[0:H, 0:S]
        iota_p = ff_room[:, S:S + P]

        acc = ctx.enter_context(nc.psum_tensor("acc", [P, 2, 2 * GW], fp32))
        scr = ctx.enter_context(nc.psum_tensor("scr", [P, 2, 2 * GW], fp32))

        x_in, gain1_in, vec_in, small_in = [sem("x_in0"), sem("x_in1")], sem("gain1_in"), sem("vec_in"), sem("small_in")
        raw_landed = [sem("raw_landed0"), sem("raw_landed1")]
        hi_ready, lo_ready = sem("hi_ready"), sem("lo_ready")
        unit_done, group_done = sem("unit_done"), sem("group_done")
        acc_free = [sem("acc_free0"), sem("acc_free1")]
        scr_ready = [sem("scr_ready0"), sem("scr_ready1")]
        scr_free = [sem("scr_free0"), sem("scr_free1")]
        consts_ready, pool_step, dve_step = sem("consts_ready"), sem("pool_step"), sem("dve_step")
        squared, mean_ready, root_ready, normed = sem("squared"), sem("mean_ready"), sem("root_ready"), sem("normed")
        r_ready, h2_ready = sem("r_ready"), sem("h2_ready")
        h_hi_ready, h_ready = sem("h_hi_ready"), sem("h_ready")
        lb_diff, lb_exp = sem("lb_diff"), sem("lb_exp")
        hqf_ready, k_sig, q_silu = sem("hqf_ready"), sem("k_sig"), sem("q_silu")
        f_ready, logf_ready, k_ready = sem("f_ready"), sem("logf_ready"), sem("k_ready")
        b_ready, reset_ready = sem("b_ready"), sem("reset_ready")
        hgate_in, hgate_ready = sem("hgate_in"), sem("hgate_ready")
        diff_ready, decay_ready, level_ready = sem("diff_ready"), sem("decay_ready"), sem("level_ready")
        wff_hi_ready, wff_ready = sem("wff_hi_ready"), sem("wff_ready")
        ff_in, ff_abs, ff_exp = sem("ff_in"), sem("ff_abs"), sem("ff_exp")
        ff_log, c_ready, attn_ready, q_scaled = sem("ff_log"), sem("c_ready"), sem("attn_ready"), sem("q_scaled")
        fv_ready, gain_free, hg_gain_in = sem("fv_ready"), sem("gain_free"), sem("hg_gain_in")
        o_ready, ob_ready, ob_hi_ready, ob_split = sem("o_ready"), sem("ob_ready"), sem("ob_hi_ready"), sem("ob_split")
        logit_ready, exp_ready, p_ready = sem("logit_ready"), sem("exp_ready"), sem("p_ready")
        pT_ready, ya_in, ya_hi_ready, ya_split = sem("pT_ready"), sem("ya_in"), sem("ya_hi_ready"), sem("ya_split")
        ga_ready, gb_ready, gb_used = sem("ga_ready"), sem("gb_ready"), sem("gb_used")
        merged_hi, merged_split = sem("merged_hi"), sem("merged_split")
        keys_in, gain2_in, gain_f_in, q_copied = sem("keys_in"), sem("gain2_in"), sem("gain_f_in"), sem("q_copied")
        shifted, gate_exp, expert_ready = sem("shifted"), sem("gate_exp"), sem("expert_ready")
        h_used = sem("h_used")
        granted, granted_w = sem("granted"), sem("granted_w")
        row_landed = [sem(f"row_landed{j}") for j in range(SLOTS)]
        row_used = [sem(f"row_used{j}") for j in range(SLOTS)]
        tanh_in, tanh_ready, weight_ready = sem("tanh_in"), sem("tanh_ready"), sem("weight_ready")
        ij_landed, ij_ready = sem("ij_landed"), sem("ij_ready")
        gate_landed, gateT_ready = sem("gate_landed"), sem("gateT_ready")
        a_ready = [sem("a_ready0"), sem("a_ready1_even"), sem("a_ready1_odd")]
        a_dist, b_hot_ready, hot_used, scattered = sem("a_dist"), sem("b_hot_ready"), sem("hot_used"), sem("scattered")
        start_landed = [sem(f"start_landed{j}") for j in range(CRING)]
        start_used = [sem(f"start_used{j}") for j in range(CRING)]
        v_landed = [sem(f"v_landed{j}") for j in range(VRING)]
        e_hi_ready, e_ready, v_hi_ready, v_ready, v_used = (
            sem("e_hi_ready"), sem("e_ready"), sem("v_hi_ready"), sem("v_ready"), sem("v_used"))
        y_summed, y_ready, out_done = sem("y_summed"), sem("y_ready"), sem("out_done")

        def weights_of_block(t, q, a):
            return weight_of[t][q][:, ds(a, 1), :].rearrange("p a s -> p (a s)")

        def v_loops(engine, body):
            turns = P // PIECES // 2
            for q in range(PIECES):
                lo_, hi_ = int(q == 0), turns - int(q == PIECES - 1)
                if q == 0:
                    body(0, 0, True)
                with engine.Fori(lo_, hi_) as i:
                    body(q, i)
                if q == PIECES - 1:
                    body(q, turns - 1)

        block = ctx.enter_context(nc.Block())

        @block.sync
        def _(sp):
            sp.dma_start(vec[:, :], hg_lb_logits.rearrange("l (h p) -> (l h) p", p=P)).then_inc(vec_in, 16)
            for t in (1, 0):
                sp.dma_start(X[:, t, :], x_d[:, t, :]).then_inc(x_in[t], 16)
            sp.dma_start(gain1, norm1_g.partition_broadcast(P).rearrange("q l f -> q (l f)")).then_inc(gain1_in, 16)

            def load(src, cols, m, u, wait=True):
                if wait:
                    sp.wait_ge(lo_ready, u - 1)
                    sp.sem_inc(granted_w, 1)
                sp.dma_start(raw[:, m % 2, :, :], src[:, m * UK:(m + 1) * UK, cols]).then_inc(raw_landed[m % 2], 16)

            def load_loop(g0, groups, src, col0):
                n = units_of(g0)
                with sp.Fori(0, groups) as i:
                    for m in range(n):
                        load(src, ds(col0 + i * GW, GW), m, UNIT0[g0] + m + i * n)

            for m in range(4):
                load(w_in_d, slice(COL_HQ, COL_HQ + GW), m, m, wait=m >= 2)
            sp.dma_start(wff[:, :, :], w_in_d[:, :, COL_FF:COL_FF + H]).then_inc(small_in, 16)
            sp.dma_start(ff_bias[:, :], fox_f_bias.rearrange("l h -> h l")).then_inc(small_in, 16)
            load_loop(G_HQF + 1, 3, w_in_d, COL_HQ + GW)
            load_loop(G_HIG, 4, w_in_d, COL_HI)
            load_loop(G_FQK, 4, w_in_d, COL_FQ)
            load_loop(G_FV, 2, w_in_d, COL_FV)
            load_loop(G_GA, 4, w_in_d, COL_GA)
            load_loop(G_AUP, 4, w_a_d, 0)
            with sp.Fori(0, 4) as i:
                for m in range(units_of(G_GB)):
                    load(w_in_d, ds(COL_GB + i * GW, GW), m, UNIT0[G_GB] + m + 6 * i)
                for m in range(units_of(G_GB + 1)):
                    load(w_b_d, ds(i * GW, GW), m, UNIT0[G_GB + 1] + m + 6 * i)
            load_loop(G_WO, 4, w_o_d, 0)
            load_loop(G_WQ, 4, wq_d, 0)
            def load_v(rows, j):
                sp.dma_start(v_raw[j // 2][:, j % 2, :], v_d[:, rows, CW + (j % 2) * VW:CW + (j % 2 + 1) * VW]
                             ).then_inc(v_landed[j], 16)

            sp.wait_ge(h_used, 1)
            load_v(slice(0, 1), 0)
            load_v(slice(0, 1), 1)
            sp.wait_ge(h_used, 2)
            load_v(slice(1, 2), 2)
            load_v(slice(1, 2), 3)
            with sp.Fori(0, P // 2 - 1) as i:
                for j in range(VRING):
                    sp.wait_ge(v_ready, VRING * i + j + 1)
                    sp.sem_inc(granted_w, 1)
                    load_v(ds(2 * i + 2 + j // 2, 1), j)
            for n in range(2 * NT):
                t, cols = n // 2, slice(n % 2 * D // 2, (n % 2 + 1) * D // 2)
                sp.wait_ge(y_ready, n + 1)
                sp.dma_start(out_d[:, t, cols], X[:, t, cols]).then_inc(out_done, 16)
            sp.wait_ge(out_done, 16 * 2 * NT)

        @block.gpsimd
        def _(pool):
            g = nc.gpsimd
            steps = Chain(pool, pool_step)
            g.memset(ident[:, :], 0.0)
            g.memset(masks[:, :, :], 0.0)
            steps.link(g.memset(fox_mask[:, :], 0.0))
            g.affine_select(out=ident[:, :], in_=ident[:, :], compare_op=ALU.not_equal, fill=1.0, base=0,
                            pattern=[[-1, P]], channel_multiplier=1).then_inc(consts_ready, 1)
            steps.link(g.affine_select(out=fox_mask[:, P:S], in_=fox_mask[:, P:S], compare_op=ALU.is_ge,
                                       fill=NEG, base=0, pattern=[[-1, P]], channel_multiplier=1))
            steps.link(g.iota(iota_p, [[1, P]], base=0, channel_multiplier=0, allow_small_or_imprecise_dtypes=True))
            steps.link(g.iota(iota16[:, :], [[1, TOPK]], base=0, channel_multiplier=0,
                              allow_small_or_imprecise_dtypes=True))
            uppers = []
            for lv in range(MASKED):
                half = 1 << lv
                uppers.append(masks[:, lv, :].rearrange("p (n u h) -> p n u h", u=2, h=half)[:, :, 1, :])
                last = g.memset(uppers[lv], 1.0)
            steps.link(last)
            for lv in range(MASKED):
                half, n = 1 << lv, P >> (lv + 1)
                last = g.affine_select(out=uppers[lv], in_=uppers[lv], compare_op=ALU.is_ge, fill=0.0, base=0,
                                       pattern=[[-2 * half, n], [0, half]], channel_multiplier=1)
            steps.link(last)
            for lv in range(MASKED):
                half, n = 1 << lv, P >> (lv + 1)
                g.affine_select(out=uppers[lv], in_=uppers[lv], compare_op=ALU.is_ge, fill=0.0, base=half - 1,
                                pattern=[[2 * half, n], [0, half]], channel_multiplier=-1)
            g.affine_select(out=masks[:, MASKED, :], in_=masks[:, MASKED, :], compare_op=ALU.not_equal, fill=1.0,
                            base=0, pattern=[[-1, P]], channel_multiplier=1).then_inc(consts_ready, 1)
            pool.wait_ge(b_ready, 1)
            for lv in range(LEVELS):
                if lv >= 2:
                    pool.wait_ge(scr_ready[1], use_number(f"level{lv - 2}b"))
                size = 2 << lv
                e_lo, e_up = halves(level[lv % 2], size)
                b_lo, b_up = halves(b_tile if lv == LEVELS - 1 else b_chunk, size)
                ref = b_lo[:, :, size // 2 - 1:size // 2].to_broadcast([P, 8 * S // size, size // 2])
                g.tensor_tensor(e_lo, ref, b_lo, ALU.subtract)
                if lv < LEVELS - 2:
                    last = g.tensor_tensor(e_up, b_up, ref, ALU.subtract)
                else:
                    last = g.tensor_copy(e_up, b_up)
                last.then_inc(diff_ready, 1)
            pool.wait_ge(gain_free, 1)
            pool.dma_start(hg_gain, hg_norm_g.partition_broadcast(P).rearrange("q l f -> q (l f)")
                           ).then_inc(hg_gain_in, 16)
            pool.wait_ge(ya_split, 2)
            pool.dma_start(keys_sb, keys_d).then_inc(keys_in, 16)
            pool.wait_ge(merged_split, 4)
            pool.dma_start(gain2, norm2_g.partition_broadcast(P).rearrange("q l f -> q (l f)")).then_inc(gain2_in, 16)
            for t in range(NT):
                for pair in range(4):
                    pool.wait_ge(expert_ready, 4 * t + pair + 1)
                    first_round = t * ROUNDS + pair * ROUNDS // 4
                    with pool.Fori(0, ROUNDS // 8) as i:
                        steps.enter(i, 2)
                        for side in range(2):
                            steps.link(g.tensor_copy(stage[:, side, :], expert[:, t, ds(
                                pair * NSEL // 4 + (2 * i + side) * SLOTS, SLOTS)]))
                            for j in range(SLOTS):
                                if t == 0 and pair == 0 and side == 0 and j == 2:
                                    pool.wait_ge(group_done, G_END)
                                pool.wait_ge(row_used[j], 1 + first_round + 2 * i + side)
                                pool.sem_inc(granted, 1)
                                pool.indirect_dma_start(
                                    slots[:, j, :], None, u_rows,
                                    bass.IndirectOffsetOnAxis(ap=stage[:, side, j:j + 1], axis=0)
                                ).then_inc(row_landed[j], 16)
                        steps.leave(ROUNDS // 8)
            with pool.Fori(0, P // SC // 4) as i:
                steps.enter(i, 2)
                for side in range(2):
                    pool.wait_ge(hot_used, P // SC - 1 + 2 * (2 * i + side))
                    steps.link(g.tensor_copy(ij_stage[:, side, :], ijT[:, 1, 0, ds((2 * i + side) * 2 * SC, SC)]))
                    pool.sem_inc(granted, 1)
                    for c in range(SC):
                        last = g.tensor_scalar(hot_a1[:, 2 * side, c, :], iota_p, ij_stage[:, side, c:c + 1], None,
                                               ALU.is_equal)
                    last.then_inc(a_ready[1], 1)
                steps.leave(P // SC // 4)

            pool.wait_ge(h_used, 2)

            def gather_starts(q, i):
                for j in range(CRING):
                    pool.wait_ge(start_used[j], 1 + q * P // PIECES // 2 + i)
                    steps.link(g.tensor_copy(start_stage[:, j:j + 1], expert[:, q // 2, ds(
                        q % 2 * (NSEL // 2) + CRING * i + j, 1)]))
                    pool.sem_inc(granted, 1)
                    pool.indirect_dma_start(starts[j // 2][:, j % 2, :], None, v_starts,
                                            bass.IndirectOffsetOnAxis(ap=start_stage[:, j:j + 1], axis=0)
                                            ).then_inc(start_landed[j], 16)

            for q in range(PIECES):
                if q == PIECES - 1:
                    pool.wait_ge(v_used, 2 * P // PIECES)
                    pool.dma_start(gain_f[:, :], norm_f_g.rearrange("(l f) -> l f", l=1).partition_broadcast(P)
                                   .rearrange("q l f -> q (l f)")).then_inc(gain_f_in, 16)
                with pool.Fori(0, P // PIECES // 2) as i:
                    steps.enter(i, CRING)
                    gather_starts(q, i)
                    steps.leave(P // PIECES // 2)

        @block.scalar
        def _(act):
            a = nc.scalar

            def hi(g, m, i=0, per=0):
                u = UNIT0[g] + m
                act.wait_ge(raw_landed[m % 2], (u // 2 + 1) * 16 + i * per * 8)
                if u >= 2 or per:
                    act.wait_ge(unit_done, u - 1 + i * per)
                a.activation(w_hi[:, m % 2, :, :], raw[:, m % 2, :, :], ACT.Copy).then_inc(hi_ready, 1)

            def group(g):
                for m in range(units_of(g)):
                    hi(g, m)

            act.wait_ge(x_in[1], 16)
            a.activation(N1[:, 1, :], X[:, 1, :], ACT.Square, accum_out=stat[:, 0, 1:2]).then_inc(squared, 1)
            act.wait_ge(mean_ready, 1)
            a.activation(stat[:, 2, 0:NT], stat[:, 1, 0:NT], ACT.Sqrt).then_inc(root_ready, 1)
            hi(0, 0)

            def split_hi(name, to, ready):
                half = half_of(name)
                act.wait_ge(scr_ready[half], use_number(name))
                a.activation(to, scr[:, half, :].rearrange("p (k s) -> p k s", k=to.shape[1]),
                             ACT.Copy).then_inc(ready, 1)

            split_hi("h0", hT_hi[:, 0:4, :], h_hi_ready)
            hi(0, 1)
            for n in range(1, 4):
                split_hi(f"h{n}", hT_hi[:, 4 * n:4 * n + 4, :], h_hi_ready)
            act.wait_ge(lb_diff, 1)
            a.activation(lb[:, 0:2, :], lb[:, 2:4, :], ACT.Exp).then_inc(lb_exp, 1)
            act.wait_ge(small_in, 32)
            a.activation(wff_hi[:, :, :], wff[:, :, :], ACT.Copy).then_inc(wff_hi_ready, 1)
            hi(0, 2)
            hi(0, 3)
            for g in range(1, G_HIG):
                group(g)
            hi(G_HIG, 0)
            hi(G_HIG, 1)
            act.wait_ge(hqf_ready, 1)
            a.activation(k_hg, k_hg, ACT.Sigmoid).then_inc(k_sig, 1)
            hi(G_HIG, 2)
            a.activation(q_hg, q_hg, ACT.Silu).then_inc(q_silu, 1)
            hi(G_HIG, 3)
            hi(G_HIG + 1, 0)
            hi(G_HIG + 1, 1)
            act.wait_ge(f_ready, 1)
            a.activation(b_tile, level[0], ACT.Ln).then_inc(logf_ready, 1)
            hi(G_HIG + 1, 2)
            hi(G_HIG + 1, 3)
            group(G_HIG + 2)
            group(G_HIG + 3)

            def decay(lv):
                act.wait_ge(diff_ready, lv + 1)
                a.activation(level[lv % 2], level[lv % 2], ACT.Exp).then_inc(decay_ready, 1)

            decay(0)
            for n in range(4):
                g = G_FQK + n
                hi(g, 0)
                hi(g, 1)
                if n == 0:
                    act.wait_ge(hgate_in, 1)
                    a.activation(hg_gate, hg_gate, ACT.Silu).then_inc(hgate_ready, 1)
                decay(2 * n + 1)
                hi(g, 2)
                hi(g, 3)
                if n < 3:
                    decay(2 * n + 2)
            hi(G_FV, 0)
            hi(G_FV, 1)
            hi(G_FV, 2)
            act.wait_ge(ff_in, 1)
            a.activation(ff[:, 1, :], ff[:, 0, :], ACT.Abs).then_inc(ff_abs, 1)
            act.wait_ge(ff_abs, 1)
            a.activation(ff[:, 2, :], ff[:, 1, :], ACT.Exp, scale=-1.0).then_inc(ff_exp, 1)
            act.wait_ge(ff_exp, 1)
            a.activation(ff[:, 1, :], ff[:, 2, :], ACT.Ln, bias=1.0).then_inc(ff_log, 1)
            hi(G_FV, 3)
            group(G_FV + 1)

            def exps(pair):
                for n in range(4 * pair, 4 * pair + 4):
                    h, t = n // NT, n % NT
                    lo = (0, P)[t]
                    act.wait_ge(logit_ready, n + 1)
                    p = prob[:, h % 2, lo:lo + (t + 1) * P]
                    a.activation(p, p, ACT.Exp, bias=fstat[:, 0, n:n + 1],
                                 accum_out=fstat[:, 1, n:n + 1]).then_inc(exp_ready, 1)

            def gate_a(n):
                act.wait_ge(group_done, G_GA + n + 1)
                a.activation(T1[:, n * 2 * GW:(n + 1) * 2 * GW], acc[:, n % 2, :], ACT.Sigmoid).then_inc(ga_ready, 1)
                act.wait_ge(ga_ready, n + 1)
                act.sem_inc(acc_free[n % 2], 1)

            for n in range(4):
                hi(G_GA + n, 0)
                hi(G_GA + n, 1)
                exps(n)
                if n:
                    gate_a(n - 1)
                hi(G_GA + n, 2)
                hi(G_GA + n, 3)

            def hi_ya(n):
                act.wait_ge(ya_in, n + 1)
                a.activation(ya_hi[:, 4 * n:4 * n + 4, :], yaT[:, 4 * n:4 * n + 4, :], ACT.Copy
                             ).then_inc(ya_hi_ready, 1)

            hi_ya(0)
            hi(G_AUP, 0)
            hi_ya(1)
            hi(G_AUP, 1)
            gate_a(3)
            for n in range(1, 4):
                group(G_AUP + n)
                if n == 2:
                    act.wait_ge(mean_ready, 2)
                    a.activation(stat[:, 2, :], stat[:, 1, :], ACT.Sqrt).then_inc(root_ready, 1)
            hi(G_GB, 0)
            hi(G_GB, 1)
            hi(G_GB, 2)
            for n, t in enumerate((1, 0)):
                split_hi(f"ob{t}", ob_hi[:, :, t * P:(t + 1) * P], ob_hi_ready)
            hi(G_GB, 3)
            for n in range(4):
                if n:
                    group(G_GB + 2 * n)
                group(G_GB + 2 * n + 1)
                act.wait_ge(group_done, G_GB + 2 * n + 1)
                act.wait_ge(gb_used, 1 + n)
                a.activation(T2[:, 0:2 * GW], acc[:, 0, :], ACT.Sigmoid).then_inc(gb_ready, 1)
                act.wait_ge(gb_ready, n + 1)
                act.sem_inc(acc_free[0], 1)

            def hi_merged(n):
                act.wait_ge(gb_used, 2 + n)
                a.activation(hT_hi[:, 4 * n:4 * n + 4, :], merged[:, 4 * n:4 * n + 4, :], ACT.Copy
                             ).then_inc(merged_hi, 1)

            hi_merged(0)
            hi_merged(1)
            hi(G_WO, 0)
            hi_merged(2)
            hi(G_WO, 1)
            hi_merged(3)
            hi(G_WO, 2)
            hi(G_WO, 3)

            def square_x(n):
                act.wait_ge(normed, 4 + n + 1)
                for t in range(NT):
                    done = 1 + NT * n + t
                    act.wait_ge(squared, done)
                    a.activation(squares[:, done % 4, :], X[:, t, n * GW:(n + 1) * GW], ACT.Square,
                                 accum_out=stat[:, 5, 4 * t + n:4 * t + n + 1]).then_inc(squared, 1)

            for n in range(4):
                g = G_WO + n + 1
                hi(g, 0)
                hi(g, 1)
                hi(g, 2)
                square_x(n)
                if n < 3:
                    hi(g, 3)
                split_hi(f"h2{n}", h2T_hi[:, 4 * n:4 * n + 4, :], h_hi_ready)
            hi(G_WQ, 3)
            act.wait_ge(mean_ready, 3)
            a.activation(stat[:, 2, 0:NT], stat[:, 1, 0:NT], ACT.Sqrt).then_inc(root_ready, 1)
            hi(G_WQ + 1, 0)
            hi(G_WQ + 1, 1)
            act.wait_ge(r_ready, 1)
            for t in range(NT):
                a.activation(N1[:, t, :], N1[:, t, :], ACT.Copy, scale=stat[:, 3, t:t + 1]).then_inc(h2_ready, 1)
            hi(G_WQ + 1, 2)
            hi(G_WQ + 1, 3)
            with act.Fori(0, 2) as i:
                for m in range(4):
                    hi(G_WQ + 2, m, i, 4)

            def scatter_out(t, n, done, token):
                act.wait_ge(hot_used, 2 + done + 1)
                src = acc[:, n % 2, 0:SC * P].rearrange("p (s a) -> p s a", a=P)
                if t:
                    a.activation(weight_of1[:, :, ds(token, SC)].rearrange("p a s -> p s a"), src, ACT.Copy
                                 ).then_inc(scattered, 1)
                    return
                for q in range(PIECES):
                    w = P // PIECES
                    to = weight_of[t][q][:, :, ds(token, SC)].rearrange("p a s -> p s a")
                    last = a.activation(to, src[:, :, q * w:(q + 1) * w], ACT.Copy)
                last.then_inc(scattered, 1)

            def hot_first(t, side, n, made):
                act.wait_ge(hot_used, P // SC - 1 + n if t else 1 + n)
                to = (hot_a, hot_a1)[t]
                for c in range(SC):
                    last = a.activation(to[:, side, c, :], iota_p, ACT.Abs, scale=-1.0,
                                        bias=ijT[:, t, 0, ds(n * SC + c, 1)])
                last.then_inc(a_dist, 1)
                act.wait_ge(a_dist, 1 + made)
                a.activation(to[:, side, :, :], to[:, side, :, :], ACT.Relu, scale=-1.0,
                             bias=1.0).then_inc(a_ready[2 * t], 1)

            for t in range(NT):
                act.wait_ge(shifted, t + 1)
                a.activation(gate[:, :], gate[:, :], ACT.Exp).then_inc(gate_exp, 1)
                act.wait_ge(tanh_in, t + 1)
                a.activation(hid[:, 1, :], hid[:, 1, :], ACT.Tanh).then_inc(tanh_ready, 1)
                if t == 0:
                    act.wait_ge(ij_ready, 1)
                    with act.Fori(0, P // SC // 4) as i:
                        for k in range(4):
                            n = 4 * i + k
                            hot_first(0, k % 2, n, n)
                            scatter_out(0, k, n, n * SC)
            hot_first(1, 1, 1, P // SC)

            def four_batches(i, last=False):
                for k in range(4):
                    n = 4 * i + k
                    if k == 0:
                        hot_first(1, 3, n + 3, P // SC + 1 + 2 * i)
                    if k == 2 and not last:
                        hot_first(1, 1, n + 3, P // SC + 2 + 2 * i)
                    scatter_out(1, k % 2, P // SC + n, n * SC)

            with act.Fori(0, P // SC // 4 - 1) as i:
                four_batches(i)
            four_batches(P // SC // 4 - 1, True)
            act.wait_ge(scattered, 2 + NT * P // SC)

            def v_high(q, i, first=False):
                for e in range(2):
                    block_ = P // PIECES * q + 2 * i + e
                    if not first:
                        act.wait_ge(v_used, 2 * block_ - 2)
                    for t in range(NT):
                        last = a.activation(e_hi[:, e, t, :], weights_of_block(t, q, 2 * i + e), ACT.Copy)
                    last.then_inc(e_hi_ready, 1)
                    for c in range(2):
                        j = 2 * e + c
                        act.wait_ge(v_landed[j], (P // PIECES // 2 * q + i + 1) * 16)
                        if not first:
                            act.wait_ge(v_used, 2 * block_ + c - 3)
                        a.activation(v_hi[:, j, :], v_raw[e][:, c, :], ACT.Copy).then_inc(v_hi_ready, 1)

            v_loops(act, v_high)
            junk = weight_of[1][0][:, :, :].rearrange("p a s -> p (a s)")[:, 0:D]
            for n in range(NT):
                act.wait_ge(y_summed, n + 1)
                a.activation(junk, X[:, n, :], ACT.Square, accum_out=stat[:, 0, n:n + 1]).then_inc(squared, 1)
                act.wait_ge(squared, 1 + 4 * NT + n + 1)
            act.wait_ge(mean_ready, 4)
            a.activation(stat[:, 2, 0:NT], stat[:, 1, 0:NT], ACT.Sqrt).then_inc(root_ready, 1)

        @block.vector
        def _(dve):
            v = nc.vector
            steps = Chain(dve, dve_step)
            link = steps.link
            for free in (*acc_free, *row_used, gb_used, *start_used):
                dve.sem_inc(free, 1)
            for free in (hot_used, scattered):
                dve.sem_inc(free, 2)

            def lo(g, m):
                dve.wait_ge(hi_ready, UNIT0[g] + m + 1)
                v.tensor_tensor(w_lo[:, m % 2, :, :], raw[:, m % 2, :, :], w_hi[:, m % 2, :, :].bitcast(fp32),
                                ALU.subtract).then_inc(lo_ready, 1)

            def scratch(name):
                dve.wait_ge(scr_ready[half_of(name)], use_number(name))
                return half_of(name)

            def inverse_root(n, width, count):
                m, root, r, s = (stat[:, k, 0:n] for k in (1, 2, 3, 4))
                v.tensor_scalar(m, stat[:, 0, 0:n], 1.0 / width, EPS, ALU.mult, ALU.add).then_inc(mean_ready, 1)
                dve.wait_ge(root_ready, count)
                link(v.reciprocal(r, root))
                link(v.tensor_tensor(s, r, r, ALU.mult))
                link(v.tensor_tensor(s, s, m, ALU.mult))
                link(v.tensor_scalar(s, s, -0.5, 1.5, ALU.mult, ALU.add))
                link(v.tensor_tensor(r, r, s, ALU.mult))

            def lo_h(n, second=False):
                half = scratch(f"h2{n}" if second else f"h{n}")
                done, to_hi, to_lo = (4 + n + 1, h2T_hi, h2T_lo) if second else (n + 1, hT_hi, hT_lo)
                dve.wait_ge(h_hi_ready, done)
                k = slice(4 * n, 4 * n + 4)
                v.tensor_tensor(to_lo[:, k, :], scr[:, half, :].rearrange("p (k s) -> p k s", k=4),
                                to_hi[:, k, :].bitcast(fp32), ALU.subtract).then_inc(h_ready, 1)
                dve.wait_ge(h_ready, done)
                dve.sem_inc(scr_free[half], 1)

            half = scratch("vectors")
            link(v.tensor_copy(vecT[:, :], scr[:, half, 0:16]))
            dve.sem_inc(scr_free[half], 1)
            dve.wait_ge(x_in[0], 16)
            link(v.scalar_tensor_tensor(out=N1[:, 0, :], in0=X[:, 0, :], scalar=1.0, in1=X[:, 0, :],
                                        op0=ALU.mult, op1=ALU.mult, accum_out=stat[:, 0, 0:1]))
            dve.wait_ge(squared, 1)
            inverse_root(NT, D, 1)
            dve.wait_ge(x_in[1], 16)
            dve.wait_ge(gain1_in, 16)
            for part in range(2):
                cols = slice(part * D // 2, (part + 1) * D // 2)
                for t in range(NT):
                    v.scalar_tensor_tensor(out=N1[:, t, cols], in0=X[:, t, cols], scalar=stat[:, 3, t:t + 1],
                                           in1=gain1[:, cols], op0=ALU.mult, op1=ALU.mult).then_inc(normed, 1)
            lo(0, 0)
            lo_h(0)
            lo(0, 1)
            for n in range(1, 4):
                lo_h(n)
            l0, l1 = vecT[:, 0:8], vecT[:, 8:16]
            link(v.tensor_tensor(lb[:, 0, :], l0, l1, ALU.max))
            v.tensor_tensor(lb[:, 2, :], l0, lb[:, 0, :], ALU.subtract)
            v.tensor_tensor(lb[:, 3, :], l1, lb[:, 0, :], ALU.subtract).then_inc(lb_diff, 1)
            dve.wait_ge(lb_exp, 1)
            link(v.tensor_tensor(lb[:, 2, :], lb[:, 0, :], lb[:, 1, :], ALU.add))
            link(v.reciprocal(lb[:, 2, :], lb[:, 2, :]))
            link(v.tensor_tensor(lb[:, 0, :], lb[:, 0, :], lb[:, 2, :], ALU.mult))
            link(v.tensor_scalar(lb[:, 1, :], lb[:, 0, :], -1.0, 1.0, ALU.mult, ALU.add))

            def copy_group(g, to):
                dve.wait_ge(group_done, g + 1)
                src = acc[:, g % 2, :]
                if len(to.shape) == 3:
                    src = src.rearrange("p (t n) -> p t n", t=NT)
                v.tensor_copy(to, src).then_inc(acc_free[g % 2], 1)

            def copied(g):
                dve.wait_ge(acc_free[g % 2], g // 2 + 2)
                dve.wait_ge(acc_free[1 - g % 2], (g + 1) // 2 + 1)

            def hqf(n):
                copy_group(G_HQF + n, Z1[:, n * 2 * GW:(n + 1) * 2 * GW])

            def hig(n):
                copy_group(G_HIG + n, N1[:, :, n * GW:(n + 1) * GW])

            def fqk(n):
                copy_group(G_FQK + n, Z2[:, n * 2 * GW:(n + 1) * 2 * GW])

            lo(0, 2)
            lo(0, 3)
            dve.wait_ge(wff_hi_ready, 1)
            v.tensor_tensor(wff_lo[:, :, :], wff[:, :, :], wff_hi[:, :, :].bitcast(fp32),
                            ALU.subtract).then_inc(wff_ready, 1)
            for n in range(1, 4):
                for m in range(4):
                    lo(G_HQF + n, m)
                    if m == 1:
                        hqf(n - 1)

            g = G_HIG
            reset = level[1]
            lo(g, 0)
            lo(g, 1)
            hqf(3)
            copied(G_HQF + 3)
            dve.sem_inc(hqf_ready, 1)
            link(v.memset(reset, 1.0))
            v.memset(reset.rearrange("p (c s) -> p c s", s=CH)[:, :, 0:1], 0.0).then_inc(reset_ready, 1)
            lo(g, 2)
            lo(g, 3)
            dve.wait_ge(k_sig, 1)
            f = level[0]
            for h in range(H):
                last = v.tensor_scalar(f[:, h * S:(h + 1) * S], k_hg[:, h * S:(h + 1) * S], lb[:, 1, h:h + 1],
                                       lb[:, 0, h:h + 1], ALU.mult, ALU.add)
            last.then_inc(f_ready, 1)
            lo(g + 1, 0)
            lo(g + 1, 1)
            hig(0)
            dve.wait_ge(f_ready, 1)
            v.tensor_scalar(k_hg, f, -1.0, 1.0, ALU.mult, ALU.add).then_inc(k_ready, 1)
            lo(g + 1, 2)
            dve.wait_ge(logf_ready, 1)
            dve.wait_ge(reset_ready, 1)
            link(v.tensor_tensor_scan(b_chunk, reset, b_tile, 0.0, ALU.mult, ALU.add))
            lo(g + 1, 3)
            bc = b_chunk.rearrange("p (u c s) -> p u c s", c=2, s=CH)
            bt = b_tile.rearrange("p (u c s) -> p u c s", c=2, s=CH)
            v.tensor_copy(bt[:, :, 0, :], bc[:, :, 0, :])
            v.tensor_tensor(bt[:, :, 1, :], bc[:, :, 1, :], bc[:, :, 0, CH - 1:CH].to_broadcast([P, 2 * H, CH]),
                            ALU.add).then_inc(b_ready, 1)
            lo(g + 2, 0)
            lo(g + 2, 1)
            hig(1)
            link(v.memset(A2[:, :], 0.0))
            lo(g + 2, 2)
            lo(g + 2, 3)
            dve.wait_ge(k_ready, 1)
            dve.wait_ge(q_silu, 1)

            def times(lv):
                dve.wait_ge(decay_ready, lv + 1)
                size = 2 << lv
                (e_lo, e_up), (k_lo, _), (_, q_up) = (halves(b, size) for b in (level[lv % 2], k_hg, q_hg))
                v.tensor_tensor(e_lo, e_lo, k_lo, ALU.mult)
                v.tensor_tensor(e_up, e_up, q_up, ALU.mult).then_inc(level_ready, 1)

            def place(lv):
                if lv == LEVELS - 1:
                    half = scratch("across")
                    v.tensor_copy(attn_across, scr[:, half, :].rearrange("p (h s) -> p h s", s=P)
                                  ).then_inc(scr_free[half], 1)
                    return
                k, stem = (MASKED, "diagonal") if lv == LEVELS else (lv, f"level{lv}")
                if lv:
                    dve.wait_ge(scr_free[1], use_number(f"level{min(lv, MASKED) - 1}b"))
                for side in range(2):
                    half = scratch(f"{stem}{'ab'[side]}")
                    to = attn[:, side * H:(side + 1) * H, :]
                    mask = masks[:, k:k + 1, :].to_broadcast([P, H, P]).bitcast(u32)
                    v.copy_predicated(to, mask, scr[:, half, :].rearrange("p (u s) -> p u s", s=P)
                                      ).then_inc(scr_free[half], 1)

            lo(g + 3, 0)
            lo(g + 3, 1)
            hig(2)
            lo(g + 3, 2)
            lo(g + 3, 3)
            dve.wait_ge(consts_ready, 2)
            for n in range(4):
                g = G_FQK + n
                lo(g, 0)
                if n:
                    place(2 * n - 1)
                lo(g, 1)
                if n == 0:
                    hig(3)
                    copied(G_HIG + 3)
                    dve.sem_inc(hgate_in, 1)
                else:
                    fqk(n - 1)
                times(2 * n)
                lo(g, 2)
                lo(g, 3)
                place(2 * n)
                times(2 * n + 1)

            lo(G_FV, 0)
            place(LEVELS - 1)
            lo(G_FV, 1)
            fqk(3)
            copied(G_FQK + 3)
            v.tensor_scalar(Z2[:, 0:8 * S], Z2[:, 0:8 * S], SCALE, None, ALU.mult).then_inc(q_scaled, 1)
            half = scratch("forget")
            v.tensor_scalar(ff[:, 0, :], scr[0:H, half, 0:S], ff_bias[:, 0:1], None, ALU.add).then_inc(ff_in, 1)
            dve.wait_ge(ff_in, 1)
            dve.sem_inc(scr_free[half], 1)
            lo(G_FV, 2)
            lo(G_FV, 3)
            dve.wait_ge(ff_log, 1)
            link(v.scalar_tensor_tensor(out=ff[:, 2, :], in0=ff[:, 0, :], scalar=0.0, in1=ff[:, 1, :],
                                        op0=ALU.min, op1=ALU.subtract))
            link(v.memset(ff[:, 0, :], 1.0))
            link(v.tensor_tensor_scan(ff[:, 1, :], ff[:, 0, :], ff[:, 2, :], 0.0, ALU.mult, ALU.add))
            v.tensor_scalar(neg_c, ff[:, 1, :], -1.0, None, ALU.mult).then_inc(c_ready, 1)
            lo(G_FV + 1, 0)
            place(LEVELS)
            dve.wait_ge(scr_free[0], use_number("diagonala"))
            dve.wait_ge(scr_free[1], use_number("diagonalb"))
            dve.sem_inc(attn_ready, 1)
            lo(G_FV + 1, 1)
            copy_group(G_FV, fv[:, :, 0:GW])
            half = scratch("cumulative")
            v.tensor_copy(c_tok[:, :, :], scr[:, half, 0:NT * H].rearrange("p (t h) -> p t h", t=NT)
                          ).then_inc(scr_free[half], 1)
            dve.wait_ge(scr_free[half], use_number("cumulative"))
            dve.sem_inc(gain_free, 1)
            lo(G_FV + 1, 2)

            def copy_o(t):
                half = scratch(f"o{t}")
                v.tensor_copy(o_hg[:, t, :], scr[:, half, :]).then_inc(o_ready, 1)
                dve.wait_ge(o_ready, 2 - t)
                dve.sem_inc(scr_free[half], 1)

            copy_o(1)
            lo(G_FV + 1, 3)

            def shift(pair):
                half = scratch(f"qk{pair}")
                if pair:
                    dve.wait_ge(scr_ready[1], use_number(f"pT{pair - 1}"))
                for b in range(2):
                    h = 2 * pair + b
                    src = scr[:, half, b * GW:b * GW + 384]
                    for t in range(NT):
                        n, at0, width = 2 * h + t, (0, P)[t], (t + 1) * P
                        link(v.scalar_tensor_tensor(out=prob[:, b, at0:at0 + width], in0=src[:, at0:at0 + width],
                                                    scalar=c_tok[:, t, h:h + 1], in1=fox_mask[:, S - width:S],
                                                    op0=ALU.add, op1=ALU.add))
                        v.tensor_reduce(fstat[:, 0, n:n + 1], prob[:, b, at0:at0 + width], AX.X, ALU.max,
                                        negate=True).then_inc(logit_ready, 1)
                dve.sem_inc(scr_free[half], 1)

            def normalize(pair):
                for b in range(2):
                    h = 2 * pair + b
                    dve.wait_ge(exp_ready, 2 * h + 2)
                    link(v.reciprocal(fstat[:, 2, 2 * h:2 * h + 2], fstat[:, 1, 2 * h:2 * h + 2]))
                    for t in range(NT):
                        n, at0, width = 2 * h + t, (0, P)[t], (t + 1) * P
                        last = v.tensor_scalar(prob[:, b, at0:at0 + width], prob[:, b, at0:at0 + width],
                                               fstat[:, 2, n:n + 1], None, ALU.mult)
                    last.then_inc(p_ready, 1)

            def copy_pT(pair):
                half = scratch(f"pT{pair}")
                v.tensor_copy(probT, scr[:, half, :].rearrange("p (b s) -> p b s", b=2)[:, :, 0:384]
                              ).then_inc(pT_ready, 1)
                dve.wait_ge(pT_ready, pair + 1)
                dve.sem_inc(scr_free[half], 1)

            def copy_ya(pair):
                half = scratch(f"pv{pair}")
                v.tensor_copy(yaT[:, 2 * pair:2 * pair + 2, :],
                              scr[:, half, :].rearrange("p (b s) -> p b s", b=2)[:, :, 0:S]
                              ).then_inc(scr_free[half], 1)
                if pair % 2:
                    dve.wait_ge(scr_free[half], use_number(f"pv{pair}"))
                    dve.sem_inc(ya_in, 1)

            def lo_ya(n):
                dve.wait_ge(ya_hi_ready, n + 1)
                k = slice(4 * n, 4 * n + 4)
                v.tensor_tensor(ya_lo[:, k, :], yaT[:, k, :], ya_hi[:, k, :].bitcast(fp32),
                                ALU.subtract).then_inc(ya_split, 1)

            for n in range(4):
                g = G_GA + n
                lo(g, 0)
                if n == 0:
                    copy_group(G_FV + 1, fv[:, :, GW:2 * GW])
                    copied(G_FV + 1)
                    dve.sem_inc(fv_ready, 1)
                lo(g, 1)
                shift(n)
                if n == 0:
                    copy_o(0)
                else:
                    copy_pT(n - 1)
                lo(g, 2)
                normalize(n)
                if n == 3:
                    copy_ya(2)
                lo(g, 3)
                if n in (1, 2):
                    copy_ya(n - 1)
            copy_pT(3)
            lo(G_AUP, 0)
            copy_ya(3)
            lo_ya(0)
            lo_ya(1)
            lo(G_AUP, 1)

            def times_ya(n):
                dve.wait_ge(group_done, G_AUP + n + 1)
                dve.wait_ge(ga_ready, n + 1)
                part = T1[:, n * 2 * GW:(n + 1) * 2 * GW]
                v.tensor_tensor(part, part, acc[:, n % 2, :], ALU.mult).then_inc(acc_free[n % 2], 1)

            o_flat, sq = Z1[:, 0:8 * S], T2[:, HW:3 * HW]
            o_heads = o_flat.rearrange("p (u n) -> p u n", n=P)
            lo(G_AUP + 1, 0)
            link(v.tensor_tensor(sq, o_flat, o_flat, ALU.mult))
            lo(G_AUP + 1, 1)
            times_ya(0)
            link(v.tensor_reduce(stat[:, 0, :], sq.rearrange("p (u n) -> p u n", n=P), AX.X, ALU.add))
            lo(G_AUP + 2, 0)
            lo(G_AUP + 2, 1)
            times_ya(1)
            inverse_root(16, P, 2)
            link(v.tensor_tensor(o_heads, o_heads, stat[:, 3, :].unsqueeze(2).to_broadcast([P, 16, P]), ALU.mult))
            lo(G_AUP + 3, 0)
            dve.wait_ge(hg_gain_in, 16)
            link(v.tensor_tensor(o_hg, o_hg, hg_gain.unsqueeze(1).to_broadcast([P, NT, HW]), ALU.mult))
            lo(G_AUP + 3, 1)
            times_ya(2)
            dve.wait_ge(hgate_ready, 1)
            v.tensor_tensor(o_hg, o_hg, hg_gate, ALU.mult).then_inc(ob_ready, 1)
            lo(G_GB, 0)
            lo(G_GB, 1)
            times_ya(3)
            lo(G_GB, 2)
            for n, t in enumerate((1, 0)):
                half = scratch(f"ob{t}")
                dve.wait_ge(ob_hi_ready, n + 1)
                cols = slice(t * P, (t + 1) * P)
                v.tensor_tensor(ob_lo[:, :, cols], scr[:, half, :].rearrange("p (h s) -> p h s", h=H),
                                ob_hi[:, :, cols].bitcast(fp32), ALU.subtract).then_inc(ob_split, 1)
                dve.wait_ge(ob_split, n + 1)
                dve.sem_inc(scr_free[half], 1)
            lo(G_GB, 3)
            gated = T2[:, 2 * GW:4 * GW]

            def add_yb(n):
                dve.wait_ge(group_done, G_GB + 2 * n + 2)
                dve.wait_ge(gb_ready, n + 1)
                if n:
                    dve.wait_ge(gb_used, 1 + n)
                part = T1[:, n * 2 * GW:(n + 1) * 2 * GW]
                link(v.tensor_tensor(gated, T2[:, 0:2 * GW], acc[:, 1, :], ALU.mult))
                dve.sem_inc(acc_free[1], 1)
                v.tensor_tensor(part, part, gated, ALU.add).then_inc(gb_used, 1)

            for n in range(4):
                if n:
                    for m in range(4):
                        lo(G_GB + 2 * n, m)
                        if m == 1:
                            add_yb(n - 1)
                            if n < 3:
                                half = scratch(f"keys{n - 1}")
                                v.tensor_copy(V1[:, (n - 1) * HW:n * HW], scr[:, half, :]
                                              ).then_inc(scr_free[half], 1)
                lo(G_GB + 2 * n + 1, 0)
                lo(G_GB + 2 * n + 1, 1)

            def lo_merged(n):
                dve.wait_ge(merged_hi, n + 1)
                k = slice(4 * n, 4 * n + 4)
                v.tensor_tensor(hT_lo[:, k, :], merged[:, k, :], hT_hi[:, k, :].bitcast(fp32),
                                ALU.subtract).then_inc(merged_split, 1)

            lo_merged(0)
            lo_merged(1)
            lo(G_WO, 0)
            lo_merged(2)
            lo(G_WO, 1)
            add_yb(3)
            lo_merged(3)
            lo(G_WO, 2)
            lo(G_WO, 3)

            def add_residual(n):
                dve.wait_ge(group_done, G_WO + n + 1)
                cols = slice(n * GW, (n + 1) * GW)
                part = X[:, :, cols]
                link(v.tensor_tensor(part, part, acc[:, n % 2, :].rearrange("p (t n) -> p t n", t=NT), ALU.add))
                dve.sem_inc(acc_free[n % 2], 1)
                dve.wait_ge(gain2_in, 16)
                v.tensor_tensor(N1[:, :, cols], part, gain2[:, cols].unsqueeze(1).to_broadcast([P, NT, GW]),
                                ALU.mult).then_inc(normed, 1)

            for n in range(3):
                g = G_WO + n + 1
                lo(g, 0)
                lo(g, 1)
                add_residual(n)
                lo(g, 2)
                lo(g, 3)
                lo_h(n, True)
            lo(G_WQ, 0)
            lo(G_WQ, 1)
            add_residual(3)
            lo(G_WQ, 2)
            lo_h(3, True)
            lo(G_WQ, 3)
            dve.wait_ge(squared, 1 + 4 * NT)
            link(v.tensor_reduce(stat[:, 0, 0:NT], stat[:, 5, 0:4 * NT].rearrange("p (t n) -> p t n", t=NT),
                                 AX.X, ALU.add))
            inverse_root(NT, D, 3)
            dve.sem_inc(r_ready, 1)

            def top16(values, src, indices):
                w = src.shape[1]
                link(v.max(values[:, 0:8], src))
                v.max_index(indices[:, 0:8], values[:, 0:8], src)
                link(v.match_replace(rest[:, 0:w], values[:, 0:8], src, -3.0e38))
                link(v.max(values[:, 8:16], rest[:, 0:w]))
                link(v.max_index(indices[:, 8:16], values[:, 8:16], rest[:, 0:w]))

            def top_keys(t, u):
                top16(topv[:, u, :], scores[:, t, u, :], topi[:, u, :])

            def top_pairs(t, pair):
                us, hs = slice(4 * pair, 4 * pair + 4), slice(2 * pair, 2 * pair + 2)
                link(v.tensor_copy(topf[:, us, :], topi[:, us, :]))
                tv = topv[:, us, :].rearrange("p (h c) k -> p h c k", c=2)
                tf = topf[:, us, :].rearrange("p (h c) k -> p h c k", c=2)
                cands = cand.rearrange("p (h i j) -> p h i j", i=TOPK, j=TOPK)
                link(v.tensor_tensor(cands, tv[:, :, 0, :].unsqueeze(3).to_broadcast([P, 2, TOPK, TOPK]),
                                     tv[:, :, 1, :].unsqueeze(2).to_broadcast([P, 2, TOPK, TOPK]), ALU.add))
                ks = slice(2 * pair * TOPK, 2 * (pair + 1) * TOPK)
                for h in range(2):
                    kh = slice((2 * pair + h) * TOPK, (2 * pair + h + 1) * TOPK)
                    top16(best[:, t, kh], cand[:, h * S:(h + 1) * S], bpos[:, 0, kh])
                v.tensor_scalar(bpos[:, 1, ks], bpos[:, 0, ks], 4, None, ALU.logical_shift_right)
                link(v.tensor_scalar(bpos[:, 2, ks], bpos[:, 0, ks], TOPK - 1, None, ALU.bitwise_and))
                link(v.tensor_copy(bposf[:, 0:2, ks], bpos[:, 1:3, ks]))
                hots = hot.rearrange("p (m i) -> p m i", i=TOPK)
                hot4 = hot.rearrange("p (h m i) -> p h m i", m=TOPK, i=TOPK)
                for c in range(2):
                    link(v.tensor_tensor(hots, bposf[:, c, ks].unsqueeze(2).to_broadcast([P, 2 * TOPK, TOPK]),
                                         iota16[:, :].unsqueeze(1).to_broadcast([P, 2 * TOPK, TOPK]), ALU.is_equal))
                    link(v.tensor_tensor(hot4, hot4, tf[:, :, c, :].unsqueeze(2).to_broadcast([P, 2, TOPK, TOPK]),
                                         ALU.mult))
                    link(v.tensor_reduce(ij[:, t, c, ks], hots, AX.X, ALU.add))
                link(v.scalar_tensor_tensor(out=bposf[:, 2, ks], in0=ij[:, t, 0, ks], scalar=float(P),
                                            in1=ij[:, t, 1, ks], op0=ALU.mult, op1=ALU.add))
                v.tensor_copy(expert[:, t, ks], bposf[:, 2, ks]).then_inc(expert_ready, 1)

            def copy_q(n):
                copy_group(G_WQ + n, T2[:, D + n % 2 * 2 * GW:D + (n % 2 + 1) * 2 * GW])
                copied(G_WQ + n)
                dve.sem_inc(q_copied, 1)

            def copy_scores(n):
                half = scratch(f"score{n}")
                for t in range(NT):
                    link(v.tensor_scalar(scores[:, t, 4 * n:4 * n + 4, :],
                                         scr[:, half, t * GW:(t + 1) * GW].rearrange("p (u n) -> p u n", n=P),
                                         stat[:, 3, t:t + 1], None, ALU.mult))
                dve.sem_inc(scr_free[half], 1)

            def select(t, pair):
                for u in range(4 * pair, 4 * pair + 4):
                    top_keys(t, u)
                top_pairs(t, pair)

            for n in range(1, 4):
                lo(G_WQ + n, 0)
                lo(G_WQ + n, 1)
                copy_q(n - 1)
                lo(G_WQ + n, 2)
                copy_scores(n - 1)
                if n < 3:
                    top_keys(0, 2 * n - 2)
                lo(G_WQ + n, 3)
                if n < 3:
                    top_keys(0, 2 * n - 1)
                else:
                    top_pairs(0, 0)
            copy_q(3)
            copy_scores(3)

            def hot_second(t, side, n):
                dve.wait_ge(hot_used, t * P // SC + 1 + n)
                for c in range(SC):
                    token = ds(n * SC + c, 1)
                    last = v.tensor_scalar(hot_b[:, side, c, :], iota_p, ijT[:, t, 1, token], gateT[:, t, token],
                                           ALU.is_equal, ALU.mult)
                last.then_inc(b_hot_ready, 1)

            def dots(t, first, n, between=None):
                with dve.Fori(0, n) as i:
                    for j in range(SLOTS):
                        if between is not None and j % 2 == 0:
                            between(i, j // 2)
                        dve.wait_ge(row_landed[j], (t * ROUNDS + first + 1 + i) * 16)
                        v.scalar_tensor_tensor(out=slots[:, j, :], in0=slots[:, j, :], scalar=1.0, in1=N1[:, t, :],
                                               op0=ALU.mult, op1=ALU.mult,
                                               accum_out=hid[:, 0, ds((i + first) * SLOTS + j, 1)]
                                               ).then_inc(row_used[j], 1)

            def weights(t):
                for j in range(SLOTS):
                    dve.wait_ge(row_used[j], 1 + (t + 1) * ROUNDS)
                g3 = gate[:, :].rearrange("p (h k) -> p h k", h=H)
                b3 = best[:, t, :].rearrange("p (h k) -> p h k", h=H)
                v.tensor_tensor(g3, b3, b3[:, :, 0:1].to_broadcast([P, H, TOPK]), ALU.subtract).then_inc(shifted, 1)
                dve.wait_ge(gate_exp, t + 1)
                link(v.tensor_reduce(gsum[:, 0, :], g3, AX.X, ALU.add))
                link(v.reciprocal(gsum[:, 1, :], gsum[:, 0, :]))
                link(v.tensor_tensor(g3, g3, gsum[:, 1, :].unsqueeze(2).to_broadcast([P, H, TOPK]), ALU.mult))
                z, w = hid[:, 0, :], hid[:, 1, :]
                link(v.tensor_tensor(w, z, z, ALU.mult))
                link(v.tensor_scalar(w, w, TANH_A * TANH_B, TANH_A, ALU.mult, ALU.add))
                v.tensor_tensor(w, w, z, ALU.mult).then_inc(tanh_in, 1)
                dve.wait_ge(tanh_ready, t + 1)
                link(v.scalar_tensor_tensor(out=hid[:, 2, :], in0=w, scalar=1.0, in1=z, op0=ALU.add, op1=ALU.mult))
                v.scalar_tensor_tensor(out=weight[:, t, :], in0=hid[:, 2, :], scalar=0.5, in1=gate[:, :],
                                       op0=ALU.mult, op1=ALU.mult).then_inc(weight_ready, 1)
                dve.wait_ge(weight_ready, t + 1)

            def copy_ij(t):
                dve.wait_ge(ij_landed, t + 1)
                v.tensor_copy(ijT[:, t, :, :], scr[:, 0, 0:2 * P].rearrange("p (c s) -> p c s", c=2)
                              ).then_inc(ij_ready, 1)
                dve.wait_ge(ij_ready, t + 1)

            def copy_gate(t):
                dve.wait_ge(gate_landed, t + 1)
                v.tensor_copy(gateT[:, t, :], scr[:, 1, 0:P]).then_inc(gateT_ready, 1)
                dve.wait_ge(gateT_ready, t + 1)

            dve.wait_ge(h2_ready, NT)
            for pair in range(4):
                dots(0, pair * ROUNDS // 4, ROUNDS // 8)
                select(*((0, pair + 1) if pair < 3 else (1, 0)))
                dots(0, (2 * pair + 1) * ROUNDS // 8, ROUNDS // 8)
            weights(0)
            dve.sem_inc(h_used, 1)
            dots(1, 0, 2)
            copy_ij(0)
            copy_gate(0)
            select(1, 1)
            dots(1, 2, 3)
            select(1, 2)
            dots(1, 5, 2)
            select(1, 3)
            dots(1, 7, 1)
            copy_ij(1)
            dots(1, 8, 8, lambda i, k: hot_second(0, k % 2, 4 * i + k))
            weights(1)
            assert D // CW == 4
            link(v.tensor_scalar(expert[:, :, :], expert[:, :, :], 2, None, ALU.logical_shift_left))
            dve.sem_inc(h_used, 1)
            copy_gate(1)
            with dve.Fori(0, P // SC // 2) as i:
                for k in range(2):
                    hot_second(1, k, 2 * i + k)

            def v_low(q, i, first=False):
                for e in range(2):
                    block_ = P // PIECES * q + 2 * i + e
                    dve.wait_ge(e_hi_ready, block_ + 1)
                    for t in range(NT):
                        last = v.tensor_tensor(e_lo[:, e, t, :], weights_of_block(t, q, 2 * i + e),
                                               e_hi[:, e, t, :].bitcast(fp32), ALU.subtract)
                    last.then_inc(e_ready, 1)
                    for c in range(2):
                        dve.wait_ge(v_hi_ready, 2 * block_ + c + 1)
                        if not first or e:
                            dve.wait_ge(v_used, 2 * block_ + c - 1)
                        v.tensor_tensor(v_lo[:, c, :], v_raw[e][:, c, :], v_hi[:, 2 * e + c, :].bitcast(fp32),
                                        ALU.subtract).then_inc(v_ready, 1)
                        j = 2 * e + c
                        dve.wait_ge(start_landed[j], (P // PIECES // 2 * q + i + 1) * 16)
                        x_start = X[:, q // 2, 0:CW]
                        k = q % 2 * (NSEL // 2) + CRING * i + j
                        dve.wait_ge(start_used[j - 1], int(j > 0) + 1 + P // PIECES // 2 * q + i)
                        v.scalar_tensor_tensor(out=x_start, in0=starts[j // 2][:, j % 2, :],
                                               scalar=weight[:, q // 2, ds(k, 1)], in1=x_start,
                                               op0=ALU.mult, op1=ALU.add).then_inc(start_used[j], 1)

            v_loops(dve, v_low)
            y = [acc[:, :, :].rearrange("p a n -> p (a n)"), scr[:, :, :].rearrange("p a n -> p (a n)")]
            dve.wait_ge(v_used, 2 * P)
            for t in range(NT):
                v.tensor_tensor(X[:, t, CW:D], y[t][:, 0:DW], X[:, t, CW:D], ALU.add).then_inc(y_summed, 1)
            dve.wait_ge(squared, 1 + 4 * NT + NT)
            inverse_root(NT, D, 4)
            dve.wait_ge(gain_f_in, 16)
            for n in range(2 * NT):
                t, cols = n // 2, slice(n % 2 * D // 2, (n % 2 + 1) * D // 2)
                v.scalar_tensor_tensor(out=X[:, t, cols], in0=X[:, t, cols], scalar=stat[:, 3, t:t + 1],
                                       in1=gain_f[:, cols], op0=ALU.mult, op1=ALU.mult).then_inc(y_ready, 1)

        @block.tensor
        def _(pe):
            t_ = nc.tensor

            def enter(name):
                if use_number(name) > 1:
                    pe.wait_ge(scr_free[half_of(name)], use_number(name) - 1)
                return half_of(name)

            def done(name, last):
                last.then_inc(scr_ready[half_of(name)], 1)

            def transposed_unit(g, m, src, i=0, per=0):
                pe.wait_ge(lo_ready, UNIT0[g] + m + 1 + i * per)
                if m == 0:
                    pe.wait_ge(acc_free[g % 2], 1 + g // 2 + i)
                hi_, lo_ = src
                end = m == units_of(g) - 1
                for k in range(UK):
                    kk = m * UK + k
                    for f in range(FB):
                        to, cols = acc[:, g % 2, f * S:(f + 1) * S], slice(f * P, (f + 1) * P)
                        wh, wl = w_hi[:, m % 2, k, cols], w_lo[:, m % 2, k, cols]
                        last_k = end and k == UK - 1
                        t_.matmul(to, wh, hi_[:, kk, :], start=kk == 0 and f % 2 == 0, stop=False,
                                  skip_group_check=True)
                        t_.matmul(to, wh, lo_[:, kk, :], start=False, stop=False, skip_group_check=True)
                        last = t_.matmul(to, wl, hi_[:, kk, :], start=False, stop=last_k, skip_group_check=True)
                last.then_inc(unit_done, 1)

            def natural_unit(g, m, src, i=0, per=0):
                pe.wait_ge(lo_ready, UNIT0[g] + m + 1 + i * per)
                if m == 0:
                    pe.wait_ge(acc_free[g % 2], 1 + g // 2 + i)
                hi_, lo_ = src
                end = m == units_of(g) - 1
                for k in range(UK):
                    kk = m * UK + k
                    for t in range(NT):
                        to, cols = acc[:, g % 2, t * GW:(t + 1) * GW], slice(t * P, (t + 1) * P)
                        t_.matmul(to, hi_[:, kk, cols], w_hi[:, m % 2, k, :], start=kk == 0, stop=False)
                        t_.matmul(to, hi_[:, kk, cols], w_lo[:, m % 2, k, :], start=False, stop=False)
                        last = t_.matmul(to, lo_[:, kk, cols], w_hi[:, m % 2, k, :], start=False,
                                         stop=end and k == UK - 1)
                last.then_inc(unit_done, 1)

            def finish(g, i=0, per=0):
                pe.wait_ge(unit_done, UNIT0[g + 1] + i * per)
                pe.sem_inc(group_done, 1)

            def loop_two(g0, unit, src, split=None):
                n = units_of(g0)
                with pe.Fori(0, 2) as i:
                    for g in (g0, g0 + 1):
                        for m in range(n):
                            if split is not None:
                                pe.wait_ge(split, m + 1)
                            unit(g, m, src, i, 2 * n)
                        finish(g, i, 2 * n)

            def transpose_norm(name, n):
                half = enter(name)
                for k in range(4):
                    for t in range(NT):
                        at0 = k * S + t * P
                        last = t_.transpose(scr[:, half, at0:at0 + P],
                                            N1[:, t, (4 * n + k) * P:(4 * n + k + 1) * P], ident[:, :])
                done(name, last)

            hT = (hT_hi, hT_lo)
            pe.wait_ge(consts_ready, 1)
            pe.wait_ge(vec_in, 16)
            half = enter("vectors")
            done("vectors", t_.transpose(scr[:, half, 0:16], vec[:, :], ident[0:16, 0:16]))
            for n in range(4):
                pe.wait_ge(normed, 2 + n // 2 * 2)
                transpose_norm(f"h{n}", n)
            loop_two(G_HQF, transposed_unit, hT, h_ready)
            loop_two(G_HIG, natural_unit, hT)

            def level_products(name, a, b, side, pieces):
                half = enter(name)
                for u in range(H):
                    at_a, at_b = pieces(side * H + u)
                    last = t_.matmul(scr[:, half, u * P:(u + 1) * P], a[:, at_a:at_a + P], b[:, at_b:at_b + P],
                                     start=True, stop=True)
                done(name, last)

            def own(u):
                return u * P, u * P

            for n in range(4):
                g = G_FQK + n
                for m in range(4):
                    transposed_unit(g, m, hT)
                    if m == 3:
                        finish(g)
                    if m % 2:
                        lv = 2 * n + m // 2
                        pe.wait_ge(level_ready, lv + 1)
                        e = level[lv % 2]
                        if lv < MASKED:
                            level_products(f"level{lv}a", e, e, 0, own)
                            level_products(f"level{lv}b", e, e, 1, own)
                        else:
                            level_products("across", e, e, 0, lambda u: (u * S, u * S + P))
            pe.wait_ge(wff_ready, 1)
            half = enter("forget")
            to = scr[0:H, half, 0:S]
            for k in range(KD):
                t_.matmul(to, wff_hi[:, k, :], hT_hi[:, k, :], start=k == 0, stop=False)
                t_.matmul(to, wff_lo[:, k, :], hT_hi[:, k, :], start=False, stop=False)
                last = t_.matmul(to, wff_hi[:, k, :], hT_lo[:, k, :], start=False, stop=k == KD - 1)
            done("forget", last)
            natural_unit(G_FV, 0, hT)
            natural_unit(G_FV, 1, hT)
            natural_unit(G_FV, 2, hT)
            natural_unit(G_FV, 3, hT)
            finish(G_FV)
            level_products("diagonala", k_hg, q_hg, 0, own)
            level_products("diagonalb", k_hg, q_hg, 1, own)
            natural_unit(G_FV + 1, 0, hT)
            natural_unit(G_FV + 1, 1, hT)
            pe.wait_ge(c_ready, 1)
            half = enter("cumulative")
            for t in range(NT):
                last = t_.transpose(scr[:, half, t * H:(t + 1) * H], ff[:, 1, t * P:(t + 1) * P], ident[0:H, 0:H])
            done("cumulative", last)

            def hg_output(t):
                half = enter(f"o{t}")
                for h in range(H):
                    to, cols = scr[:, half, h * P:(h + 1) * P], slice(h * P, (h + 1) * P)
                    if t:
                        t_.matmul(to, attn_across[:, h, :], hg_v[:, 0, cols], start=True, stop=False)
                    last = t_.matmul(to, attn[:, 2 * h + t, :], hg_v[:, t, cols], start=(t == 0), stop=True)
                done(f"o{t}", last)

            pe.wait_ge(attn_ready, 1)
            hg_output(1)
            natural_unit(G_FV + 1, 2, hT)
            natural_unit(G_FV + 1, 3, hT)
            finish(G_FV + 1)

            def logits(pair):
                half = enter(f"qk{pair}")
                for b in range(2):
                    h = 2 * pair + b
                    for t in range(NT):
                        at0, width = b * GW + (0, P)[t], (t + 1) * P
                        to = scr[:, half, at0:at0 + width]
                        t_.matmul(to, fqT[:, h, t * P:(t + 1) * P], fkT[:, h, 0:width], start=True, stop=False)
                        last = t_.matmul(to, ident[0:H, h:h + 1].to_broadcast([H, P]), neg_c[:, 0:width],
                                         start=False, stop=True)
                done(f"qk{pair}", last)

            def transpose_p(pair):
                half = enter(f"pT{pair}")
                for b in range(2):
                    pe.wait_ge(p_ready, 2 * pair + b + 1)
                    for n in range(3):
                        last = t_.transpose(scr[:, half, b * GW + n * P:b * GW + (n + 1) * P],
                                            prob[:, b, n * P:(n + 1) * P], ident[:, :])
                done(f"pT{pair}", last)

            def weighted_v(pair):
                half = enter(f"pv{pair}")
                pe.wait_ge(pT_ready, pair + 1)
                for b in range(2):
                    h = 2 * pair + b
                    cols = slice(h * P, (h + 1) * P)
                    t_.matmul(scr[:, half, b * GW:b * GW + S], fv[:, 0, cols], probT[:, b, 0:S],
                              start=True, stop=False)
                    last = t_.matmul(scr[:, half, b * GW + P:b * GW + S], fv[:, 1, cols], probT[:, b, S:384],
                                     start=False, stop=True)
                done(f"pv{pair}", last)

            pe.wait_ge(q_scaled, 1)
            logits(0)
            hg_output(0)
            for n in range(4):
                g = G_GA + n
                transposed_unit(g, 0, hT)
                transposed_unit(g, 1, hT)
                if n:
                    if n == 1:
                        pe.wait_ge(fv_ready, 1)
                    weighted_v(n - 1)
                transposed_unit(g, 2, hT)
                if n == 3:
                    transpose_p(3)
                transposed_unit(g, 3, hT)
                finish(g)
                if n < 3:
                    transpose_p(n)
                    logits(n + 1)
            weighted_v(3)
            loop_two(G_AUP, transposed_unit, (ya_hi, ya_lo), ya_split)
            for n in range(4):
                g = G_GB + 2 * n
                for m in range(4):
                    transposed_unit(g, m, hT)
                    if n == 0 and m == 1:
                        pe.wait_ge(ob_ready, 1)
                        for t in (1, 0):
                            half = enter(f"ob{t}")
                            for h in range(H):
                                last = t_.transpose(scr[:, half, h * P:(h + 1) * P], o_hg[:, t, h * P:(h + 1) * P],
                                                    ident[:, :])
                            done(f"ob{t}", last)
                finish(g)
                if n == 0:
                    pe.wait_ge(ob_split, 2)
                transposed_unit(g + 1, 0, (ob_hi, ob_lo))
                transposed_unit(g + 1, 1, (ob_hi, ob_lo))
                finish(g + 1)
                if n < 2:
                    pe.wait_ge(keys_in, 16)
                    half = enter(f"keys{n}")
                    for u in range(8):
                        last = t_.transpose(scr[:, half, u * P:(u + 1) * P], keys_sb[:, 8 * n + u, :], ident[:, :])
                    done(f"keys{n}", last)
            for m in range(4):
                pe.wait_ge(merged_split, m + 1)
                natural_unit(G_WO, m, hT)
            finish(G_WO)
            for g in range(G_WO + 1, G_WQ):
                for m in range(4):
                    natural_unit(g, m, hT)
                    if m == 2:
                        n = g - G_WO - 1
                        pe.wait_ge(normed, 4 + n + 1)
                        transpose_norm(f"h2{n}", n)
                finish(g)

            def score(n):
                half = enter(f"score{n}")
                pe.wait_ge(q_copied, n + 1)
                for t in range(NT):
                    for u in range(4):
                        last = t_.matmul(scr[:, half, (4 * t + u) * P:(4 * t + u + 1) * P],
                                         pqT[:, n % 2, u, t * P:(t + 1) * P], keysT[:, 4 * n + u, :],
                                         start=True, stop=True)
                done(f"score{n}", last)

            for n in range(4):
                g = G_WQ + n
                for m in range(4):
                    if n == 0:
                        pe.wait_ge(h_ready, 4 + m + 1)
                    transposed_unit(g, m, (h2T_hi, h2T_lo))
                    if n == 0 and m == 1:
                        pe.wait_ge(normed, 8)
                        transpose_norm("h23", 3)
                    if n and m == 1:
                        score(n - 1)
                finish(g)
            score(3)
            def turn_ij(t):
                if t:
                    pe.wait_ge(ij_ready, t)
                pe.wait_ge(expert_ready, 4 * t + 4)
                for c in range(2):
                    last = t_.transpose(scr[:, 0, c * P:(c + 1) * P], ij[:, t, c, :], ident[:, :])
                last.then_inc(ij_landed, 1)

            def turn_gate(t):
                pe.wait_ge(weight_ready, t + 1)
                t_.transpose(scr[:, 1, 0:P], weight[:, t, :], ident[:, :]).then_inc(gate_landed, 1)

            def scatter(t, side, n, half_n=0, place=0):
                pe.wait_ge(scattered, t * P // SC + 1 + n)
                pe.wait_ge(*((a_ready[1 + side], 1 + half_n) if t else (a_ready[0], 1 + n)))
                pe.wait_ge(b_hot_ready, t * P // SC + 1 + n)
                for c in range(SC):
                    last = t_.matmul(acc[:, side, c * P:(c + 1) * P], hot_b[:, side, c, :],
                                     hot_a1[:, place, c, :] if t else hot_a[:, side, c, :],
                                     start=True, stop=True)
                last.then_inc(hot_used, 1)

            pe.wait_ge(scr_free[0], use_number("score2"))
            pe.wait_ge(scr_free[1], use_number("score3"))
            pe.wait_ge(acc_free[0], 1 + G_END // 2)
            pe.wait_ge(acc_free[1], 1 + G_END // 2)
            turn_ij(0)
            turn_gate(0)
            turn_ij(1)
            with pe.Fori(0, P // SC // 2) as i:
                for side in range(2):
                    scatter(0, side, 2 * i + side)
            turn_gate(1)
            with pe.Fori(0, P // SC // 4) as i:
                for k in range(4):
                    scatter(1, k % 2, 4 * i + k, 2 * i + k // 2, k)
            pe.wait_ge(scattered, 2 + NT * P // SC)

            def v_products(q, i, first=False):
                final = q == PIECES - 1 and isinstance(i, int)
                for e in range(2):
                    block_ = P // PIECES * q + 2 * i + e
                    pe.wait_ge(e_ready, block_ + 1)
                    for c in range(2):
                        pe.wait_ge(v_ready, 2 * block_ + c + 1)
                        start, stop = first and e == 0, final and e == 1
                        for t in range(NT):
                            flat = (acc, scr)[t][:, :, :].rearrange("p a n -> p (a n)")
                            for lo_, hi_ in ((0, 2), (2, 3)) if c == 0 else ((0, 1), (1, 3)):
                                cols = slice(lo_ * VW // 3, hi_ * VW // 3)
                                to = flat[:, c * VW + lo_ * VW // 3:c * VW + hi_ * VW // 3]
                                clear = start and not (c == 1 and lo_ == 0)
                                t_.matmul(to, e_hi[:, e, t, :], v_hi[:, 2 * e + c, cols], start=clear, stop=False,
                                          skip_group_check=True)
                                t_.matmul(to, e_hi[:, e, t, :], v_lo[:, c, cols], start=False, stop=False,
                                          skip_group_check=True)
                                last = t_.matmul(to, e_lo[:, e, t, :], v_hi[:, 2 * e + c, cols], start=False, stop=stop,
                                                 skip_group_check=True)
                        last.then_inc(v_used, 1)

            v_loops(pe, v_products)


_INS = ["x", "norm1_g", "w_in", "fox_f_bias", "hg_lb_logits", "hg_norm_g", "w_a_up", "w_b_up", "w_o", "norm2_g",
        "peer_wq", "peer_keys", "peer_u", "peer_v", "norm_f_g"]


def kernel(**inputs):
    import numpy as np
    import concourse.bacc as bacc
    from concourse.bass_utils import run_bass_kernel_spmd as run

    nc = bacc.Bacc("TRN2", target_bir_lowering=False, num_devices=1)
    arrays, args = {}, []
    for name in _INS:
        a = np.ascontiguousarray(inputs[name])
        arrays[f"in_{name}"] = a
        args.append(nc.dram_tensor(f"in_{name}", a.shape, mybir.dt.from_np(a.dtype), kind="ExternalInput").ap())
    args.append(nc.dram_tensor("out_0", (1, S, D), mybir.dt.float32, kind="ExternalOutput").ap())
    build(nc, *args)
    return run(nc, [arrays], core_ids=[0]).results[0]["out_0"]
```
